# Optimizing a Trainium2 kernel written in Bass

```python
import math
import jax, jax.numpy as jnp
from jax import lax
import numpy as np

D_MODEL = 1024
BATCH = 1
SEQ = 512
DEPTH = 2

HEAD_DIM = 64
N_TOK_HEADS = 12
TOK_W = N_TOK_HEADS * HEAD_DIM
N_MEM_HEADS = 4
MEM_W = N_MEM_HEADS * HEAD_DIM
MIX_W = TOK_W + MEM_W
N_MEM = 256
Q_BLOCK = 128
DECAY_LORA = 64
AAA_LORA = 64
GATE_LORA = 128
RWKV_SHIFT_W = 3 * TOK_W + DECAY_LORA + AAA_LORA + GATE_LORA
RWKV_IN_W = RWKV_SHIFT_W + MEM_W
FOX_IN_W = 4 * TOK_W + N_TOK_HEADS + MEM_W
N_EXPERTS = 64
TOP_K = 6
D_EXPERT = 256
D_SHARED = 256
ROUTED_SCALE = 2.5
EXPERT_BLOCK = 128
N_FOX_LAYERS = (DEPTH + 1) // 2
N_RWKV_LAYERS = DEPTH // 2
DEEPNORM_ALPHA = (2 * DEPTH) ** 0.25
DEEPNORM_BETA = (8 * DEPTH) ** -0.25
LN_EPS = 1e-5
GN_EPS = 64e-5

kernel_name = 'hybrid_fox_rwkv7_memxattn_moe_deepnorm'

def layer_norm(x, g, b):
    xf = x.astype(jnp.float32)
    mu = jnp.mean(xf, axis=-1, keepdims=True)
    var = jnp.mean(jnp.square(xf - mu), axis=-1, keepdims=True)
    return ((xf - mu) * lax.rsqrt(var + LN_EPS) * g + b).astype(x.dtype)

def token_shift(h):
    return jnp.pad(h[:, :-1], ((0, 0), (1, 0), (0, 0)))

def split_heads(t, n_heads):
    return t.reshape(t.shape[0], t.shape[1], n_heads, HEAD_DIM)

def memory_cross_attention(q_mem, k_mem, v_mem):
    B_, S_, _ = q_mem.shape
    q = split_heads(q_mem, N_MEM_HEADS)
    s = jnp.einsum('bshd,bmhd->bhsm', q, k_mem).astype(jnp.float32) * (HEAD_DIM ** -0.5)
    p = jax.nn.softmax(s, axis=-1).astype(v_mem.dtype)
    return jnp.einsum('bhsm,bmhd->bshd', p, v_mem).reshape(B_, S_, MEM_W)

def forgetting_attention(q, k, v, c):
    cT = jnp.swapaxes(c, 1, 2)
    scale = HEAD_DIM ** -0.5
    n_blocks = q.shape[1] // Q_BLOCK
    outs = []
    for blk in range(n_blocks):
        q0 = blk * Q_BLOCK
        q1 = q0 + Q_BLOCK
        s = jnp.einsum('bqhd,bkhd->bhqk', q[:, q0:q1], k[:, :q1]).astype(jnp.float32) * scale
        s = s + cT[:, :, q0:q1, None] - cT[:, :, None, :q1]
        causal = jnp.arange(q1)[None, :] <= jnp.arange(q0, q1)[:, None]
        s = jnp.where(causal, s, -jnp.inf)
        p = jax.nn.softmax(s, axis=-1).astype(v.dtype)
        outs.append(jnp.einsum('bhqk,bkhd->bqhd', p, v[:, :q1]))
    return jnp.concatenate(outs, axis=1)

def fox_mix(x, w_in, b_f):
    h = x @ w_in
    q, k, v, og, fl, q_mem = jnp.split(
        h, [TOK_W, 2 * TOK_W, 3 * TOK_W, 4 * TOK_W, 4 * TOK_W + N_TOK_HEADS], axis=-1)
    log_f = jax.nn.log_sigmoid((fl + b_f).astype(jnp.float32))
    c = jnp.cumsum(log_f, axis=1)
    o = forgetting_attention(split_heads(q, N_TOK_HEADS), split_heads(k, N_TOK_HEADS),
                             split_heads(v, N_TOK_HEADS), c)
    tok = o.reshape(x.shape[0], x.shape[1], TOK_W) * jax.nn.sigmoid(og)
    return tok.astype(x.dtype), q_mem

def wkv7_scan(r, w, k, v, a, b):
    B_, S_, H_, N_ = r.shape

    def step(state, inp):
        r_t, w_t, k_t, v_t, a_t, b_t = inp
        sa = jnp.einsum('bhij,bhj->bhi', state, a_t)
        state = (state * w_t[:, :, None, :] + sa[..., None] * b_t[:, :, None, :]
                 + v_t[..., None] * k_t[:, :, None, :])
        return state, jnp.einsum('bhij,bhj->bhi', state, r_t)

    xs = tuple(jnp.moveaxis(t, 1, 0) for t in (r, w, k, v, a, b))
    state0 = jnp.zeros((B_, H_, N_, N_), jnp.float32)
    _, y = lax.scan(step, state0, xs)
    return jnp.moveaxis(y, 0, 1)

def rwkv7_mix(x, w_in, mu, w0, w2, a0, a2, g2, k_k, k_a, r_k, lnx_g, lnx_b):
    B_, S_, _ = x.shape
    h = x @ w_in
    hs = h[..., :RWKV_SHIFT_W].astype(jnp.float32)
    hs = hs + mu * (token_shift(hs) - hs)
    r, k, v, wd, ad, gd = jnp.split(
        hs, [TOK_W, 2 * TOK_W, 3 * TOK_W, 3 * TOK_W + DECAY_LORA, 3 * TOK_W + DECAY_LORA + AAA_LORA], axis=-1)
    q_mem = h[..., RWKV_SHIFT_W:]
    w = -jax.nn.softplus(-(w0 + jnp.tanh(wd) @ w2)) - 0.5
    decay = jnp.exp(-jnp.exp(w))
    a = jax.nn.sigmoid(a0 + ad @ a2)
    g = jax.nn.sigmoid(gd) @ g2
    kk = split_heads(k * k_k, N_TOK_HEADS)
    kk = kk / jnp.maximum(jnp.sqrt(jnp.sum(kk * kk, axis=-1, keepdims=True)), 1e-12)
    k = k * (1.0 + (a - 1.0) * k_a)
    rh = split_heads(r, N_TOK_HEADS)
    kh = split_heads(k, N_TOK_HEADS)
    vh = split_heads(v, N_TOK_HEADS)
    ah = split_heads(a, N_TOK_HEADS)
    y = wkv7_scan(rh, split_heads(decay, N_TOK_HEADS), kh, vh, -kk, kk * ah)
    m = jnp.mean(y, axis=-1, keepdims=True)
    var = jnp.mean(jnp.square(y - m), axis=-1, keepdims=True)
    y = ((y - m) * lax.rsqrt(var + GN_EPS)).reshape(B_, S_, TOK_W) * lnx_g + lnx_b
    y = split_heads(y, N_TOK_HEADS) + jnp.sum(rh * kh * r_k, axis=-1, keepdims=True) * vh
    tok = y.reshape(B_, S_, TOK_W) * g
    return tok.astype(x.dtype), q_mem

def moe_ffn(x2, w_router, router_bias, w_gate, w_up, w_down, w_sh_gate, w_sh_up, w_sh_down):
    T = x2.shape[0]
    TK = T * TOP_K
    scores = jax.nn.sigmoid((x2 @ w_router).astype(jnp.float32))
    _, idx = lax.top_k(scores + router_bias.astype(jnp.float32), TOP_K)
    gate = jnp.take_along_axis(scores, idx, axis=1)
    gate = gate / jnp.sum(gate, axis=-1, keepdims=True) * ROUTED_SCALE
    e = idx.reshape(-1)
    tok = jnp.arange(TK, dtype=jnp.int32) // TOP_K
    gflat = gate.reshape(-1)
    counts = jnp.bincount(e, length=N_EXPERTS)
    padded = (counts + EXPERT_BLOCK - 1) // EXPERT_BLOCK * EXPERT_BLOCK
    ends = jnp.cumsum(padded)
    starts = ends - padded
    order = jnp.argsort(e)
    e_sorted = e[order]
    rank = jnp.arange(TK, dtype=jnp.int32) - (jnp.cumsum(counts) - counts)[e_sorted]
    dest = starts[e_sorted] + rank
    n_slots = TK + N_EXPERTS * EXPERT_BLOCK
    n_blocks = n_slots // EXPERT_BLOCK
    slot_tok = jnp.full((n_slots,), T, jnp.int32).at[dest].set(tok[order])
    slot_gate = jnp.zeros((n_slots,), jnp.float32).at[dest].set(gflat[order])
    block_exp = jnp.minimum(
        jnp.searchsorted(ends, jnp.arange(n_blocks, dtype=ends.dtype) * EXPERT_BLOCK, side='right'),
        N_EXPERTS - 1)
    x_pad = jnp.concatenate([x2, jnp.zeros((1, x2.shape[1]), x2.dtype)], axis=0)

    def body(acc, blk):
        tok_b, gate_b, eb = blk
        xb = x_pad[tok_b]
        hb = jax.nn.silu(xb @ w_gate[eb]) * (xb @ w_up[eb])
        yb = hb @ w_down[eb]
        return acc.at[tok_b].add((yb * gate_b[:, None]).astype(acc.dtype)), None

    acc, _ = lax.scan(body, jnp.zeros((T + 1, x2.shape[1]), x2.dtype),
                      (slot_tok.reshape(n_blocks, EXPERT_BLOCK),
                       slot_gate.reshape(n_blocks, EXPERT_BLOCK), block_exp))
    shared = (jax.nn.silu(x2 @ w_sh_gate) * (x2 @ w_sh_up)) @ w_sh_down
    return acc[:T] + shared

def setup_inputs(seed: int = 0) -> dict:
    key = jax.random.key(seed)
    ks = jax.random.split(key, 32)
    n = lambda k, shape: jax.random.normal(k, shape, jnp.float32)
    D = D_MODEL
    NF, NR = N_FOX_LAYERS, N_RWKV_LAYERS
    return {
        'x': n(ks[0], (BATCH, SEQ, D)),
        'mem': n(ks[1], (BATCH, N_MEM, D)),
        'mem_ln_g': 1.0 + 0.02 * n(ks[2], (D,)),
        'mem_ln_b': 0.02 * n(ks[3], (D,)),
        'w_mem_kv': n(ks[4], (D, 2 * MEM_W)) * D ** -0.5,
        'fox_w_in': n(ks[5], (NF, D, FOX_IN_W)) * D ** -0.5,
        'fox_b_f': 2.0 + 0.5 * n(ks[6], (NF, N_TOK_HEADS)),
        'rwkv_w_in': n(ks[7], (NR, D, RWKV_IN_W)) * D ** -0.5,
        'rwkv_mu': jax.random.uniform(ks[8], (NR, RWKV_SHIFT_W), jnp.float32),
        'rwkv_w0': -2.0 + 1.5 * n(ks[9], (NR, TOK_W)),
        'rwkv_w2': n(ks[10], (NR, DECAY_LORA, TOK_W)) * 0.5 * DECAY_LORA ** -0.5,
        'rwkv_a0': 0.5 * n(ks[11], (NR, TOK_W)),
        'rwkv_a2': n(ks[12], (NR, AAA_LORA, TOK_W)) * 0.5 * AAA_LORA ** -0.5,
        'rwkv_g2': n(ks[13], (NR, GATE_LORA, TOK_W)) * GATE_LORA ** -0.5,
        'rwkv_k_k': 1.0 + 0.1 * n(ks[14], (NR, TOK_W)),
        'rwkv_k_a': 1.0 + 0.1 * n(ks[15], (NR, TOK_W)),
        'rwkv_r_k': 0.1 * n(ks[16], (NR, N_TOK_HEADS, HEAD_DIM)),
        'rwkv_lnx_g': 1.0 + 0.02 * n(ks[17], (NR, TOK_W)),
        'rwkv_lnx_b': 0.02 * n(ks[18], (NR, TOK_W)),
        'w_out': n(ks[19], (DEPTH, MIX_W, D)) * MIX_W ** -0.5 * DEEPNORM_BETA,
        'ln1_g': 1.0 + 0.02 * n(ks[20], (DEPTH, D)),
        'ln1_b': 0.02 * n(ks[21], (DEPTH, D)),
        'w_router': n(ks[22], (DEPTH, D, N_EXPERTS)) * D ** -0.5,
        'router_bias': 0.01 * n(ks[23], (DEPTH, N_EXPERTS)),
        'w_exp_gate': n(ks[24], (DEPTH, N_EXPERTS, D, D_EXPERT)) * D ** -0.5,
        'w_exp_up': n(ks[25], (DEPTH, N_EXPERTS, D, D_EXPERT)) * D ** -0.5,
        'w_exp_down': n(ks[26], (DEPTH, N_EXPERTS, D_EXPERT, D)) * D_EXPERT ** -0.5 * DEEPNORM_BETA,
        'w_sh_gate': n(ks[27], (DEPTH, D, D_SHARED)) * D ** -0.5,
        'w_sh_up': n(ks[28], (DEPTH, D, D_SHARED)) * D ** -0.5,
        'w_sh_down': n(ks[29], (DEPTH, D_SHARED, D)) * D_SHARED ** -0.5 * DEEPNORM_BETA,
        'ln2_g': 1.0 + 0.02 * n(ks[30], (DEPTH, D)),
        'ln2_b': 0.02 * n(ks[31], (DEPTH, D)),
    }

def reference(x, mem, mem_ln_g, mem_ln_b, w_mem_kv, fox_w_in, fox_b_f, rwkv_w_in, rwkv_mu,
              rwkv_w0, rwkv_w2, rwkv_a0, rwkv_a2, rwkv_g2, rwkv_k_k, rwkv_k_a, rwkv_r_k,
              rwkv_lnx_g, rwkv_lnx_b, w_out, ln1_g, ln1_b, w_router, router_bias,
              w_exp_gate, w_exp_up, w_exp_down, w_sh_gate, w_sh_up, w_sh_down, ln2_g, ln2_b):
    B_, S_, D = x.shape
    kv = layer_norm(mem, mem_ln_g, mem_ln_b) @ w_mem_kv
    k_mem = split_heads(kv[..., :MEM_W], N_MEM_HEADS)
    v_mem = split_heads(kv[..., MEM_W:], N_MEM_HEADS)
    for i in range(DEPTH):
        j = i // 2
        if i % 2 == 0:
            tok, q_mem = fox_mix(x, fox_w_in[j], fox_b_f[j])
        else:
            tok, q_mem = rwkv7_mix(x, rwkv_w_in[j], rwkv_mu[j], rwkv_w0[j], rwkv_w2[j], rwkv_a0[j],
                                   rwkv_a2[j], rwkv_g2[j], rwkv_k_k[j], rwkv_k_a[j], rwkv_r_k[j],
                                   rwkv_lnx_g[j], rwkv_lnx_b[j])
        mem_out = memory_cross_attention(q_mem, k_mem, v_mem)
        mixed = jnp.concatenate([tok, mem_out.astype(tok.dtype)], axis=-1) @ w_out[i]
        x = layer_norm(DEEPNORM_ALPHA * x + mixed, ln1_g[i], ln1_b[i])
        ffn = moe_ffn(x.reshape(B_ * S_, D), w_router[i], router_bias[i], w_exp_gate[i], w_exp_up[i],
                      w_exp_down[i], w_sh_gate[i], w_sh_up[i], w_sh_down[i]).reshape(B_, S_, D)
        x = layer_norm(DEEPNORM_ALPHA * x + ffn, ln2_g[i], ln2_b[i])
    return x


_drawn_inputs = setup_inputs


def setup_inputs(seed=0):
    import zlib

    import numpy as np

    out = dict(_drawn_inputs(seed))
    spreads = {}
    factors = {'mem_ln_g': 5.24,
     'rwkv_w2': 3.202,
     'rwkv_k_k': 2.849,
     'rwkv_lnx_g': 4.712,
     'rwkv_lnx_b': 4.843}
    for name, (base, spread) in spreads.items():
        noise = np.random.default_rng([zlib.crc32(name.encode()), seed]).standard_normal(out[name].shape)
        drawn = base * np.exp(spread * noise) if base else spread * noise
        out[name] = __import__('jax').numpy.asarray(drawn.astype(out[name].dtype))
    for name, factor in factors.items():
        out[name] = (out[name] * factor).astype(out[name].dtype)
    return out
```

```python
from contextlib import ExitStack

import numpy as np

import concourse.bass as bass
from concourse import mybir

F32, BF16, I32, U32 = mybir.dt.float32, mybir.dt.bfloat16, mybir.dt.int32, mybir.dt.uint32
ALU, ACT, AX = mybir.AluOpType, mybir.ActivationFunctionType, mybir.AxisListType

P = 128
D = 1024
T = 512
NT = T // P
KD = D // P
DEPTH = 2
HD = 64
NH = 12
NMH = 4
TOKW = NH * HD
MEMW = NMH * HD
NMEM = 256
E = 64
TOPK = 6
FE = 256
SLOTS = 64
PAIRS = E // 2
UNROLL = 8
AHEAD = 3
EXTRA = T // SLOTS - 1
MAX_EXTRA = T * TOPK // SLOTS
NOBODY = 4096
PAIR_STEPS = 4
ROUTED_SCALE = 2.5
ALPHA = (2 * DEPTH) ** 0.25
LN_EPS = 1e-5
GN_EPS = 64e-5


class Names:
    pass


class Chain:

    def __init__(self, eng, sem, start=0):
        self.eng, self.sem, self.n = eng, sem, start

    def inc(self, ins):
        ins.then_inc(self.sem, 1)
        self.n = self.n + 1
        return ins

    def __call__(self, ins):
        self.inc(ins)
        self.eng.wait_ge(self.sem, self.n)


class Phase(ExitStack):

    def __init__(self, nc):
        super().__init__()
        self.nc, self.sems = nc, []

    def sem(self, name):
        self.sems.append(self.nc.alloc_semaphore(name=name))
        return self.sems[-1]

    def __exit__(self, *what):
        if what[0] is None:
            self.nc.clear_and_free_semaphores(self.sems)
            self.nc.all_engine_barrier()
        return super().__exit__(*what)


def wait_from(eng, sem, value):
    if not (isinstance(value, int) and value <= 0):
        eng.wait_ge(sem, value)


def constants(K, scope):
    nc = K.nc

    def sb(name, shape, dt=F32):
        return scope.enter_context(nc.sbuf_tensor(name, shape, dt))

    K.ident = sb("ident", [P, P])
    K.before = sb("before", [P, P], BF16)
    K.ident16 = sb("ident16", [P, P], BF16)
    K.causal = sb("causal", [P, P], BF16)
    K.upto = sb("upto_f32", [P, P])
    K.ones = sb("ones_f32", [P, P])
    K.heads = sb("heads", [P, P])
    K.masks4 = sb("masks4", [P, 4 * P], BF16)
    K.level = sb("level", [P, 7, P], BF16)
    K.ones16 = sb("ones16", [P, P], BF16)
    K.iota_e = sb("iota_e", [P, E])
    K.iota_s = sb("iota_s", [P, T])
    K.iota_j = sb("iota_j", [P, TOPK])
    K.levels = sb("levels", [P, EXTRA])
    K.place = sb("place", [P, NT, E])
    K.slot_cols = sb("slot_cols", [P, NT, PAIRS + 6, 4], BF16)
    K.rank = sb("rank", [P, NT, E + 12])
    K.gates = sb("gates", [P, NT, TOPK])
    K.extra_n = sb("extra_n", [1, PAIRS], I32)
    K.extra_upto = sb("extra_upto", [1, PAIRS + 1], I32)
    scratch = sb("iota_scratch", [P, T], I32)
    made = scope.enter_context(nc.semaphore("constants_made"))
    with nc.Block() as block:
        @block.gpsimd
        def _(pool):
            step = Chain(pool, made)
            step.inc(pool.memset(K.ident[:], 0.0))
            step.inc(pool.memset(K.before[:], 1.0))
            step.inc(pool.memset(K.ones16[:], 1.0))
            step.inc(pool.memset(K.ident16[:], 0.0))
            step.inc(pool.memset(K.causal[:], 0.0))
            step.inc(pool.memset(K.upto[:], 1.0))
            step.inc(pool.memset(K.ones[:], 1.0))
            step.inc(pool.memset(K.rank[:], -1.0))
            step(pool.memset(K.slot_cols[:], 0.0))
            step.inc(pool.affine_select(out=K.ident[:], in_=K.ident[:], compare_op=ALU.not_equal, fill=1.0, base=0,
                                        pattern=[[-1, P]], channel_multiplier=1))
            step.inc(pool.affine_select(out=K.ident16[:], in_=K.ident16[:], compare_op=ALU.not_equal, fill=1.0, base=0,
                                        pattern=[[-1, P]], channel_multiplier=1))
            step.inc(pool.affine_select(out=K.causal[:], in_=K.causal[:], compare_op=ALU.is_ge, fill=-1e30, base=0,
                                        pattern=[[-1, P]], channel_multiplier=1))
            step.inc(pool.affine_select(out=K.upto[:], in_=K.upto[:], compare_op=ALU.is_ge, fill=0.0, base=0,
                                        pattern=[[1, P]], channel_multiplier=-1))
            step.inc(pool.affine_select(out=K.before[:], in_=K.before[:], compare_op=ALU.is_ge, fill=0.0, base=-1,
                                        pattern=[[1, P]], channel_multiplier=-1))
            for dst, pattern, base, mult in (
                    (K.iota_s[:], [[1, T]], 0, 0), (K.iota_e[:], [[1, E]], 0, 0), (K.iota_j[:], [[T, TOPK]], 0, 0),
                    (K.levels[:], [[SLOTS, EXTRA]], SLOTS, 0)):
                n = dst.shape[1]
                step(pool.iota(scratch[:, 0:n], pattern=pattern, base=base, channel_multiplier=mult))
                step(pool.tensor_copy(dst, scratch[:, 0:n]))
            n = PAIRS + 6
            step(pool.iota(scratch[:, 0:n], pattern=[[0, n]], base=0, channel_multiplier=1))
            step(pool.memset(K.level[:, 6, :], 1.0))
            for lv in range(5, -1, -1):
                nb, w = P // (2 << lv), 2 << lv
                same = K.level[:, lv, :].rearrange("p (b w) -> p b w", w=w)
                step(pool.memset(K.level[:, lv, :], 1.0))
                step(pool.affine_select(out=same, in_=same, compare_op=ALU.is_ge, fill=0.0, base=0, pattern=[[-w, nb], [0, w]], channel_multiplier=1))
                step(pool.affine_select(out=same, in_=same, compare_op=ALU.is_ge, fill=0.0, base=w - 1, pattern=[[w, nb], [0, w]], channel_multiplier=-1))
            step(pool.tensor_copy(K.heads[:], K.level[:, 5, :]))
            for lv in range(6, -1, -1):
                below = K.level[:, lv - 1, :] if lv else K.ident[:]
                step(pool.tensor_tensor(K.level[:, lv, :], K.level[:, lv, :], below, ALU.subtract))
                step(pool.tensor_tensor(K.level[:, lv, :], K.level[:, lv, :], K.upto[:], ALU.mult))
            for q in range(4):
                step(pool.tensor_copy(K.masks4[:, q * P:(q + 1) * P], (K.upto if q % 2 else K.before)[:]))
            for t in range(NT):
                step(pool.tensor_copy(K.slot_cols[:, t, :, 0], scratch[:, 0:n]))
                step(pool.memset(K.slot_cols[:, t, :, 1], float(P * t - NOBODY)))
def routed_experts_tables(K, L):
    nc, X, XT, ident = K.nc, K.X, K.XT, K.ident
    B = K.banks
    with Phase(nc) as scope:
        def sb(name, shape, dt=F32):
            return scope.enter_context(nc.sbuf_tensor(f"{name}{L}", shape, dt))

        def sem(name):
            return scope.sem(f"route{L}_{name}")

        w_router = sb("w_router", [P, KD, E])
        bias = sb("router_bias", [P, 1, E])
        w_sh = sb("w_sh", [P, 2, KD * FE])
        w_shd = sb("w_shd", [P, 2, D])
        negexp = sb("negexp", [P, NT, E])
        score = sb("score", [P, NT, E])
        choose = sb("choose", [P, NT, E])
        top = sb("top", [P, NT, 8])
        top_at = sb("top_at", [P, NT, 8], U32)
        top_f = sb("top_f", [P, NT, 8])
        hot = sb("hot", [P, NT * TOPK, E])
        hot_w = sb("hot_w", [P, NT * TOPK, E])
        mask = sb("mask", [P, NT, E])
        mask16 = sb("mask16", [P, NT, E], BF16)
        gsum = sb("gsum", [P, NT, 1])
        most = sb("most", [P, PAIRS, 1])
        over = sb("over", [P, PAIRS, EXTRA])
        n_extra = sb("n_extra", [P, PAIRS])
        upto = sb("upto", [P, PAIRS])
        sh_e = sb("sh_e", [P, 2, T])
        sh_h = sb("sh_h", [P, 2, T])

        loaded = sem("loaded")
        loaded_sh = sem("loaded_sh")
        stored = sem("stored")
        turned = sem("turned")
        xt_a, xt_d = sem("xt_a"), sem("xt_d")
        logits = sem("logits")
        negexp_done = sem("negexp")
        mask_done = sem("mask")
        ranked = sem("ranked")
        sh_gu = sem("sh_gu")
        sh_exp = sem("sh_exp")
        sh_hidden = sem("sh_hidden")
        sh_out = sem("sh_out")
        steps = sem("steps")

        with nc.Block() as block:
            @block.sync
            def _(sp):
                sp.dma_start(w_router[:], K.in_["w_router"][L].rearrange("(p k) e -> p k e", k=KD)).then_inc(loaded, 16)
                sp.dma_start(bias[:, 0, :], K.in_["router_bias"][L:L + 1, :].broadcast_to([P, E])).then_inc(loaded, 16)
                sp.dma_start(w_sh[:, 0, :], K.in_["w_sh_gate"][L].rearrange("(p k) f -> p (k f)", k=KD)).then_inc(loaded_sh, 16)
                sp.dma_start(w_sh[:, 1, :], K.in_["w_sh_up"][L].rearrange("(p k) f -> p (k f)", k=KD)).then_inc(loaded_sh, 16)
                sp.dma_start(w_shd[:], K.in_["w_sh_down"][L].rearrange("(j p) d -> p j d", p=P)).then_inc(loaded_sh, 16)
                sp.dma_start(K.x_rows.rearrange("(t p) d -> p t d", p=P), X[:]).then_inc(stored, 16)
                for i in range(2):
                    load_pair(K, sp, L, i, i)
                sp.wait_ge(stored, 16)

            @block.tensor
            def _(pe):
                for k in range(KD):
                    if k >= 4:
                        pe.wait_ge(xt_a if k % 2 == 0 else xt_d, (k - 4) // 2 + 1)
                    for t in range(NT):
                        last = pe.transpose(B[k % 4][:, t * P:(t + 1) * P], K.Xk[:, t, k, :], ident[:])
                    last.then_inc(turned, 1)
                pe.wait_ge(loaded, 32)
                pe.wait_ge(xt_a, KD // 2)
                pe.wait_ge(xt_d, KD // 2)
                for t in range(NT):
                    for k in range(KD):
                        last = pe.matmul(B[4][:, t * E:(t + 1) * E], XT[:, k, t * P:(t + 1) * P], w_router[:, k, :],
                                         start=(k == 0), stop=(k == KD - 1))
                last.then_inc(logits, 1)
                pe.wait_ge(loaded_sh, 48)
                for gu in range(2):
                    for j in range(2):
                        for k in range(KD):
                            last = pe.matmul(B[gu * 2 + j][:], w_sh[:, gu, k * FE + j * P:k * FE + (j + 1) * P],
                                             XT[:, k, :], start=(k == 0), stop=(k == KD - 1))
                        last.then_inc(sh_gu, 1)
                pe.wait_ge(mask_done, 1)
                for t in range(NT):
                    for t0 in range(t + 1):
                        last = pe.matmul(B[5][:, t * E:(t + 1) * E], (K.before if t0 == t else K.ones16)[:],
                                         mask16[:, t0, :], start=(t0 == 0), stop=(t0 == t))
                for t in range(NT):
                    last = pe.matmul(B[5][:, NT * E:(NT + 1) * E], K.ones16[:], mask16[:, t, :],
                                     start=(t == 0), stop=(t == NT - 1))
                last.then_inc(ranked, 1)
                pe.wait_ge(sh_hidden, 2)
                for t in range(NT):
                    for n in range(2):
                        i = t * 2 + n
                        if i >= 2:
                            pe.wait_ge(K.sh_added, L * 8 + i - 1)
                        for j in range(2):
                            last = pe.matmul(B[6 + n][:], sh_h[:, j, t * P:(t + 1) * P], w_shd[:, j, n * 512:(n + 1) * 512],
                                             start=(j == 0), stop=(j == 1))
                        last.then_inc(sh_out, 1)

            @block.scalar
            def _(act):
                for k in range(0, KD, 2):
                    act.wait_ge(turned, k + 1)
                    act.activation(XT[:, k, :], B[k % 4][:], ACT.Copy).then_inc(xt_a, 1)
                act.wait_ge(logits, 1)
                act.activation(negexp[:], B[4][:, 0:NT * E].rearrange("p (t e) -> p t e", t=NT), ACT.Exp, scale=-1.0).then_inc(negexp_done, 1)
                for j in range(2):
                    act.wait_ge(sh_gu, j + 1)
                    act.activation(sh_e[:, j, :], B[j][:], ACT.Exp, scale=-1.0).then_inc(sh_exp, 1)

            @block.vector
            def _(dve):
                step = Chain(dve, steps)
                for k in range(1, KD, 2):
                    dve.wait_ge(turned, k + 1)
                    dve.tensor_copy(XT[:, k, :], B[k % 4][:]).then_inc(xt_d, 1)
                dve.wait_ge(loaded, 32)
                dve.wait_ge(negexp_done, 1)
                step(dve.tensor_scalar_add(negexp[:], negexp[:], 1.0))
                step(dve.reciprocal(score[:], negexp[:]))
                step(dve.tensor_tensor(choose[:], score[:], bias[:].to_broadcast([P, NT, E]), ALU.add))
                for t in range(NT):
                    step(dve.max(top[:, t, :], choose[:, t, :]))
                    last = dve.max_index(top_at[:, t, :], top[:, t, :], choose[:, t, :])
                    step.inc(last)
                dve.wait_ge(steps, step.n)
                step(dve.tensor_copy(top_f[:], top_at[:]))
                hot4 = hot[:].rearrange("p (t j) e -> p t j e", t=NT)
                hotw4 = hot_w[:].rearrange("p (t j) e -> p t j e", t=NT)
                for t in range(NT):
                    step.inc(dve.tensor_tensor(hot4[:, t], top_f[:, t, 0:TOPK].unsqueeze(2).to_broadcast([P, TOPK, E]),
                                               K.iota_e[:].unsqueeze(1).to_broadcast([P, TOPK, E]), ALU.is_equal))
                dve.wait_ge(steps, step.n)
                step(dve.tensor_reduce(mask[:], hot4.rearrange("p t j e -> p t e j"), AX.X, ALU.add))
                dve.tensor_copy(mask16[:], mask[:]).then_inc(mask_done, 1)
                for t in range(NT):
                    step.inc(dve.tensor_tensor(hotw4[:, t], hot4[:, t], K.iota_j[:].unsqueeze(2).to_broadcast([P, TOPK, E]), ALU.mult))
                dve.wait_ge(steps, step.n)
                with nc.allow_low_precision(reason="multiples of 512 up to 2560 are exact in bfloat16"):
                    step(dve.tensor_reduce(K.slot_cols[:, :, 0:PAIRS, 2:4].rearrange("p t i a -> p t (i a)") if False else K.place[:], hotw4.rearrange("p t j e -> p t e j"), AX.X, ALU.add))
                for t in range(NT):
                    step.inc(dve.tensor_copy(K.slot_cols[:, t, 0:PAIRS, 2:4], K.place[:, t, :].rearrange("p (i a) -> p i a", a=2)))
                for t in range(NT):
                    step.inc(dve.tensor_tensor(hotw4[:, t], hot4[:, t], score[:, t, :].unsqueeze(1).to_broadcast([P, TOPK, E]), ALU.mult))
                dve.wait_ge(steps, step.n)
                step(dve.tensor_reduce(K.gates[:], hotw4, AX.X, ALU.add))
                step(dve.tensor_reduce(gsum[:, :, 0], K.gates[:], AX.X, ALU.add))
                step(dve.reciprocal(gsum[:], gsum[:]))
                step(dve.tensor_scalar_mul(gsum[:], gsum[:], ROUTED_SCALE))
                step(dve.tensor_tensor(K.gates[:], K.gates[:], gsum[:].to_broadcast([P, NT, TOPK]), ALU.mult))
                dve.wait_ge(ranked, 1)
                for t in range(NT):
                    step.inc(dve.scalar_tensor_tensor(K.rank[:, t, 0:E], B[5][:, t * E:(t + 1) * E], 1.0, mask[:, t, :], ALU.add, ALU.mult))
                dve.wait_ge(steps, step.n)
                step(dve.tensor_scalar_add(K.rank[:, :, 0:E], K.rank[:, :, 0:E], -1.0))
                cnt = B[5][:, NT * E:(NT + 1) * E].rearrange("p (i a) -> p i a", a=2)
                step(dve.tensor_reduce(most[:, :, 0], cnt, AX.X, ALU.max))
                step(dve.tensor_tensor(over[:], most[:].to_broadcast([P, PAIRS, EXTRA]), K.levels[:].unsqueeze(1).to_broadcast([P, PAIRS, EXTRA]), ALU.is_gt))
                step(dve.tensor_reduce(n_extra[:], over[:], AX.X, ALU.add))
                step(dve.tensor_tensor_scan(upto[:], n_extra[:], n_extra[:], 0.0, ALU.add, ALU.bypass))
                step.inc(dve.tensor_copy(K.extra_upto[:, 1:PAIRS + 1], upto[0:1, :]))
                step.inc(dve.tensor_copy(K.extra_n[:], n_extra[0:1, :]))
                step(dve.memset(K.extra_upto[:, 0:1], 0))
                for j in range(2):
                    dve.wait_ge(sh_exp, j + 1)
                    step(dve.tensor_scalar_add(sh_e[:, j, :], sh_e[:, j, :], 1.0))
                    step(dve.reciprocal(sh_e[:, j, :], sh_e[:, j, :]))
                    step(dve.tensor_tensor(sh_e[:, j, :], sh_e[:, j, :], B[j][:], ALU.mult))
                    dve.wait_ge(sh_gu, 3 + j)
                    dve.tensor_tensor(sh_h[:, j, :], sh_e[:, j, :], B[2 + j][:], ALU.mult).then_inc(sh_hidden, 1)
                dve.wait_ge(stored, 16)
                for t in range(NT):
                    for n in range(2):
                        dve.wait_ge(sh_out, t * 2 + n + 1)
                        xs = X[:, t, n * 512:(n + 1) * 512]
                        dve.scalar_tensor_tensor(xs, xs, ALPHA, B[6 + n][:], ALU.mult, ALU.add).then_inc(K.sh_added, 1)


def load_pair(K, sp, L, i, slot, which=(0, 1, 2)):
    for m in which:
        name = ("w_exp_gate", "w_exp_up", "w_exp_down")[m]
        src = K.in_[name].rearrange("l e r c -> (l e) r c")[bass.ds(L * E + i * 2, 2)]
        src = src.rearrange("e (p k) f -> p e (k f)", p=P)
        sp.dma_start(K.W[:, slot, :, m, :], src).then_inc(K.w_gu[slot] if m < 2 else K.w_dn[slot], 16)


def expert_loop(K, L):
    nc, B, ident = K.nc, K.banks, K.ident
    with Phase(nc) as scope:
        def sb(name, shape, dt=F32):
            return scope.enter_context(nc.sbuf_tensor(f"{name}{L}", shape, dt))

        def flow(kind):
            f = Names()
            f.onehot = scope.sem(f"{kind}{L}_onehot")
            f.slots = scope.sem(f"{kind}{L}_slots")
            f.index = scope.sem(f"{kind}{L}_index")
            f.turned = scope.sem(f"{kind}{L}_turned")
            f.xt_a = scope.sem(f"{kind}{L}_xt_a")
            f.xt_d = scope.sem(f"{kind}{L}_xt_d")
            f.gate_up = scope.sem(f"{kind}{L}_gate_up")
            f.exp = scope.sem(f"{kind}{L}_exp")
            f.hidden = scope.sem(f"{kind}{L}_hidden")
            f.h_turned = scope.sem(f"{kind}{L}_h_turned")
            f.ht = scope.sem(f"{kind}{L}_ht")
            f.down = scope.sem(f"{kind}{L}_down")
            f.y_a = scope.sem(f"{kind}{L}_y_a")
            f.y_d = scope.sem(f"{kind}{L}_y_d")
            f.settled = scope.sem(f"{kind}{L}_settled")
            f.steps = scope.sem(f"{kind}{L}_steps")
            f.gathered = [scope.sem(f"{kind}{L}_gathered{s}") for s in range(4)]
            f.stored = [scope.sem(f"{kind}{L}_stored{s}") for s in range(4)]
            f.given = 0 if kind == "base" else 1
            return f

        xt_room = K.XT[:].rearrange("p k t -> p (k t)")

        def buffers(kind, bank, two, four, eight):
            b = Names()
            b.onehot = [sb(f"{kind}_onehot{s}", [P, NT, 2, SLOTS], BF16) for s in range(two)]
            b.tok_f = [sb(f"{kind}_tokf{s}", [P, 1]) for s in range(two)]
            b.tok = [sb(f"{kind}_tok{s}", [P, 1], I32) for s in range(eight)]
            b.row = [sb(f"{kind}_row{s}", [P, 1], I32) for s in range(eight)]
            b.xg = [xt_room[:, s * D:(s + 1) * D] for s in range(4)] if kind == "b" else [sb(f"{kind}_xg", [P, D])[:]]
            b.xt = [sb(f"{kind}_xt{s}", [P, KD, P]) for s in range(two)]
            b.y = [sb(f"{kind}_y{s}", [P, D]) for s in range(four)]
            b.ex, b.gu, b.h = sb(f"{kind}_ex", [P, FE]), sb(f"{kind}_gu", [P, FE]), sb(f"{kind}_h", [P, FE])
            b.ht = sb(f"{kind}_ht", [P, 2, P])
            b.slots = bank
            return b

        base, extra = flow("base"), flow("extra")
        bb, xb = buffers("b", B[4][:, 0:4], 2, 4, UNROLL), buffers("x", B[7][:, 0:4], 1, 1, 1)
        cleared = scope.sem(f"cleared{L}")

        def through(f, n, s):
            return 4 * (n - s) + 16 if f is base else n * 16 + 16

        def one_hot(dve, f, b, s, pair, level):
            for t in range(NT):
                last = dve.tensor_tensor(
                    b.onehot[s][:, t], K.rank[:, t, bass.ds(pair * 2, 2)].unsqueeze(2).to_broadcast([P, 2, SLOTS]),
                    K.iota_s[:, bass.ds(level * SLOTS, SLOTS)].unsqueeze(1).to_broadcast([P, 2, SLOTS]), ALU.is_equal)
            last.then_inc(f.onehot, 1)

        def slot_rows(pe, f, b, s, n, pair):
            pe.wait_ge(f.onehot, n + 1)
            for t in range(NT):
                last = pe.matmul(b.slots, b.onehot[s][:, t].rearrange("p a s -> p (a s)"), K.slot_cols[:, t, pair, :]
                                 if isinstance(pair, int) else K.slot_cols[:, t, bass.ds(pair, 1), :].rearrange("p i c -> p (i c)"),
                                 start=(t == 0), stop=(t == NT - 1))
            last.then_inc(f.slots, 1)

        def index_rows(dve, f, b, s, s4, n, step):
            dve.wait_ge(f.slots, n + 1)
            step(dve.tensor_scalar(b.tok_f[s][:], b.slots[:, 0:1], float(NOBODY), b.slots[:, 1:2], ALU.add, ALU.add))
            dve.tensor_copy(b.tok[s4][:], b.tok_f[s][:])
            for a in range(2):
                h = slice(64 * a, 64 * a + 64)
                last = dve.tensor_tensor(b.row[s4][h, :], b.slots[h, 2 + a:3 + a], b.tok_f[s][h, :], ALU.add)
            last.then_inc(f.index, 1)

        def held(eng, value):
            return value if isinstance(value, int) else eng.to_reg(value)

        def gather(pool, f, b, s, s4, n):
            value = held(pool, n + 1)
            pool.wait_ge(cleared, 1)
            pool.wait_ge(f.index, value)
            pool.indirect_dma_start(out=b.xg[s], out_offset=None, in_=K.x_rows,
                                    in_offset=bass.IndirectOffsetOnAxis(ap=b.tok[s4][:], axis=0),
                                    bounds_check=T - 1, oob_is_err=False).then_inc(f.gathered[s], 16)

        def turn_x(pe, f, b, s4, s, n):
            pe.wait_ge(f.gathered[s4], through(f, n, s4))
            xk = b.xg[s4].rearrange("p (q k) -> p k q", k=KD)
            for k in range(KD):
                ins = pe.transpose(B[k // 4][:, (k % 4) * P:(k % 4 + 1) * P], xk[:, k, :], ident[:])
                if k % 4 == 3:
                    ins.then_inc(f.turned, 1)

        def keep_xt(eng, f, b, s, n, half):
            eng.wait_ge(f.turned, 2 * n + 1 + half)
            dst = b.xt[s][:, 4 * half:4 * half + 4, :].rearrange("p k t -> p (k t)")
            if half == 0:
                eng.activation(dst, B[0][:], ACT.Copy).then_inc(f.xt_a, 1)
            else:
                eng.tensor_copy(dst, B[1][:]).then_inc(f.xt_d, 1)

        def gate_up(pe, f, b, s, n, w):
            pe.wait_ge(f.xt_a, n + 1)
            pe.wait_ge(f.xt_d, n + 1)
            for k in range(KD):
                for a in range(2):
                    rhs = K.W[:, w, a, 0:2, k * FE:(k + 1) * FE]
                    last = pe.matmul(B[2][64 * a:64 * a + 64, :], b.xt[s][:, k, 64 * a:64 * a + 64], rhs,
                                     start=(k == 0), stop=(k == KD - 1))
            last.then_inc(f.gate_up, 1)

        def neg_exp(act, f, b, n):
            act.wait_ge(f.gate_up, n + 1 + f.given)
            act.activation(b.ex[:], B[2][:, 0:FE], ACT.Exp, scale=-1.0).then_inc(f.exp, 1)

        def hidden(dve, f, b, n, step):
            dve.wait_ge(f.exp, n + 1)
            step(dve.tensor_scalar_add(b.ex[:], b.ex[:], 1.0))
            step(dve.reciprocal(b.ex[:], b.ex[:]))
            step(dve.tensor_tensor(b.gu[:], b.ex[:], B[2][:, 0:FE], ALU.mult))
            dve.tensor_tensor(b.h[:], b.gu[:], B[2][:, FE:2 * FE], ALU.mult).then_inc(f.hidden, 1)

        def turn_h(pe, f, b, n):
            pe.wait_ge(f.hidden, n + 1)
            hk = b.h[:].rearrange("p (q j) -> p j q", j=2)
            for j in range(2):
                last = pe.transpose(B[3][:, j * P:(j + 1) * P], hk[:, j, :], ident[:])
            last.then_inc(f.h_turned, 1)

        def keep_ht(dve, f, b, n):
            dve.wait_ge(f.h_turned, n + 1)
            dve.tensor_copy(b.ht[:].rearrange("p j t -> p (j t)"), B[3][:, 0:2 * P]).then_inc(f.ht, 1)

        def down(pe, f, b, n, w):
            pe.wait_ge(f.ht, n + 1)
            for half in range(2):
                for j in range(2):
                    for a in range(2):
                        last = pe.matmul(B[5 + half][64 * a:64 * a + 64, :], b.ht[:, j, 64 * a:64 * a + 64],
                                         K.W[:, w, a, 2, j * D + half * 512:j * D + half * 512 + 512],
                                         start=(j == 0), stop=(j == 1))
                last.then_inc(f.down, 1)

        def keep_y(eng, f, b, s, n, half):
            eng.wait_ge(f.down, 2 * (n + f.given) + 1 + half)
            dst = b.y[s][:, half * 512:half * 512 + 512]
            if half == 0:
                eng.activation(dst, B[5][:], ACT.Copy).then_inc(f.y_a, 1)
            else:
                eng.tensor_copy(dst, B[6][:]).then_inc(f.y_d, 1)

        def scatter(pool, f, b, s, s4, n):
            value = held(pool, n + 1)
            pool.wait_ge(cleared, 1)
            pool.wait_ge(f.y_a, value)
            pool.wait_ge(f.y_d, value)
            pool.indirect_dma_start(out=K.y_rows, out_offset=bass.IndirectOffsetOnAxis(ap=b.row[s4][:], axis=0),
                                    in_=b.y[s][:], in_offset=None,
                                    bounds_check=TOPK * T - 1, oob_is_err=False).then_inc(f.stored[s], 16)

        def overflow(eng, i, body):
            n = eng.value_load(K.extra_n[0:1, bass.ds(i, 1)], min_val=0, max_val=EXTRA)
            with eng.If(n > 0):
                before = eng.value_load(K.extra_upto[0:1, bass.ds(i, 1)], min_val=0, max_val=MAX_EXTRA)
                with eng.Fori(1, n + 1) as level:
                    body(before + level - 1, level)
                eng.nop()
            with eng.Else():
                eng.nop()

        def loop(eng, body):
            for u in range(UNROLL):
                body(u, u)
            with eng.Fori(1, PAIRS // UNROLL) as turn:
                for u in range(UNROLL):
                    body(turn * UNROLL + u, u)

        with nc.Block() as block:
            @block.sync
            def _(sp):
                def refill(i, u):
                    done = sp.value_load(K.extra_upto[0:1, bass.ds(i + 1, 1)], min_val=0, max_val=MAX_EXTRA)
                    used, used_extra = held(sp, i + 1), held(sp, done + extra.given)
                    used2, used2_extra = held(sp, 2 * (i + 1)), held(sp, (done + extra.given) * 2)
                    sp.wait_ge(base.gate_up, 1)
                    sp.wait_ge(base.gate_up, used)
                    sp.wait_ge(extra.gate_up, used_extra)
                    load_pair(K, sp, L, i + 2, u % 2, (0, 1))
                    sp.wait_ge(base.down, 2)
                    sp.wait_ge(base.down, used2)
                    sp.wait_ge(extra.down, used2_extra)
                    load_pair(K, sp, L, i + 2, u % 2, (2,))

                with sp.Fori(0, PAIRS // 2 - 1) as turn:
                    for u in range(2):
                        refill(turn * 2 + u, u)

            @block.gpsimd
            def _(pool):
                for s in range(4):
                    pool.memset(bb.xg[s], 0.0)
                pool.memset(xb.xg[0], 0.0).then_inc(cleared, 1)
                pool.sem_inc(extra.settled, extra.given)
                pool.wait_ge(cleared, 1)
                for n in range(AHEAD):
                    gather(pool, base, bb, n, n, n)

                def pair(i, u):
                    wait_from(pool, base.turned, 2 * i)
                    gather(pool, base, bb, (u + AHEAD) % 4, (u + AHEAD) % UNROLL, i + AHEAD)
                    scatter(pool, base, bb, u % 4, u, i)

                    def more(x, level):
                        gather(pool, extra, xb, 0, 0, x)
                        scatter(pool, extra, xb, 0, 0, x)
                        pool.wait_ge(extra.stored[0], through(extra, x, 0))
                        pool.sem_inc(extra.settled, 1)
                    overflow(pool, i, more)

                loop(pool, pair)
                for s in range(4):
                    pool.wait_ge(base.stored[s], through(base, PAIRS - 4 + s, s))
                    pool.wait_ge(base.gathered[s], through(base, PAIRS + (s if s < AHEAD else s - 4), s))
                total = pool.value_load(K.extra_upto[0:1, PAIRS:PAIRS + 1], min_val=0, max_val=MAX_EXTRA)
                pool.wait_ge(extra.settled, total + 1)

            @block.tensor
            def _(pe):
                pe.sem_inc(extra.gate_up, extra.given)
                pe.sem_inc(extra.down, 2 * extra.given)
                for n in range(AHEAD + 1):
                    if n:
                        pe.wait_ge(base.index, n)
                    slot_rows(pe, base, bb, n % 2, n, n)
                turn_x(pe, base, bb, 0, 0, 0)

                def pair(i, u):
                    w = u % 2
                    pe.wait_ge(K.w_gu[w], K.w_gu_base + 32 * (i // 2 + 1) if isinstance(i, int) else K.w_gu_base + i * 16 - 16 * w + 32)
                    gate_up(pe, base, bb, u % 2, i, w)
                    turn_x(pe, base, bb, (u + 1) % 4, (u + 1) % 2, i + 1)
                    pe.wait_ge(base.index, i + AHEAD + 1)
                    slot_rows(pe, base, bb, (u + AHEAD + 1) % 2, i + AHEAD + 1, i + AHEAD + 1)
                    turn_h(pe, base, bb, i)
                    pe.wait_ge(K.w_dn[w], K.w_dn_base + 16 * (i // 2 + 1) if isinstance(i, int) else K.w_dn_base + i * 8 - 8 * w + 16)
                    wait_from(pe, base.y_a, i)
                    wait_from(pe, base.y_d, i)
                    down(pe, base, bb, i, w)

                    def more(x, level):
                        slot_rows(pe, extra, xb, 0, x, i)
                        pe.wait_ge(base.xt_a, i + 2)
                        pe.wait_ge(base.xt_d, i + 2)
                        turn_x(pe, extra, xb, 0, 0, x)
                        gate_up(pe, extra, xb, 0, x, w)
                        turn_h(pe, extra, xb, x)
                        pe.wait_ge(base.y_a, i + 1)
                        pe.wait_ge(base.y_d, i + 1)
                        down(pe, extra, xb, x, w)
                        pe.wait_ge(extra.y_a, x + 1)
                        pe.wait_ge(extra.y_d, x + 1)
                    overflow(pe, i, more)

                loop(pe, pair)

            @block.scalar
            def _(act):
                keep_xt(act, base, bb, 0, 0, 0)

                def pair(i, u):
                    wait_from(act, base.hidden, i)
                    neg_exp(act, base, bb, i)
                    keep_xt(act, base, bb, (u + 1) % 2, i + 1, 0)
                    wait_from(act, base.stored[u % 4], through(base, i - 4, u % 4))
                    keep_y(act, base, bb, u % 4, i, 0)

                    def more(x, level):
                        keep_xt(act, extra, xb, 0, x, 0)
                        neg_exp(act, extra, xb, x)
                        act.wait_ge(extra.settled, x + 1)
                        keep_y(act, extra, xb, 0, x, 0)
                    overflow(act, i, more)

                loop(act, pair)

            @block.vector
            def _(dve):
                step = Chain(dve, base.steps)
                one_hot(dve, base, bb, 0, 0, 0)
                one_hot(dve, base, bb, 1, 1, 0)
                for n in range(AHEAD + 1):
                    index_rows(dve, base, bb, n % 2, n, n, step)
                    one_hot(dve, base, bb, n % 2, n + 2, 0)
                keep_xt(dve, base, bb, 0, 0, 1)
                start = step.n

                def pair(i, u):
                    step = Chain(dve, base.steps, start + i * PAIR_STEPS)
                    hidden(dve, base, bb, i, step)
                    keep_xt(dve, base, bb, (u + 1) % 2, i + 1, 1)
                    keep_ht(dve, base, bb, i)
                    wait_from(dve, base.stored[u % 4], through(base, i - 4, u % 4))
                    n = i + AHEAD + 1
                    index_rows(dve, base, bb, (u + AHEAD + 1) % 2, (u + AHEAD + 1) % UNROLL, n, step)
                    one_hot(dve, base, bb, (u + AHEAD + 1) % 2, n + 2, 0)
                    keep_y(dve, base, bb, u % 4, i, 1)

                    def more(x, level):
                        step = Chain(dve, extra.steps, x * PAIR_STEPS)
                        one_hot(dve, extra, xb, 0, i, level)
                        dve.wait_ge(extra.settled, x + 1)
                        index_rows(dve, extra, xb, 0, 0, x, step)
                        keep_xt(dve, extra, xb, 0, x, 1)
                        hidden(dve, extra, xb, x, step)
                        keep_ht(dve, extra, xb, x)
                        keep_y(dve, extra, xb, 0, x, 1)
                    overflow(dve, i, more)

                loop(dve, pair)


def combine(K, L):
    nc, X = K.nc, K.X
    with Phase(nc) as scope:
        def sb(name, shape, dt=F32):
            return scope.enter_context(nc.sbuf_tensor(f"{name}{L}", shape, dt))

        def sem(name):
            return scope.sem(f"combine{L}_{name}")
        rows = [sb(f"rows{s}", [P, TOPK, D]) for s in range(2)]
        loaded = [sem("rows0"), sem("rows1")]
        added = sem("added")
        ln = LayerNorm(K, scope, f"ln2_{L}", K.in_["ln2_g"][L:L + 1, :], K.in_["ln2_b"][L:L + 1, :])
        y = K.y_rows.rearrange("(j t p) d -> t p j d", j=TOPK, p=P)
        with nc.Block() as block:
            @block.sync
            def _(sp):
                ln.load(sp)
                for t in range(NT):
                    if t >= 2:
                        sp.wait_ge(added, TOPK * (t - 1))
                    sp.dma_start(rows[t % 2][:], y[t]).then_inc(loaded[t % 2], 16)

            @block.vector
            def _(dve):
                for t in range(NT):
                    dve.wait_ge(loaded[t % 2], 16 * (t // 2 + 1))
                    for j in range(TOPK):
                        dve.scalar_tensor_tensor(X[:, t, :], rows[t % 2][:, j, :], K.gates[:, t, j:j + 1], X[:, t, :],
                                                 ALU.mult, ALU.add).then_inc(added, 1)
                        dve.wait_ge(added, TOPK * t + j + 1)
                    ln.normalize(dve, X[:, t, :], t)

            @block.scalar
            def _(act):
                for t in range(NT):
                    ln.root(act, t)

            @block.gpsimd
            def _(pool):
                for t in range(NT):
                    ln.affine(pool, X[:, t, :], t)


class LayerNorm:

    def __init__(self, K, scope, name, g, b):
        nc = K.nc
        self.src = (g, b)
        self.g = scope.enter_context(nc.sbuf_tensor(f"{name}_g", [P, D], F32))
        self.b = scope.enter_context(nc.sbuf_tensor(f"{name}_b", [P, D], F32))
        self.stats = scope.enter_context(nc.sbuf_tensor(f"{name}_stats", [P, 2, 6], F32))
        self.mv = scope.enter_context(nc.sbuf_tensor(f"{name}_mv", [P, 2], F32))
        self.rstd = scope.enter_context(nc.sbuf_tensor(f"{name}_rstd", [P, 1], F32))
        self.loaded = scope.sem(f"{name}_loaded")
        self.steps = scope.sem(f"{name}_steps")
        self.normal = scope.sem(f"{name}_normal")
        self.rooted = scope.sem(f"{name}_rooted")
        self.done = scope.sem(f"{name}_done")

    def load(self, eng):
        for dst, src in zip((self.g, self.b), self.src):
            eng.dma_start(dst[:], src.broadcast_to([P, D])).then_inc(self.loaded, 16)

    def normalize(self, dve, x, t):
        step = Chain(dve, self.steps, t * 4)
        dve.bn_stats(self.stats[:, 0, :], x[:, 0:512])
        step(dve.bn_stats(self.stats[:, 1, :], x[:, 512:D]))
        step(dve.bn_aggr(self.mv[:], self.stats[:].rearrange("p a b -> p (a b)")))
        step(dve.tensor_scalar_add(self.rstd[:], self.mv[:, 1:2], LN_EPS))
        dve.wait_ge(self.rooted, t + 1)
        step(dve.reciprocal(self.rstd[:], self.rstd[:]))
        ins = dve.tensor_scalar(x, x, self.mv[:, 0:1], self.rstd[:], ALU.subtract, ALU.mult)
        ins.then_inc(self.normal, 1)
        dve.wait_ge(self.normal, t + 1)

    def root(self, act, t):
        act.wait_ge(self.steps, 4 * t + 3)
        act.activation(self.rstd[:], self.rstd[:], ACT.Sqrt).then_inc(self.rooted, 1)

    def affine(self, pool, x, t):
        if t == 0:
            pool.wait_ge(self.loaded, 32)
        pool.wait_ge(self.normal, t + 1)
        pool.tensor_tensor(x, x, self.g[:], ALU.mult).then_inc(self.done, 1)
        pool.wait_ge(self.done, 2 * t + 1)
        pool.tensor_tensor(x, x, self.b[:], ALU.add).then_inc(self.done, 1)


class Turner:

    def __init__(self, K, scope, name, src, dst, n_tiles):
        self.K, self.dst, self.n_tiles = K, dst, n_tiles
        self.src = src.rearrange("p t (q k) -> p t k q", k=KD)
        self.turned = scope.sem(f"{name}_turned")
        self.by_act = scope.sem(f"{name}_by_act")
        self.by_dve = scope.sem(f"{name}_by_dve")

    def turn(self, pe):
        for k in range(KD):
            if k >= 4:
                pe.wait_ge(self.by_dve if k % 2 else self.by_act, (k - 4) // 2 + 1)
            for t in range(self.n_tiles):
                last = pe.transpose(self.K.banks[k % 4][:, t * P:(t + 1) * P], self.src[:, t, k, :], self.K.ident[:])
            last.then_inc(self.turned, 1)

    def copy_even(self, act):
        for k in range(0, KD, 2):
            act.wait_ge(self.turned, k + 1)
            act.activation(self.dst[:, k, :], self.K.banks[k % 4][:, 0:self.n_tiles * P], ACT.Copy).then_inc(self.by_act, 1)

    def copy_odd(self, dve):
        for k in range(1, KD, 2):
            dve.wait_ge(self.turned, k + 1)
            dve.tensor_copy(self.dst[:, k, :], self.K.banks[k % 4][:, 0:self.n_tiles * P]).then_inc(self.by_dve, 1)

    def await_all(self, eng):
        eng.wait_ge(self.by_act, KD // 2)
        eng.wait_ge(self.by_dve, KD // 2)


def memory_keys(K):
    nc, B = K.nc, K.banks
    NM = NMEM // P
    with Phase(nc) as scope:
        def sb(name, shape, dt=F32):
            return scope.enter_context(nc.sbuf_tensor(name, shape, dt))

        def sem(name):
            return scope.sem(f"mem_{name}")

        M = sb("mem", [P, NM, D])
        MT = sb("memT", [P, KD, NMEM])
        w = sb("w_mem", [P, KD, 2 * MEMW])
        ln = LayerNorm(K, scope, "mem_ln", K.in_["mem_ln_g"].rearrange("(a d) -> a d", a=1),
                       K.in_["mem_ln_b"].rearrange("(a d) -> a d", a=1))
        turner = Turner(K, scope, "mem_turn", M[:], MT, NM)
        loaded, loaded_w, made, kept = sem("loaded"), sem("loaded_w"), sem("made"), sem("kept")
        with nc.Block() as block:
            @block.sync
            def _(sp):
                sp.dma_start(M[:], K.in_["mem"][0].rearrange("(t p) d -> p t d", p=P)).then_inc(loaded, 16)
                ln.load(sp)
                sp.dma_start(K.X[:], K.in_["x"][0].rearrange("(t p) d -> p t d", p=P)).then_inc(K.x_loaded, 16)
                sp.dma_start(w[:], K.in_["w_mem_kv"].rearrange("(p k) n -> p k n", k=KD)).then_inc(loaded_w, 16)
                sp.wait_ge(K.x_loaded, 16)

            @block.vector
            def _(dve):
                dve.wait_ge(loaded, 16)
                for t in range(NM):
                    ln.normalize(dve, M[:, t, :], t)
                turner.copy_odd(dve)
                for j in range(2):
                    dve.wait_ge(made, 3 + j)
                    dve.tensor_copy(K.v_mem[:, j, :], B[6 + j][:, 0:MEMW]).then_inc(kept, 1)

            @block.scalar
            def _(act):
                for t in range(NM):
                    ln.root(act, t)
                turner.copy_even(act)
                for j in range(2):
                    act.wait_ge(made, j + 1)
                    for o in range(2):
                        act.activation(K.k_memT[:, 2 * j + o, :], B[4 + j][o * HD:(o + 1) * HD, 0:NMEM], ACT.Copy).then_inc(kept, 1)

            @block.gpsimd
            def _(pool):
                for t in range(NM):
                    ln.affine(pool, M[:, t, :], t)

            @block.tensor
            def _(pe):
                pe.wait_ge(ln.done, 2 * NM)
                turner.turn(pe)
                turner.await_all(pe)
                pe.wait_ge(loaded_w, 16)
                for j in range(2):
                    for k in range(KD):
                        last = pe.matmul(B[4 + j][:, 0:NMEM], w[:, k, j * P:(j + 1) * P], MT[:, k, :], start=(k == 0), stop=(k == KD - 1))
                    last.then_inc(made, 1)
                for j in range(NM):
                    for k in range(KD):
                        last = pe.matmul(B[6 + j][:, 0:MEMW], MT[:, k, j * P:(j + 1) * P], w[:, k, MEMW:2 * MEMW], start=(k == 0), stop=(k == KD - 1))
                    last.then_inc(made, 1)


WC = 256


def fox_layer(K, L, j):
    nc, B, arena = K.nc, K.banks, K.arena
    at = [0]

    def carve(parts, shape):
        n = int(np.prod(shape))
        view = arena[0:parts, at[0]:at[0] + n]
        at[0] += n
        return view.rearrange("p (a b) -> p a b", a=shape[0])

    HK = HD + 1
    qT = carve(HK, (NH, T))
    kT = carve(HK, (NH, T))
    v = carve(P, (NT, TOKW))
    sg = carve(P, (NT, TOKW))
    qmT = carve(HD, (NMH, T))
    mix = carve(P, (NT, D))
    w_in = K.in_["fox_w_in"][j].rearrange("(p k) n -> p k n", k=KD)

    with Phase(nc) as scope:
        def sb(name, shape, dt=F32):
            return scope.enter_context(nc.sbuf_tensor(name, shape, dt))

        def sem(name):
            return scope.sem(f"foxin_{name}")

        NB = 4
        wc = [sb(f"foxw{s}", [P, KD, WC]) for s in range(NB)]
        wf = sb("foxwf", [P, KD, NH])
        bf = sb("foxbf", [P, 1, NH])
        fl = sb("foxfl", [P, NT, NH])
        ab = sb("foxab", [P, NT, NH])
        cT = sb("foxcT", [NH, T])
        chunks = [("q", c) for c in range(3)] + [("k", c) for c in range(3)] + [("v", c) for c in range(3)] \
            + [("g", c) for c in range(3)] + [("m", 0)]
        first_col = {"q": 0, "k": TOKW, "v": 2 * TOKW, "g": 3 * TOKW, "m": 4 * TOKW + NH}
        turner = Turner(K, scope, "fox_turn", K.X[:], K.XT, NT)
        loaded = [sem(f"loaded{s}") for s in range(NB)]
        loaded_f, made, kept_a, kept_d = sem("loaded_f"), sem("made"), sem("kept_a"), sem("kept_d")
        f_made, f_steps, f_act, c_made, c_kept, c_moved = (sem(n) for n in ("f_made", "f_steps", "f_act", "c_made", "c_kept", "c_moved"))
        ones_row = sem("ones_row")

        with nc.Block() as block:
            @block.sync
            def _(sp):
                sp.dma_start(wf[:], w_in[:, :, 4 * TOKW:4 * TOKW + NH]).then_inc(loaded_f, 16)
                sp.dma_start(bf[:, 0, :], K.in_["fox_b_f"][j:j + 1, :].broadcast_to([P, NH])).then_inc(loaded_f, 16)
                for n, (kind, c) in enumerate(chunks):
                    if n >= NB:
                        sp.wait_ge(made, 2 * (n - NB + 1))
                    c0 = first_col[kind] + c * WC
                    sp.dma_start(wc[n % NB][:], w_in[:, :, c0:c0 + WC]).then_inc(loaded[n % NB], 16)
                sp.wait_ge(c_kept, 1)
                sp.wait_ge(ones_row, 1)
                sp.dma_start(kT[HD:HK, :, :].rearrange("p h t -> p (h t)"), cT[:, :]).then_inc(c_moved, 16)
                sp.wait_ge(c_moved, 16)

            @block.gpsimd
            def _(pool):
                pool.memset(qT[HD:HK], 1.0).then_inc(ones_row, 1)

            @block.tensor
            def _(pe):
                turner.turn(pe)
                turner.await_all(pe)
                pe.wait_ge(loaded_f, 32)
                for t in range(NT):
                    for k in range(KD):
                        last = pe.matmul(B[0][:, t * NH:(t + 1) * NH], K.XT[:, k, t * P:(t + 1) * P], wf[:, k, :],
                                         start=(k == 0), stop=(k == KD - 1))
                last.then_inc(f_made, 1)
                for n, (kind, c) in enumerate(chunks):
                    pe.wait_ge(loaded[n % NB], 16 * (n // NB + 1))
                    for o in range(2):
                        bank = B[4 + (2 * n + o) % 4]
                        if n >= 2:
                            pe.wait_ge(kept_a if o == 0 else kept_d, n - 1)
                        if kind in "qkm":
                            for k in range(KD):
                                last = pe.matmul(bank[:], wc[n % NB][:, k, o * P:(o + 1) * P], K.XT[:, k, :],
                                                 start=(k == 0), stop=(k == KD - 1))
                        else:
                            for t in range(2):
                                for k in range(KD):
                                    tt = 2 * o + t
                                    last = pe.matmul(bank[:, t * WC:(t + 1) * WC], K.XT[:, k, tt * P:(tt + 1) * P], wc[n % NB][:, k, :],
                                                     start=(k == 0), stop=(k == KD - 1))
                        last.then_inc(made, 1)
                    if n == 4:
                        pe.wait_ge(f_steps, 4)
                        for t in range(NT):
                            for t0 in range(t + 1):
                                last = pe.matmul(B[1][0:NH, t * P:(t + 1) * P], fl[:, t0, :], (K.upto if t0 == t else K.ones)[:],
                                                 start=(t0 == 0), stop=(t0 == t))
                        last.then_inc(c_made, 1)

            def keep(eng, o, is_act, kept):
                for n, (kind, c) in enumerate(chunks):
                    eng.wait_ge(made, 2 * n + 1 + o)
                    bank = B[4 + (2 * n + o) % 4]
                    if kind in "qkm":
                        dst = {"q": qT, "k": kT, "m": qmT}[kind]
                        for e in range(2):
                            out, src = dst[0:HD, 4 * c + 2 * o + e, :], bank[e * HD:(e + 1) * HD, :]
                            last = eng.activation(out, src, ACT.Copy) if is_act else eng.tensor_copy(out, src)
                    else:
                        dst = (v if kind == "v" else sg)[:, 2 * o:2 * o + 2, c * WC:(c + 1) * WC]
                        src = bank[:].rearrange("p (t c) -> p t c", t=2)
                        if kind == "g":
                            last = eng.activation(dst, src, ACT.Exp, scale=-1.0) if is_act else eng.tensor_copy(dst, src)
                        else:
                            last = eng.activation(dst, src, ACT.Copy) if is_act else eng.tensor_copy(dst, src)
                    last.then_inc(kept, 1)
                    yield n

            @block.scalar
            def _(act):
                turner.copy_even(act)
                for n in keep(act, 0, True, kept_a):
                    if n == 0:
                        act.wait_ge(f_steps, 2)
                        act.activation(ab[:], ab[:], ACT.Exp, scale=-1.0).then_inc(f_act, 1)
                    if n == 1:
                        act.wait_ge(f_steps, 3)
                        act.activation(ab[:], ab[:], ACT.Ln).then_inc(f_act, 1)
                act.wait_ge(kept_d, len(chunks))
                act.activation(sg[:, 2:4, :], sg[:, 2:4, :], ACT.Exp, scale=-1.0).then_inc(f_act, 1)

            @block.vector
            def _(dve):
                step = Chain(dve, f_steps)
                turner.copy_odd(dve)
                for n in keep(dve, 1, False, kept_d):
                    if n == 0:
                        dve.wait_ge(f_made, 1)
                        step(dve.tensor_tensor(fl[:], B[0][:, 0:NT * NH].rearrange("p (t h) -> p t h", t=NT),
                                               bf[:].to_broadcast([P, NT, NH]), ALU.add))
                        step(dve.scalar_tensor_tensor(ab[:], fl[:], -1.0, fl[:], ALU.mult, ALU.max))
                        dve.wait_ge(f_act, 1)
                        step(dve.tensor_scalar_add(ab[:], ab[:], 1.0))
                        dve.wait_ge(f_act, 2)
                        step(dve.scalar_tensor_tensor(fl[:], fl[:], 0.0, ab[:], ALU.min, ALU.subtract))
                    if n == 6:
                        dve.wait_ge(c_made, 1)
                        dve.tensor_scalar_mul(cT[:], B[1][0:NH, :], -(HD ** 0.5)).then_inc(c_kept, 1)
                dve.wait_ge(f_act, 3)
                dve.wait_ge(kept_a, len(chunks))
                step(dve.tensor_scalar_add(sg[:], sg[:], 1.0))
                step(dve.reciprocal(sg[:], sg[:]))

    units = [("tok", h, t) for h in range(NH) for t in range(NT)] + [("mem", h, t) for h in range(NMH) for t in range(NT)]
    attention(K, f"att{L}", units, dict(qT=qT, kT=kT, v=v, sg=sg, qmT=qmT, mix=mix))
    output_projection(K, L, mix)


def attention(K, name, units, d):
    nc, B = K.nc, K.banks
    SCALE = HD ** -0.5
    with Phase(nc) as scope:
        def sb(nm, shape, dt=F32):
            return scope.enter_context(nc.sbuf_tensor(f"{name}_{nm}", shape, dt))

        def sem(nm):
            return scope.sem(f"{name}_{nm}")
        prob = [sb(f"prob{s}", [P, T]) for s in range(2)]
        probT = [sb(f"probT{s}", [P, T]) for s in range(2)]
        N = len(units)
        nmax = sb("nmax", [P, 2])
        total = sb("total", [P, 4])
        inv = sb("inv", [P, 2])
        scored, maxed, exped, turned, kept, weighed, out = (sem(n) for n in ("scored", "maxed", "exped", "turned", "kept", "weighed", "out"))
        steps = sem("steps")

        def keys(u):
            return P * (u[2] + 1) if u[0] == "tok" else NMEM

        with nc.Block() as block:
            @block.tensor
            def _(pe):
                def scores(n):
                    kind, h, t = units[n]
                    if n >= 2:
                        pe.wait_ge(exped, n - 1)
                    bank = B[n % 2]
                    if kind == "tok":
                        pe.matmul(bank[:, 0:keys(units[n])], d["qT"][:, h, t * P:(t + 1) * P], d["kT"][:, h, 0:keys(units[n])],
                                  start=True, stop=False, skip_group_check=True)
                        last = pe.matmul(bank[:, t * P:(t + 1) * P], K.ident16[:], K.causal[:], start=False, stop=True, skip_group_check=True)
                    else:
                        last = pe.matmul(bank[:, 0:NMEM], d["qmT"][:, h, t * P:(t + 1) * P], K.k_memT[:, h, :], start=True, stop=True)
                    last.then_inc(scored, 1)

                def turn(n):
                    pe.wait_ge(exped, n + 1)
                    if n >= 2:
                        pe.wait_ge(kept, n - 1)
                    for b in range(keys(units[n]) // P):
                        last = pe.transpose(B[2 + n % 2][:, b * P:(b + 1) * P], prob[n % 2][:, b * P:(b + 1) * P], K.ident[:])
                    last.then_inc(turned, 1)

                def weigh(n):
                    kind, h, t = units[n]
                    pe.wait_ge(kept, n + 1)
                    if n >= 2:
                        pe.wait_ge(out, n - 1)
                    val = d["v"] if kind == "tok" else K.v_mem
                    nb = keys(units[n]) // P
                    for b in range(nb):
                        last = pe.matmul(B[4 + n % 2][:, 0:HD], probT[n % 2][:, b * P:(b + 1) * P], val[:, b, h * HD:(h + 1) * HD],
                                         start=(b == 0), stop=(b == nb - 1))
                    last.then_inc(weighed, 1)

                for n in range(N + 2):
                    if n < N:
                        scores(n)
                    if 1 <= n <= N:
                        turn(n - 1)
                    if n >= 2:
                        weigh(n - 2)

            @block.scalar
            def _(act):
                for n in range(N + 1):
                    if n < N:
                        act.wait_ge(maxed, n + 1)
                        if n >= 2:
                            act.wait_ge(turned, n - 1)
                        if n >= 4:
                            act.wait_ge(out, n - 3)
                        w = keys(units[n])
                        act.activation(prob[n % 2][:, 0:w], B[n % 2][:, 0:w], ACT.Exp, bias=nmax[:, n % 2:n % 2 + 1], scale=SCALE,
                                       accum_out=total[:, n % 4:n % 4 + 1]).then_inc(exped, 1)
                    if n >= 1:
                        m = n - 1
                        act.wait_ge(turned, m + 1)
                        if m >= 2:
                            act.wait_ge(weighed, m - 1)
                        w = keys(units[m])
                        act.activation(probT[m % 2][:, 0:w], B[2 + m % 2][:, 0:w], ACT.Copy).then_inc(kept, 1)

            @block.vector
            def _(dve):
                step = Chain(dve, steps)
                for n in range(N + 2):
                    if n < N:
                        dve.wait_ge(scored, n + 1)
                        if n >= 2:
                            dve.wait_ge(exped, n - 1)
                        step(dve.tensor_reduce(nmax[:, n % 2:n % 2 + 1], B[n % 2][:, 0:keys(units[n])], AX.X, ALU.max))
                        dve.tensor_scalar_mul(nmax[:, n % 2:n % 2 + 1], nmax[:, n % 2:n % 2 + 1], -SCALE).then_inc(maxed, 1)
                    if n >= 2:
                        m = n - 2
                        kind, h, t = units[m]
                        dve.wait_ge(exped, m + 1)
                        step(dve.reciprocal(inv[:, m % 2:m % 2 + 1], total[:, m % 4:m % 4 + 1]))
                        dve.wait_ge(weighed, m + 1)
                        o = B[4 + m % 2][:, 0:HD]
                        if kind == "tok":
                            dve.scalar_tensor_tensor(d["mix"][:, t, h * HD:(h + 1) * HD], o, inv[:, m % 2:m % 2 + 1],
                                                     d["sg"][:, t, h * HD:(h + 1) * HD], ALU.mult, ALU.mult).then_inc(out, 1)
                        else:
                            dve.tensor_scalar_mul(d["mix"][:, t, TOKW + h * HD:TOKW + (h + 1) * HD], o, inv[:, m % 2:m % 2 + 1]).then_inc(out, 1)


def output_projection(K, L, mix):
    nc, B, X = K.nc, K.banks, K.X
    with Phase(nc) as scope:
        w = scope.enter_context(nc.sbuf_tensor(f"w_out{L}", [P, KD, D], F32))
        ln = LayerNorm(K, scope, f"ln1_{L}", K.in_["ln1_g"][L:L + 1, :], K.in_["ln1_b"][L:L + 1, :])
        turner = Turner(K, scope, f"mix_turn{L}", mix, K.XT, NT)
        loaded, made, added = (scope.sem(f"outp{L}_{n}") for n in ("loaded", "made", "added"))
        with nc.Block() as block:
            @block.sync
            def _(sp):
                sp.dma_start(w[:], K.in_["w_out"][L].rearrange("(p k) n -> p k n", k=KD)).then_inc(loaded, 16)
                ln.load(sp)

            @block.tensor
            def _(pe):
                turner.turn(pe)
                turner.await_all(pe)
                pe.wait_ge(loaded, 16)
                for t in range(NT):
                    for n in range(2):
                        i = 2 * t + n
                        if i >= 4:
                            pe.wait_ge(added, i - 3)
                        for k in range(KD):
                            last = pe.matmul(B[4 + i % 4][:], K.XT[:, k, t * P:(t + 1) * P], w[:, k, n * 512:(n + 1) * 512],
                                             start=(k == 0), stop=(k == KD - 1))
                        last.then_inc(made, 1)

            @block.scalar
            def _(act):
                turner.copy_even(act)
                for t in range(NT):
                    ln.root(act, t)

            @block.vector
            def _(dve):
                turner.copy_odd(dve)
                for t in range(NT):
                    for n in range(2):
                        i = 2 * t + n
                        dve.wait_ge(made, i + 1)
                        xs = X[:, t, n * 512:(n + 1) * 512]
                        dve.scalar_tensor_tensor(xs, xs, ALPHA, B[4 + i % 4][:], ALU.mult, ALU.add).then_inc(added, 1)
                    dve.wait_ge(added, 2 * t + 2)
                    ln.normalize(dve, X[:, t, :], t)

            @block.gpsimd
            def _(pool):
                for t in range(NT):
                    ln.affine(pool, X[:, t, :], t)


C0 = float(np.exp(-0.5))
TILES = TOKW // P
N_VEC = 20 + 5 * TILES
MU, W0, A0, KK, KA, RK = 0, 20, 26, 32, 38, 44
GROUPS, GH = 3, 4
LEVELS = 7


def rwkv_layer(K, L, j):
    nc, B, arena = K.nc, K.banks, K.arena
    at = [0]

    def carve(parts, shape, start=None):
        n = int(np.prod(shape))
        s = at[0] if start is None else start
        if start is None:
            at[0] += n
        return arena[0:parts, s:s + n].rearrange("p (a b) -> p a b", a=shape[0])

    R = Names()
    R.AR = carve(P, (TILES * NT, 2 * P))
    R.vT = carve(P, (TILES, T), 0)
    R.bT = carve(P, (TILES, T))
    R.kT = carve(P, (TILES, T))
    R.V = carve(P, (NT, TOKW))
    rk_at = at[0]
    R.r = carve(P, (TILES, T))
    R.k = carve(P, (TILES, T))
    mix = carve(P, (NT, D), rk_at)
    R.Bt = carve(P, (1, TOKW), rk_at + NT * D)
    R.Kt = carve(P, (1, TOKW), rk_at + NT * D + TOKW)
    R.gd = carve(P, (1, T))
    qmT = carve(HD, (NMH, T))
    R.S = carve(P, (TILES, HD))
    w_in = K.in_["rwkv_w_in"][j].rearrange("(p k) n -> p k n", k=KD)

    with ExitStack() as outer:
        def sbo(name, shape, dt=F32):
            return outer.enter_context(nc.sbuf_tensor(f"rwkv_{name}", shape, dt))
        R.bonus = sbo("bonus", [P, NT, NH])
        R.f = sbo("f", [P, TILES, NT])
        g2 = sbo("g2", [P, TOKW])
        with Phase(nc) as scope:
            def sb(name, shape, dt=F32):
                return scope.enter_context(nc.sbuf_tensor(f"rwkv_{name}", shape, dt))
            R.vec = sb("vec", [P, N_VEC])
            R.neg = sb("neg", [P, 3 * TILES])
            R.lo = sb("lo", [P, T])
            R.w2a2 = sb("w2a2", [P, TOKW])
            rwkv_inputs(K, R, j, w_in, qmT, g2)
            rwkv_channels(K, R)
        rwkv_chunks(K, R, j, g2, mix)
    units = [("mem", h, t) for h in range(NMH) for t in range(NT)]
    attention(K, f"att{L}", units, dict(qmT=qmT, mix=mix))
    output_projection(K, L, mix)


def rwkv_inputs(K, R, j, w_in, qmT, g2):
    nc, B = K.nc, K.banks
    with Phase(nc) as scope:
        def sb(name, shape, dt=F32):
            return scope.enter_context(nc.sbuf_tensor(f"rin_{name}", shape, dt))

        def sem(name):
            return scope.sem(f"rin_{name}")
        NB = 3
        wc = [sb(f"w{s}", [P, KD, WC]) for s in range(NB)]
        h = [sb(f"h{s}", [P, T + 1]) for s in range(2)]
        rows = sb("rows", [N_VEC, P])
        turner = Turner(K, scope, "rin_turn", K.X[:], K.XT, NT)
        loaded = [sem(f"loaded{s}") for s in range(NB)]
        small, vec_t, vec_k, made, copied, zeroed, mixed, steps, lora = (
            sem(n) for n in ("small", "vec_t", "vec_k", "made", "copied", "zeroed", "mixed", "steps", "lora"))
        dests = [R.r[:, i, :] for i in range(6)] + [R.k[:, i, :] for i in range(6)] + [R.vT[:, i, :] for i in range(6)] \
            + [R.lo[:], R.gd[:, 0, :]]
        n_mixed, n_tiles = len(dests), len(dests) + 2
        with nc.Block() as block:
            @block.sync
            def _(sp):
                I = K.in_
                vectors = [(I["rwkv_mu"][j].rearrange("(n p) -> n p", p=P), MU)] + [
                    (I[nm][j].rearrange("(n p) -> n p", p=P), o)
                    for nm, o in (("rwkv_w0", W0), ("rwkv_a0", A0), ("rwkv_k_k", KK), ("rwkv_k_a", KA))] + [
                    (I["rwkv_r_k"][j].rearrange("(n two) d -> n (two d)", two=2), RK)]
                for src, o in vectors:
                    sp.dma_start(rows[o:o + src.shape[0], :], src).then_inc(small, 16)
                sp.dma_start(R.w2a2[0:64, :], I["rwkv_w2"][j]).then_inc(small, 16)
                sp.dma_start(R.w2a2[64:128, :], I["rwkv_a2"][j]).then_inc(small, 16)
                sp.dma_start(g2[:], I["rwkv_g2"][j]).then_inc(small, 16)
                for n in range(n_tiles // 2):
                    if n >= NB:
                        sp.wait_ge(made, 2 * (n - NB + 1))
                    sp.dma_start(wc[n % NB][:], w_in[:, :, n * WC:(n + 1) * WC]).then_inc(loaded[n % NB], 16)
                sp.wait_ge(small, 16 * 9)

            @block.tensor
            def _(pe):
                turner.turn(pe)
                pe.wait_ge(small, 16 * 9)
                turner.await_all(pe)
                pe.transpose(B[0][:, 0:N_VEC], rows[:], K.ident[0:N_VEC, 0:N_VEC]).then_inc(vec_t, 1)
                for i in range(n_tiles):
                    n, o = i // 2, i % 2
                    pe.wait_ge(loaded[n % NB], 16 * (n // NB + 1))
                    if i >= 4:
                        pe.wait_ge(copied, i - 3)
                    for k in range(KD):
                        last = pe.matmul(B[4 + i % 4][:], wc[n % NB][:, k, o * P:(o + 1) * P], K.XT[:, k, :],
                                         start=(k == 0), stop=(k == KD - 1))
                    last.then_inc(made, 1)

            @block.gpsimd
            def _(pool):
                for s in range(2):
                    last = pool.memset(h[s][:, 0:1], 0.0)
                last.then_inc(zeroed, 1)

            @block.scalar
            def _(act):
                turner.copy_even(act)
                for i in range(n_tiles):
                    act.wait_ge(made, i + 1)
                    if i < n_mixed:
                        if i >= 2:
                            act.wait_ge(mixed, i - 1)
                        act.activation(h[i % 2][:, 1:T + 1], B[4 + i % 4][:], ACT.Copy).then_inc(copied, 1)
                    else:
                        for e in range(2):
                            last = act.activation(qmT[:, 2 * (i - n_mixed) + e, :], B[4 + i % 4][e * HD:(e + 1) * HD, :], ACT.Copy)
                        last.then_inc(copied, 1)
                act.wait_ge(mixed, n_mixed)
                act.activation(R.lo[0:64, :], R.lo[0:64, :], ACT.Tanh)
                act.activation(R.gd[:, 0, :], R.gd[:, 0, :], ACT.Exp, scale=-1.0).then_inc(lora, 1)

            @block.vector
            def _(dve):
                turner.copy_odd(dve)
                step = Chain(dve, steps)
                dve.wait_ge(vec_t, 1)
                step(dve.tensor_copy(R.vec[:], B[0][:, 0:N_VEC]))
                step.inc(dve.tensor_scalar_mul(R.neg[:, 0:2 * TILES], R.vec[:, W0:W0 + 2 * TILES], -1.0))
                step(dve.tensor_scalar(R.neg[:, 2 * TILES:], R.vec[:, KA:KA + TILES], -1.0, 1.0, ALU.mult, ALU.add))
                dve.wait_ge(zeroed, 1)
                for i in range(n_mixed):
                    dve.wait_ge(copied, i + 1)
                    hi = h[i % 2]
                    step(dve.tensor_tensor(dests[i], hi[:, 0:T], hi[:, 1:T + 1], ALU.subtract))
                    dve.scalar_tensor_tensor(dests[i], dests[i], R.vec[:, MU + i:MU + i + 1], hi[:, 1:T + 1], ALU.mult, ALU.add).then_inc(mixed, 1)
                dve.wait_ge(lora, 1)
                step(dve.tensor_scalar_add(R.gd[:, 0, :], R.gd[:, 0, :], 1.0))
                step(dve.reciprocal(R.gd[:, 0, :], R.gd[:, 0, :]))


def rwkv_channels(K, R):
    nc, B = K.nc, K.banks
    with Phase(nc) as scope:
        def sb(name, shape, dt=F32):
            return scope.enter_context(nc.sbuf_tensor(f"rch_{name}", shape, dt))

        def sem(name):
            return scope.sem(f"rch_{name}")
        sq = [sb(f"sq{s}", [P, T]) for s in range(2)]
        nrm = [sb(f"nrm{s}", [P, T]) for s in range(2)]
        ew = [sb(f"ew{s}", [P, T]) for s in range(2)]
        ea = [sb(f"ea{s}", [P, T]) for s in range(2)]
        Sx = [sb(f"S{s}", [P, NT, P + 1]) for s in range(2)]
        ep = [sb(f"ep{s}", [P, NT, P + 1]) for s in range(2)]
        en = [sb(f"en{s}", [P, NT, P]) for s in range(2)]
        kf = [sb(f"kf{s}", [P, T]) for s in range(2)]
        rk = [sb(f"rk{s}", [P, T]) for s in range(2)]
        mid = [sb(f"mid{s}", [P, 2, NT]) for s in range(2)]
        fa = [sb(f"fa{s}", [P, NT - 1]) for s in range(2)]
        v_t, v_k, kk1, sqd, ssd, rooted, norm, steps = (sem(n) for n in ("v_t", "v_k", "kk1", "sqd", "ssd", "rooted", "norm", "steps"))
        lin, exps, scanned, decayed, af, rkd, bonus, zeroed, b_made, tile_done = (
            sem(n) for n in ("lin", "exps", "scanned", "decayed", "af", "rkd", "bonus", "zeroed", "b_made", "tile_done"))
        AR = R.AR.rearrange("p (i c) (x t) -> p i c x t", i=TILES, x=2)
        halves = ((0, 4), (4, 2))

        with nc.Block() as block:
            @block.tensor
            def _(pe):
                n = 0
                for t in range(NT):
                    for i0, ni in halves:
                        if n >= 4:
                            pe.wait_ge(v_k, n - 3)
                        for i in range(ni):
                            last = pe.transpose(B[n % 4][:, i * P:(i + 1) * P], R.vT[:, i0 + i, t * P:(t + 1) * P], K.ident[:])
                        last.then_inc(v_t, 1)
                        n += 1
                for i in range(TILES):
                    pe.wait_ge(sqd, i + 1)
                    if i >= 2:
                        pe.wait_ge(rooted, i - 1)
                    pe.matmul(B[4 + i % 2][:], K.heads[:], sq[i % 2][:], start=True, stop=True).then_inc(ssd, 1)
                pe.wait_ge(rooted, TILES)
                for i in range(TILES + 1):
                    if i < TILES:
                        if i >= 1:
                            pe.wait_ge(exps, 2 * i)
                        cols = slice(i * P, (i + 1) * P)
                        pe.matmul(B[4][:], R.w2a2[0:64, cols], R.lo[0:64, :], start=True, stop=True).then_inc(lin, 1)
                        pe.matmul(B[5][:], R.w2a2[64:128, cols], R.lo[64:128, :], start=True, stop=True).then_inc(lin, 1)
                    if i >= 1:
                        m = i - 1
                        pe.wait_ge(rkd, m + 1)
                        for t in range(NT):
                            last = pe.matmul(B[7][:, t * NH + 2 * m:t * NH + 2 * m + 2], rk[m % 2][:, t * P:(t + 1) * P],
                                             K.heads[:].rearrange("p (a b) -> p a b", a=2)[:, :, 0], start=True, stop=True)
                        last.then_inc(bonus, 1)

            @block.scalar
            def _(act):
                n = 0
                for t in range(NT):
                    for i0, ni in halves:
                        act.wait_ge(v_t, n + 1)
                        act.activation(R.V[:, t, i0 * P:(i0 + ni) * P], B[n % 4][:, 0:ni * P], ACT.Copy).then_inc(v_k, 1)
                        n += 1
                for i in range(TILES):
                    act.wait_ge(ssd, i + 1)
                    if i >= 2:
                        act.wait_ge(norm, i - 1)
                    act.activation(nrm[i % 2][:], B[4 + i % 2][:], ACT.Sqrt).then_inc(rooted, 1)
                for i in range(TILES):
                    s = i % 2
                    if i >= 2:
                        act.wait_ge(tile_done, i - 1)
                        act.wait_ge(b_made, i - 1)
                    act.wait_ge(lin, 2 * i + 1)
                    act.activation(ew[s][:], B[4][:], ACT.Exp, bias=R.neg[:, i:i + 1], scale=-1.0).then_inc(exps, 1)
                    act.wait_ge(lin, 2 * i + 2)
                    act.activation(ea[s][:], B[5][:], ACT.Exp, bias=R.neg[:, TILES + i:TILES + i + 1], scale=-1.0).then_inc(exps, 1)
                    act.wait_ge(scanned, i + 1)
                    for c in range(NT):
                        act.activation(ep[s][:, c, :], Sx[s][:, c, :], ACT.Exp, bias=mid[s][:, 0, c:c + 1], scale=-C0)
                        act.activation(en[s][:, c, :], Sx[s][:, c, 1:P + 1], ACT.Exp, bias=mid[s][:, 1, c:c + 1], scale=C0)
                    act.activation(R.f[:, i, 0:NT - 1], fa[s][:], ACT.Exp, scale=-C0).then_inc(decayed, 1)

            @block.gpsimd
            def _(pool):
                for s in range(2):
                    last = pool.memset(Sx[s][:], 0.0)
                last.then_inc(zeroed, 1)
                for i in range(TILES):
                    pool.wait_ge(kk1, i + 1)
                    if i >= 2:
                        pool.wait_ge(ssd, i - 1)
                    pool.tensor_tensor(sq[i % 2][:], R.bT[:, i, :], R.bT[:, i, :], ALU.mult).then_inc(sqd, 1)
                for i in range(TILES):
                    pool.wait_ge(tile_done, i + 1)
                    pool.tensor_tensor(R.bT[:, i, :], R.bT[:, i, :], ea[i % 2][:], ALU.mult).then_inc(af, 1)
                    pool.wait_ge(af, i + 1)
                    pool.tensor_tensor(R.bT[:, i, :], R.bT[:, i, :], en[i % 2][:].rearrange("p c t -> p (c t)"), ALU.mult).then_inc(b_made, 1)

            @block.vector
            def _(dve):
                step = Chain(dve, steps)
                for i in range(TILES + 1):
                    if i < TILES:
                        dve.tensor_scalar_mul(R.bT[:, i, :], R.k[:, i, :], R.vec[:, KK + i:KK + i + 1]).then_inc(kk1, 1)
                    if i >= 1:
                        m = i - 1
                        dve.wait_ge(rooted, m + 1)
                        nm = nrm[m % 2][:]
                        step(dve.tensor_scalar_max(nm, nm, 1e-12))
                        step(dve.reciprocal(nm, nm))
                        dve.wait_ge(sqd, m + 1)
                        dve.tensor_tensor(R.bT[:, m, :], R.bT[:, m, :], nm, ALU.mult).then_inc(norm, 1)
                dve.wait_ge(norm, TILES)
                dve.wait_ge(v_t, 2 * NT)
                dve.wait_ge(zeroed, 1)
                for i in range(TILES):
                    s = i % 2
                    dve.wait_ge(exps, 2 * i + 1)
                    step(dve.tensor_scalar_add(ew[s][:], ew[s][:], 1.0))
                    step(dve.reciprocal(ew[s][:], ew[s][:]))
                    for c in range(NT):
                        w = ew[s][:, c * P:(c + 1) * P]
                        step.inc(dve.tensor_tensor_scan(Sx[s][:, c, 1:P + 1], w, w, 0.0, ALU.add, ALU.bypass))
                    dve.wait_ge(steps, step.n)
                    middle, end = Sx[s][:, :, P // 2], Sx[s][:, :, P]
                    step.inc(dve.tensor_scalar_mul(mid[s][:, 0, :], middle, C0))
                    step.inc(dve.tensor_scalar_mul(mid[s][:, 1, :], middle, -C0))
                    step(dve.tensor_tensor(fa[s][:], end[:, 0:NT - 1], middle[:, 0:NT - 1], ALU.subtract))
                    dve.tensor_tensor(fa[s][:], fa[s][:], middle[:, 1:NT], ALU.add).then_inc(scanned, 1)
                    dve.wait_ge(exps, 2 * i + 2)
                    step(dve.tensor_scalar_add(ea[s][:], ea[s][:], 1.0))
                    step(dve.reciprocal(ea[s][:], ea[s][:]))
                    if i >= 2:
                        dve.wait_ge(bonus, i - 1)
                    step(dve.tensor_scalar(kf[s][:], ea[s][:], R.vec[:, KA + i:KA + i + 1], R.neg[:, 2 * TILES + i:2 * TILES + i + 1], ALU.mult, ALU.add))
                    step(dve.tensor_tensor(kf[s][:], kf[s][:], R.k[:, i, :], ALU.mult))
                    dve.scalar_tensor_tensor(rk[s][:], R.r[:, i, :], R.vec[:, RK + i:RK + i + 1], kf[s][:], ALU.mult, ALU.mult).then_inc(rkd, 1)
                    dve.wait_ge(decayed, i + 1)
                    r4, k4 = (x[:, i, :].rearrange("p (c t) -> p c t", c=NT) for x in (R.r, R.bT))
                    dve.tensor_tensor(AR[:, i, :, 1, :], r4, ep[s][:, :, 1:P + 1], ALU.mult)
                    dve.scalar_tensor_tensor(AR[:, i, :, 0, :], k4, -1.0, ep[s][:, :, 0:P], ALU.mult, ALU.mult)
                    dve.tensor_tensor(R.kT[:, i, :], kf[s][:], en[s][:].rearrange("p c t -> p (c t)"), ALU.mult).then_inc(tile_done, 1)
                dve.wait_ge(bonus, TILES)
                step(dve.tensor_copy(R.bonus[:], B[7][:, 0:NT * NH].rearrange("p (t h) -> p t h", t=NT)))


def rwkv_chunks(K, R, j, g2, mix):
    nc, B = K.nc, K.banks
    with Phase(nc) as scope:
        def sb(name, shape, dt=F32):
            return scope.enter_context(nc.sbuf_tensor(f"rck_{name}", shape, dt))

        def sem(name):
            return scope.sem(f"rck_{name}")
        XTf = K.XT[:].rearrange("p k t -> p (k t)")
        Tm = XTf[:, 0:NH * P].rearrange("p (h t) -> p h t", h=NH)
        Xm = XTf[:, NH * P:2 * NH * P].rearrange("p (h t) -> p h t", h=NH)
        U = XTf[:, 2 * NH * P:2 * NH * P + TOKW].rearrange("p (h i) -> p h i", h=NH)
        A = sb("A", [P, NH, 4 * P])
        QT = sb("QT", [P, NH, P])
        W = sb("W", [P, NH, P])
        Z = sb("Z", [P, NH, HD])
        S = R.S
        y = sb("y", [P, NH, HD])
        yq = sb("yq", [P, NH, HD])
        G = sb("G", [P, TOKW])
        lnx = sb("lnx", [P, 2, TOKW])
        st = sb("st", [P, 3, NH])
        m = Names()
        m.small = sem("small")
        m.tok_t = sem("tok_t")
        m.tok_k = sem("tok_k")
        m.a_made = sem("a_made")
        m.a_kept = sem("a_kept")
        m.q = sem("q")
        m.w0 = sem("w0")
        m.t0_t = sem("t0_t")
        m.t0_k = sem("t0_k")
        m.x_made = sem("x_made")
        m.x_kept = sem("x_kept")
        m.t_made = sem("t_made")
        m.w_made = sem("w_made")
        m.t_added = sem("t_added")
        m.w_added = sem("w_added")
        m.z_made = sem("z_made")
        m.z_kept = sem("z_kept")
        m.u_made = sem("u_made")
        m.u_kept = sem("u_kept")
        m.y_made = sem("y_made")
        m.y_kept = sem("y_kept")
        m.st_made = sem("st_made")
        m.s_sum = sem("s_sum")
        m.s_done = sem("s_done")
        m.g_made = sem("g_made")
        m.g_kept = sem("g_kept")
        m.gn = sem("gn")
        m.v_ready = sem("v_ready")
        m.root = sem("root")
        m.outs = sem("outs")
        ARv = R.AR.rearrange("p (i c) x -> p i c x", i=TILES)
        LAST = LEVELS - 1

        def heads(h):
            return h // 2, slice(64 * (h % 2), 64 * (h % 2) + 64)

        def slot(bank_even, h):
            return B[bank_even + h % 2][:, (h // 2) * HD:(h // 2 + 1) * HD]

        with nc.Block() as block:
            @block.sync
            def _(sp):
                for n, nm in enumerate(("rwkv_lnx_g", "rwkv_lnx_b")):
                    sp.dma_start(lnx[:, n, :], K.in_[nm][j:j + 1, :].broadcast_to([P, TOKW])).then_inc(m.small, 16)

            @block.tensor
            def _(pe):
                for c in range(NT):
                    tok = slice(c * P, (c + 1) * P)
                    if c:
                        pe.wait_ge(m.y_kept, c)
                        pe.wait_ge(m.s_sum, c)
                        pe.wait_ge(m.g_kept, c)
                    n = 0
                    for src in (R.bT, R.kT):
                        for i0, ni in ((0, 4), (4, 2)):
                            for i in range(ni):
                                last = pe.transpose(B[n][:, i * P:(i + 1) * P], src[:, i0 + i, tok], K.ident[:])
                            last.then_inc(m.tok_t, 1)
                            n += 1
                    for h in range(NH):
                        i, p = heads(h)
                        if h >= 4:
                            pe.wait_ge(m.a_kept, c * NH + h - 3)
                        bank = B[4 + h % 4]
                        pe.matmul(bank[:, 0:2 * P], R.bT[p, i, tok], ARv[p, i, c, :], start=True, stop=True)
                        pe.matmul(bank[:, 2 * P:4 * P], R.kT[p, i, tok], ARv[p, i, c, :], start=True, stop=True).then_inc(m.a_made, 1)
                    pe.wait_ge(m.tok_k, 4 * (c + 1))
                    for g in range(GROUPS):
                        pe.wait_ge(m.w0, c * GROUPS + g + 1)
                        for h in range(GH * g, GH * g + GH):
                            last = pe.transpose(B[g][:, (h % GH) * P:(h % GH + 1) * P], W[:, h, :], K.ident[:])
                        last.then_inc(m.t0_t, 1)
                    pe.wait_ge(m.a_kept, (c + 1) * NH)
                    for l in range(1, LEVELS):
                        nt, nx = c * GROUPS * (LEVELS - 2) + (l - 1) * GROUPS, c * GROUPS * (LEVELS - 1) + (l - 1) * GROUPS
                        for g in range(GROUPS):
                            pe.wait_ge(m.q, c * GROUPS * LEVELS + l * GROUPS + g + 1)
                            if l == 1:
                                pe.wait_ge(m.t0_k, c * GROUPS + g + 1)
                            else:
                                pe.wait_ge(m.t_added, nt - GROUPS + g + 1)
                            for h in range(GH * g, GH * g + GH):
                                last = pe.matmul(B[g][:, (h % GH) * P:(h % GH + 1) * P], QT[:, h, :], Tm[:, h, :], start=True, stop=True)
                            last.then_inc(m.x_made, 1)
                        for g in range(GROUPS):
                            pe.wait_ge(m.x_kept, nx + g + 1)
                            if l > 1:
                                pe.wait_ge(m.w_added, nx - GROUPS + g + 1)
                            if l < LAST:
                                for h in range(GH * g, GH * g + GH):
                                    last = pe.matmul(B[g][:, (h % GH) * P:(h % GH + 1) * P], W[:, h, :], Xm[:, h, :], start=True, stop=True)
                                last.then_inc(m.t_made, 1)
                            for h in range(GH * g, GH * g + GH):
                                last = pe.matmul(B[3 + g][:, (h % GH) * P:(h % GH + 1) * P], Xm[:, h, :], W[:, h, :], start=True, stop=True)
                            last.then_inc(m.w_made, 1)
                    if c:
                        pe.wait_ge(m.s_done, c)
                    for h in range(NH):
                        i, p = heads(h)
                        last = pe.matmul(slot(6, h), A[:, h, 2 * P:3 * P], R.V[:, c, h * HD:(h + 1) * HD], start=True, stop=(c == 0))
                        if c:
                            last = pe.matmul(slot(6, h), ARv[p, i, c, 0:P], S[p, i, :], start=False, stop=True)
                    last.then_inc(m.z_made, 1)
                    pe.wait_ge(m.z_kept, c + 1)
                    pe.wait_ge(m.w_added, (c + 1) * GROUPS * (LEVELS - 1))
                    for h in range(NH):
                        last = pe.matmul(slot(0, h), W[:, h, :], Z[:, h, :], start=True, stop=True)
                    last.then_inc(m.u_made, 1)
                    for half in range(2):
                        last = pe.matmul(B[5 + half][:, 0:TOKW // 2], R.gd[:, 0, tok], g2[:, half * (TOKW // 2):(half + 1) * (TOKW // 2)],
                                         start=True, stop=True)
                    last.then_inc(m.g_made, 1)
                    pe.wait_ge(m.u_kept, c + 1)
                    if c < NT - 1:
                        for h in range(NH):
                            i, p = heads(h)
                            o = B[4][p, i * HD:(i + 1) * HD]
                            pe.matmul(o, R.Bt[:, 0, h * HD:(h + 1) * HD], U[:, h, :], start=True, stop=False)
                            last = pe.matmul(o, R.Kt[:, 0, h * HD:(h + 1) * HD], R.V[:, c, h * HD:(h + 1) * HD], start=False, stop=True)
                        last.then_inc(m.st_made, 1)
                    for h in range(NH):
                        i, p = heads(h)
                        pe.matmul(slot(2, h), A[:, h, P:2 * P], U[:, h, :], start=True, stop=False)
                        last = pe.matmul(slot(2, h), A[:, h, 3 * P:4 * P], R.V[:, c, h * HD:(h + 1) * HD], start=False, stop=(c == 0))
                        if c:
                            last = pe.matmul(slot(2, h), ARv[p, i, c, P:2 * P], S[p, i, :], start=False, stop=True)
                    last.then_inc(m.y_made, 1)

            @block.gpsimd
            def _(pool):
                for c in range(NT):
                    for l in range(LEVELS):
                        for g in range(GROUPS):
                            hs = slice(GH * g, GH * g + GH)
                            if l == 0:
                                pool.wait_ge(m.a_kept, c * NH + GH * (g + 1))
                                if c:
                                    pool.wait_ge(m.u_made, c)
                            elif l == 1:
                                pool.wait_ge(m.w0, c * GROUPS + g + 1)
                            else:
                                pool.wait_ge(m.x_made, c * GROUPS * (LEVELS - 1) + (l - 2) * GROUPS + g + 1)
                            nq = c * GROUPS * LEVELS + l * GROUPS + g + 1
                            pool.tensor_tensor(QT[:, hs, :], A[:, hs, 0:P], K.level[:, l:l + 1, :].to_broadcast([P, GH, P]), ALU.mult).then_inc(m.q, 1)
                            if l == 0:
                                pool.wait_ge(m.q, nq)
                                pool.tensor_tensor(W[:, hs, :], QT[:, hs, :], K.ident[:].unsqueeze(1).to_broadcast([P, GH, P]), ALU.add).then_inc(m.w0, 1)

            @block.scalar
            def _(act):
                for c in range(NT):
                    n = 0
                    for dst in (R.Bt, R.Kt):
                        for i0, ni in ((0, 4), (4, 2)):
                            act.wait_ge(m.tok_t, 4 * c + n + 1)
                            act.activation(dst[:, 0, i0 * P:(i0 + ni) * P], B[n][:, 0:ni * P], ACT.Copy).then_inc(m.tok_k, 1)
                            n += 1
                    for g in range(GROUPS):
                        act.wait_ge(m.t0_t, c * GROUPS + g + 1)
                        act.activation(Tm[:, GH * g:GH * g + GH, :], B[g][:].rearrange("p (h t) -> p h t", h=GH), ACT.Copy).then_inc(m.t0_k, 1)
                    for l in range(1, LEVELS):
                        nx = c * GROUPS * (LEVELS - 1) + (l - 1) * GROUPS
                        for g in range(GROUPS):
                            act.wait_ge(m.x_made, nx + g + 1)
                            wait_from(act, m.w_made, nx - GROUPS + g + 1)
                            act.activation(Xm[:, GH * g:GH * g + GH, :], B[g][:].rearrange("p (h t) -> p h t", h=GH), ACT.Copy).then_inc(m.x_kept, 1)
                    act.wait_ge(m.z_made, c + 1)
                    for o in range(2):
                        last = act.activation(Z[:].rearrange("p (i o) d -> p i o d", o=2)[:, :, o, :],
                                              B[6 + o][:, 0:TILES * HD].rearrange("p (i d) -> p i d", i=TILES), ACT.Copy)
                    last.then_inc(m.z_kept, 1)
                    act.wait_ge(m.u_made, c + 1)
                    for o in range(2):
                        last = act.activation(U.rearrange("p (i o) d -> p i o d", o=2)[:, :, o, :],
                                              B[o][:, 0:TILES * HD].rearrange("p (i d) -> p i d", i=TILES), ACT.Copy)
                    last.then_inc(m.u_kept, 1)
                    act.wait_ge(m.g_made, c + 1)
                    wait_from(act, m.outs, c)
                    for o in range(2):
                        last = act.activation(G[:, o * (TOKW // 2):(o + 1) * (TOKW // 2)], B[5 + o][:, 0:TOKW // 2], ACT.Copy)
                    last.then_inc(m.g_kept, 1)
                    act.wait_ge(m.v_ready, c + 1)
                    act.activation(st[:, 1, :], st[:, 1, :], ACT.Sqrt).then_inc(m.root, 1)

            @block.vector
            def _(dve):
                step = Chain(dve, m.gn)

                def outputs(c):
                    b3 = [P, NH, HD]
                    step(dve.tensor_reduce(st[:, 0, :], y[:], AX.X, ALU.add))
                    step(dve.tensor_scalar_mul(st[:, 0, :], st[:, 0, :], 1.0 / HD))
                    step(dve.tensor_tensor(y[:], y[:], st[:, 0, :].unsqueeze(2).to_broadcast(b3), ALU.subtract))
                    step(dve.tensor_tensor(yq[:], y[:], y[:], ALU.mult))
                    step(dve.tensor_reduce(st[:, 1, :], yq[:], AX.X, ALU.add))
                    dve.tensor_scalar(st[:, 1, :], st[:, 1, :], 1.0 / HD, GN_EPS, ALU.mult, ALU.add).then_inc(m.v_ready, 1)
                    dve.wait_ge(m.root, c + 1)
                    step(dve.reciprocal(st[:, 2, :], st[:, 1, :]))
                    step(dve.tensor_tensor(y[:], y[:], st[:, 2, :].unsqueeze(2).to_broadcast(b3), ALU.mult))
                    dve.wait_ge(m.small, 32)
                    yf, qf = y[:].rearrange("p h d -> p (h d)"), yq[:].rearrange("p h d -> p (h d)")
                    step.inc(dve.tensor_tensor(yf, yf, lnx[:, 0, :], ALU.mult))
                    step(dve.tensor_tensor(yq[:], R.V[:, c, :].rearrange("p (h d) -> p h d", h=NH), R.bonus[:, c, :].unsqueeze(2).to_broadcast(b3), ALU.mult))
                    step(dve.tensor_tensor(yf, yf, lnx[:, 1, :], ALU.add))
                    step(dve.tensor_tensor(yf, yf, qf, ALU.add))
                    dve.wait_ge(m.g_kept, c + 1)
                    dve.tensor_tensor(mix[:, c, 0:TOKW], yf, G[:], ALU.mult).then_inc(m.outs, 1)

                for c in range(NT):
                    for h in range(NH):
                        dve.wait_ge(m.a_made, c * NH + h + 1)
                        dve.tensor_tensor(A[:, h, :], B[4 + h % 4][:], K.masks4[:], ALU.mult).then_inc(m.a_kept, 1)
                    for l in range(1, LEVELS):
                        nt, nx = c * GROUPS * (LEVELS - 2) + (l - 1) * GROUPS, c * GROUPS * (LEVELS - 1) + (l - 1) * GROUPS
                        for g in range(GROUPS):
                            hs = slice(GH * g, GH * g + GH)
                            if l < LAST:
                                dve.wait_ge(m.t_made, nt + g + 1)
                                wait_from(dve, m.t_added, nt - GROUPS + g + 1)
                                dve.tensor_tensor(Tm[:, hs, :], Tm[:, hs, :], B[g][:].rearrange("p (h t) -> p h t", h=GH), ALU.add).then_inc(m.t_added, 1)
                            dve.wait_ge(m.w_made, nx + g + 1)
                            wait_from(dve, m.w_added, nx - GROUPS + g + 1)
                            dve.tensor_tensor(W[:, hs, :], W[:, hs, :], B[3 + g][:].rearrange("p (h t) -> p h t", h=GH), ALU.add).then_inc(m.w_added, 1)
                    if c < NT - 1:
                        dve.wait_ge(m.st_made, c + 1)
                        stp = B[4][:, 0:TILES * HD].rearrange("p (i d) -> p i d", i=TILES)
                        dve.wait_ge(m.y_made, c + 1)
                        if c:
                            dve.wait_ge(m.s_done, c)
                            dve.tensor_tensor(S[:], S[:], stp, ALU.add).then_inc(m.s_sum, 1)
                        else:
                            dve.tensor_copy(S[:], stp).then_inc(m.s_sum, 1)
                        dve.wait_ge(m.s_sum, c + 1)
                        dve.tensor_tensor(S[:], S[:], R.f[:, :, c:c + 1].to_broadcast([P, TILES, HD]), ALU.mult).then_inc(m.s_done, 1)
                    dve.wait_ge(m.y_made, c + 1)
                    wait_from(dve, m.outs, c)
                    for o in range(2):
                        last = dve.tensor_copy(y[:].rearrange("p (i o) d -> p i o d", o=2)[:, :, o, :],
                                               B[2 + o][:, 0:TILES * HD].rearrange("p (i d) -> p i d", i=TILES))
                    last.then_inc(m.y_kept, 1)
                    dve.wait_ge(m.y_kept, c + 1)
                    outputs(c)


def shared_state(nc, scope, ins):
    def sb(name, shape, dt=F32):
        return scope.enter_context(nc.sbuf_tensor(name, shape, dt))

    def sem(name):
        return scope.enter_context(nc.semaphore(name))

    K = Names()
    K.nc, K.in_ = nc, ins
    K.banks = [scope.enter_context(nc.psum_tensor(f"bank{i}", [P, 512], F32)) for i in range(8)]
    K.X = sb("X", [P, NT, D])
    K.XT = sb("XT", [P, KD, T])
    K.Xk = K.X[:].rearrange("p t (q k) -> p t k q", k=KD)
    K.W = sb("W", [P, 2, 2, 3, KD * FE])
    K.arena = K.W[:].rearrange("p a b c d -> p (a b c d)")
    K.k_memT = sb("k_memT", [HD, NMH, NMEM])
    K.v_mem = sb("v_mem", [P, NMEM // P, MEMW])
    K.x_rows = nc.dram_tensor("x_rows", [T, D], F32).ap()
    K.y_rows = nc.dram_tensor("y_rows", [TOPK * T, D], F32).ap()
    K.w_gu = [sem("w_gu0"), sem("w_gu1")]
    K.w_dn = [sem("w_dn0"), sem("w_dn1")]
    K.sh_added, K.x_loaded, K.out_stored = sem("sh_added"), sem("x_loaded"), sem("out_stored")
    return K


def decoder_trunk(nc, ins, out):
    with ExitStack() as scope:
        K = shared_state(nc, scope, ins)
        constants(K, scope)
        memory_keys(K)
        for L in range(DEPTH):
            if L % 2 == 0:
                fox_layer(K, L, L // 2)
            else:
                rwkv_layer(K, L, L // 2)
            K.w_gu_base, K.w_dn_base = L * 16 * PAIRS, L * 8 * PAIRS
            routed_experts_tables(K, L)
            expert_loop(K, L)
            combine(K, L)
        with nc.Block() as block:
            @block.sync
            def _(sp):
                sp.dma_start(out[0].rearrange("(t p) d -> p t d", p=P), K.X[:]).then_inc(K.out_stored, 16)
                sp.wait_ge(K.out_stored, 16)


_INS = ["x", "mem", "mem_ln_g", "mem_ln_b", "w_mem_kv", "fox_w_in", "fox_b_f", "rwkv_w_in", "rwkv_mu", "rwkv_w0",
        "rwkv_w2", "rwkv_a0", "rwkv_a2", "rwkv_g2", "rwkv_k_k", "rwkv_k_a", "rwkv_r_k", "rwkv_lnx_g", "rwkv_lnx_b",
        "w_out", "ln1_g", "ln1_b", "w_router", "router_bias", "w_exp_gate", "w_exp_up", "w_exp_down",
        "w_sh_gate", "w_sh_up", "w_sh_down", "ln2_g", "ln2_b"]


def kernel(**inputs):
    import numpy as _np
    import concourse.bacc as _bacc
    from concourse import mybir as _mybir
    from concourse.bass_utils import run_bass_kernel_spmd as _run

    nc = _bacc.Bacc("TRN2", target_bir_lowering=False, num_devices=1)
    arrays, aps = {}, {}
    for name in _INS:
        a = _np.ascontiguousarray(inputs[name])
        arrays[f"in_{name}_dram"] = a
        aps[name] = nc.dram_tensor(f"in_{name}_dram", a.shape, _mybir.dt.from_np(a.dtype), kind="ExternalInput").ap()
    out = nc.dram_tensor("out_dram", (1, T, D), F32, kind="ExternalOutput").ap()
    decoder_trunk(nc, aps, out)
    r = _run(nc, [arrays], core_ids=[0])
    return r.results[0]["out_dram"]
```

```python
from contextlib import ExitStack

import numpy as np

import concourse.bass as bass
from concourse import mybir

F32, BF16, I32, U32 = mybir.dt.float32, mybir.dt.bfloat16, mybir.dt.int32, mybir.dt.uint32
ALU, ACT, AX = mybir.AluOpType, mybir.ActivationFunctionType, mybir.AxisListType

P = 128
D = 1024
T = 512
NT = T // P
KD = D // P
DEPTH = 2
HD = 64
NH = 12
NMH = 4
TOKW = NH * HD
MEMW = NMH * HD
NMEM = 256
E = 64
TOPK = 6
FE = 256
SLOTS = 64
PAIRS = E // 2
EXTRA = T // SLOTS - 1
MAX_PASSES = PAIRS + T * TOPK // SLOTS
NOBODY = 4096
PASS_STEPS = 2
BY_VECTOR = 3
ROUTED_SCALE = 2.5
ALPHA = (2 * DEPTH) ** 0.25
LN_EPS = 1e-5
GN_EPS = 64e-5


class Names:
    pass


class Chain:

    def __init__(self, eng, sem, start=0):
        self.eng, self.sem, self.n = eng, sem, start

    def inc(self, ins):
        ins.then_inc(self.sem, 1)
        self.n = self.n + 1
        return ins

    def __call__(self, ins):
        self.inc(ins)
        self.eng.wait_ge(self.sem, self.n)


class Phase(ExitStack):

    def __init__(self, nc):
        super().__init__()
        self.nc, self.sems = nc, []

    def sem(self, name):
        self.sems.append(self.nc.alloc_semaphore(name=name))
        return self.sems[-1]

    def __exit__(self, *what):
        if what[0] is None:
            self.nc.clear_and_free_semaphores(self.sems)
            self.nc.all_engine_barrier()
        return super().__exit__(*what)


def wait_from(eng, sem, value):
    if not (isinstance(value, int) and value <= 0):
        eng.wait_ge(sem, value)


def constants(K, scope):
    nc = K.nc

    def sb(name, shape, dt=F32):
        return scope.enter_context(nc.sbuf_tensor(name, shape, dt))

    K.ident = sb("ident", [P, P])
    K.before = sb("before", [P, P], BF16)
    K.ident16 = sb("ident16", [P, P], BF16)
    K.causal = sb("causal", [P, P], BF16)
    K.upto = sb("upto_f32", [P, P])
    K.ones = sb("ones_f32", [P, P])
    K.heads = sb("heads", [P, P])
    K.masks4 = sb("masks4", [P, 4 * P], BF16)
    K.level = sb("level", [P, 7, P], BF16)
    K.ones16 = sb("ones16", [P, P], BF16)
    K.iota_e = sb("iota_e", [P, E])
    K.iota_s = sb("iota_s", [P, T])
    K.iota_j = sb("iota_j", [P, TOPK])
    K.levels = sb("levels", [P, EXTRA])
    K.place = sb("place", [P, NT, E])
    K.slot_cols = sb("slot_cols", [P, NT, PAIRS, 4], BF16)
    K.rank = sb("rank", [P, NT, E])
    K.gates = sb("gates", [P, NT, TOPK])
    K.plan_pair = sb("plan_pair", [1, MAX_PASSES + 4], I32)
    K.plan_level = sb("plan_level", [1, MAX_PASSES + 4], I32)
    K.plan_slot = sb("plan_slot", [1, MAX_PASSES + 4], I32)
    K.plan_end = sb("plan_end", [1, PAIRS], I32)
    K.plan_turns = sb("plan_turns", [1, 1], I32)
    scratch = sb("iota_scratch", [P, T], I32)
    K.constants_made = scope.enter_context(nc.semaphore("constants_made"))

    def make(pool):
        step = Chain(pool, K.constants_made)
        step.inc(pool.memset(K.ident[:], 0.0))
        step.inc(pool.memset(K.before[:], 1.0))
        step.inc(pool.memset(K.ones16[:], 1.0))
        step.inc(pool.memset(K.ident16[:], 0.0))
        step.inc(pool.memset(K.causal[:], 0.0))
        step.inc(pool.memset(K.upto[:], 1.0))
        step.inc(pool.memset(K.ones[:], 1.0))
        step.inc(pool.memset(K.rank[:], -1.0))
        step(pool.memset(K.slot_cols[:], 0.0))
        step.inc(pool.affine_select(out=K.ident[:], in_=K.ident[:], compare_op=ALU.not_equal, fill=1.0, base=0,
                                    pattern=[[-1, P]], channel_multiplier=1))
        K.ident_made = step.n
        step.inc(pool.affine_select(out=K.ident16[:], in_=K.ident16[:], compare_op=ALU.not_equal, fill=1.0, base=0,
                                    pattern=[[-1, P]], channel_multiplier=1))
        step.inc(pool.affine_select(out=K.causal[:], in_=K.causal[:], compare_op=ALU.is_ge, fill=-1e30, base=0,
                                    pattern=[[-1, P]], channel_multiplier=1))
        step.inc(pool.affine_select(out=K.upto[:], in_=K.upto[:], compare_op=ALU.is_ge, fill=0.0, base=0,
                                    pattern=[[1, P]], channel_multiplier=-1))
        step.inc(pool.affine_select(out=K.before[:], in_=K.before[:], compare_op=ALU.is_ge, fill=0.0, base=-1,
                                    pattern=[[1, P]], channel_multiplier=-1))
        for dst, pattern, base, mult in (
                (K.iota_s[:], [[1, T]], 0, 0), (K.iota_e[:], [[1, E]], 0, 0), (K.iota_j[:], [[T, TOPK]], 0, 0),
                (K.levels[:], [[SLOTS, EXTRA]], SLOTS, 0)):
            n = dst.shape[1]
            step(pool.iota(scratch[:, 0:n], pattern=pattern, base=base, channel_multiplier=mult))
            step(pool.tensor_copy(dst, scratch[:, 0:n]))
        n = PAIRS
        step(pool.iota(scratch[:, 0:n], pattern=[[0, n]], base=0, channel_multiplier=1))
        step(pool.memset(K.level[:, 6, :], 1.0))
        for lv in range(5, -1, -1):
            nb, w = P // (2 << lv), 2 << lv
            same = K.level[:, lv, :].rearrange("p (b w) -> p b w", w=w)
            step(pool.memset(K.level[:, lv, :], 1.0))
            step(pool.affine_select(out=same, in_=same, compare_op=ALU.is_ge, fill=0.0, base=0, pattern=[[-w, nb], [0, w]], channel_multiplier=1))
            step(pool.affine_select(out=same, in_=same, compare_op=ALU.is_ge, fill=0.0, base=w - 1, pattern=[[w, nb], [0, w]], channel_multiplier=-1))
        step(pool.tensor_copy(K.heads[:], K.level[:, 5, :]))
        for lv in range(6, -1, -1):
            below = K.level[:, lv - 1, :] if lv else K.ident[:]
            step(pool.tensor_tensor(K.level[:, lv, :], K.level[:, lv, :], below, ALU.subtract))
            step(pool.tensor_tensor(K.level[:, lv, :], K.level[:, lv, :], K.upto[:], ALU.mult))
        for q in range(4):
            step(pool.tensor_copy(K.masks4[:, q * P:(q + 1) * P], (K.upto if q % 2 else K.before)[:]))
        for t in range(NT):
            step(pool.tensor_copy(K.slot_cols[:, t, :, 0], scratch[:, 0:n]))
            step(pool.memset(K.slot_cols[:, t, :, 1], float(P * t - NOBODY)))

    return make


def routed_experts_tables(K, L):
    nc, X, XT, ident = K.nc, K.X, K.XT, K.ident
    B = K.banks
    with Phase(nc) as scope:
        def sb(name, shape, dt=F32):
            return scope.enter_context(nc.sbuf_tensor(f"{name}{L}", shape, dt))

        def sem(name):
            return scope.sem(f"route{L}_{name}")

        w_router = sb("w_router", [P, KD, E])
        bias = sb("router_bias", [P, 1, E])
        w_sh = sb("w_sh", [P, 2, KD * FE])
        w_shd = sb("w_shd", [P, 2, D])
        negexp = sb("negexp", [P, NT, E])
        score = sb("score", [P, NT, E])
        choose = sb("choose", [P, NT, E])
        top = sb("top", [P, NT, 8])
        top_at = sb("top_at", [P, NT, 8], U32)
        top_f = sb("top_f", [P, NT, 8])
        hot = sb("hot", [P, NT * TOPK, E])
        hot_w = sb("hot_w", [P, NT * TOPK, E])
        mask = sb("mask", [P, NT, E])
        mask16 = sb("mask16", [P, NT, E], BF16)
        gsum = sb("gsum", [P, NT, 1])
        most = sb("most", [P, PAIRS, 1])
        over = sb("over", [P, PAIRS, EXTRA])
        n_extra = sb("n_extra", [P, PAIRS])
        ended = sb("ended", [P, PAIRS - 1])
        evens = sb("evens", [P, 1])
        plan = sb("plan", [P, 3])
        end = sb("end", [P, PAIRS])
        turn = sb("turn", [P, MAX_PASSES // 2])
        sh_e = sb("sh_e", [P, 2, T])
        sh_h = sb("sh_h", [P, 2, T])

        loaded = sem("loaded")
        loaded_sh = sem("loaded_sh")
        stored = sem("stored")
        turned = sem("turned")
        xt_a, xt_d = sem("xt_a"), sem("xt_d")
        logits = sem("logits")
        negexp_done = sem("negexp")
        mask_done = sem("mask")
        ranked = sem("ranked")
        sh_gu = sem("sh_gu")
        planned, plan_turned = sem("planned"), sem("plan_turned")
        sh_exp = sem("sh_exp")
        sh_hidden = sem("sh_hidden")
        sh_out = sem("sh_out")
        steps = sem("steps")

        with nc.Block() as block:
            @block.sync
            def _(sp):
                sp.dma_start(w_router[:], K.in_["w_router"][L].rearrange("(p k) e -> p k e", k=KD)).then_inc(loaded, 16)
                sp.dma_start(bias[:, 0, :], K.in_["router_bias"][L:L + 1, :].broadcast_to([P, E])).then_inc(loaded, 16)
                sp.dma_start(w_sh[:, 0, :], K.in_["w_sh_gate"][L].rearrange("(p k) f -> p (k f)", k=KD)).then_inc(loaded_sh, 16)
                sp.dma_start(w_sh[:, 1, :], K.in_["w_sh_up"][L].rearrange("(p k) f -> p (k f)", k=KD)).then_inc(loaded_sh, 16)
                sp.dma_start(w_shd[:], K.in_["w_sh_down"][L].rearrange("(j p) d -> p j d", p=P)).then_inc(loaded_sh, 16)
                sp.dma_start(K.x_rows.rearrange("(t p) d -> p t d", p=P), X[:]).then_inc(stored, 16)
                for i in range(2):
                    load_pair(K, sp, L, i, i)
                sp.wait_ge(stored, 16)

            @block.tensor
            def _(pe):
                for k in range(KD):
                    if k >= 4:
                        pe.wait_ge(xt_a if k % 2 == 0 else xt_d, (k - 4) // 2 + 1)
                    for t in range(NT):
                        last = pe.transpose(B[k % 4][:, t * P:(t + 1) * P], K.Xk[:, t, k, :], ident[:])
                    last.then_inc(turned, 1)
                pe.wait_ge(loaded, 32)
                pe.wait_ge(xt_a, KD // 2)
                pe.wait_ge(xt_d, KD // 2)
                for t in range(NT):
                    for k in range(KD):
                        last = pe.matmul(B[4][:, t * E:(t + 1) * E], XT[:, k, t * P:(t + 1) * P], w_router[:, k, :],
                                         start=(k == 0), stop=(k == KD - 1))
                last.then_inc(logits, 1)
                pe.wait_ge(loaded_sh, 48)
                def shared_products(gu):
                    for j in range(2):
                        for k in range(KD):
                            last = pe.matmul(B[gu * 2 + j][:], w_sh[:, gu, k * FE + j * P:k * FE + (j + 1) * P],
                                             XT[:, k, :], start=(k == 0), stop=(k == KD - 1))
                        last.then_inc(sh_gu, 1)

                shared_products(0)
                pe.wait_ge(mask_done, 1)
                for t in range(NT):
                    for t0 in range(t + 1):
                        last = pe.matmul(B[5][:, t * E:(t + 1) * E], (K.before if t0 == t else K.ones16)[:],
                                         mask16[:, t0, :], start=(t0 == 0), stop=(t0 == t))
                for t in range(NT):
                    last = pe.matmul(B[5][:, NT * E:(NT + 1) * E], K.ones16[:], mask16[:, t, :],
                                     start=(t == 0), stop=(t == NT - 1))
                last.then_inc(ranked, 1)
                shared_products(1)
                pe.wait_ge(planned, 1)
                for q in range(3):
                    last = pe.matmul(B[4][0:1, q * P:(q + 1) * P], plan[:, q:q + 1], ident[:], start=True, stop=True)
                last.then_inc(plan_turned, 1)
                pe.wait_ge(sh_hidden, 2)
                for t in range(NT):
                    for n in range(2):
                        i = t * 2 + n
                        if i >= 2:
                            pe.wait_ge(K.sh_added, L * 8 + i - 1)
                        for j in range(2):
                            last = pe.matmul(B[6 + n][:], sh_h[:, j, t * P:(t + 1) * P], w_shd[:, j, n * 512:(n + 1) * 512],
                                             start=(j == 0), stop=(j == 1))
                        last.then_inc(sh_out, 1)

            @block.scalar
            def _(act):
                for k in range(0, KD, 2):
                    act.wait_ge(turned, k + 1)
                    act.activation(XT[:, k, :], B[k % 4][:], ACT.Copy).then_inc(xt_a, 1)
                act.wait_ge(logits, 1)
                act.activation(negexp[:], B[4][:, 0:NT * E].rearrange("p (t e) -> p t e", t=NT), ACT.Exp, scale=-1.0).then_inc(negexp_done, 1)
                for j in range(2):
                    act.wait_ge(sh_gu, j + 1)
                    act.activation(sh_e[:, j, :], B[j][:], ACT.Sigmoid).then_inc(sh_exp, 1)

            @block.vector
            def _(dve):
                step = Chain(dve, steps)
                for k in range(1, KD, 2):
                    dve.wait_ge(turned, k + 1)
                    dve.tensor_copy(XT[:, k, :], B[k % 4][:]).then_inc(xt_d, 1)
                dve.wait_ge(loaded, 32)
                dve.wait_ge(negexp_done, 1)
                step(dve.tensor_scalar_add(negexp[:], negexp[:], 1.0))
                step(dve.reciprocal(score[:], negexp[:]))
                step(dve.tensor_tensor(choose[:], score[:], bias[:].to_broadcast([P, NT, E]), ALU.add))
                for t in range(NT):
                    step(dve.max(top[:, t, :], choose[:, t, :]))
                    last = dve.max_index(top_at[:, t, :], top[:, t, :], choose[:, t, :])
                    step.inc(last)
                dve.wait_ge(steps, step.n)
                step(dve.tensor_copy(top_f[:], top_at[:]))
                hot4 = hot[:].rearrange("p (t j) e -> p t j e", t=NT)
                hotw4 = hot_w[:].rearrange("p (t j) e -> p t j e", t=NT)
                for t in range(NT):
                    step.inc(dve.tensor_tensor(hot4[:, t], top_f[:, t, 0:TOPK].unsqueeze(2).to_broadcast([P, TOPK, E]),
                                               K.iota_e[:].unsqueeze(1).to_broadcast([P, TOPK, E]), ALU.is_equal))
                dve.wait_ge(steps, step.n)
                step(dve.tensor_reduce(mask[:], hot4.rearrange("p t j e -> p t e j"), AX.X, ALU.add))
                dve.tensor_copy(mask16[:], mask[:]).then_inc(mask_done, 1)
                for t in range(NT):
                    step.inc(dve.tensor_tensor(hotw4[:, t], hot4[:, t], K.iota_j[:].unsqueeze(2).to_broadcast([P, TOPK, E]), ALU.mult))
                dve.wait_ge(steps, step.n)
                with nc.allow_low_precision(reason="multiples of 512 up to 2560 are exact in bfloat16"):
                    step(dve.tensor_reduce(K.place[:], hotw4.rearrange("p t j e -> p t e j"), AX.X, ALU.add))
                for t in range(NT):
                    step.inc(dve.tensor_copy(K.slot_cols[:, t, 0:PAIRS, 2:4], K.place[:, t, :].rearrange("p (i a) -> p i a", a=2)))
                for t in range(NT):
                    step.inc(dve.tensor_tensor(hotw4[:, t], hot4[:, t], score[:, t, :].unsqueeze(1).to_broadcast([P, TOPK, E]), ALU.mult))
                dve.wait_ge(steps, step.n)
                step(dve.tensor_reduce(K.gates[:], hotw4, AX.X, ALU.add))
                step(dve.tensor_reduce(gsum[:, :, 0], K.gates[:], AX.X, ALU.add))
                step(dve.reciprocal(gsum[:], gsum[:]))
                step(dve.tensor_scalar_mul(gsum[:], gsum[:], ROUTED_SCALE))
                step(dve.tensor_tensor(K.gates[:], K.gates[:], gsum[:].to_broadcast([P, NT, TOPK]), ALU.mult))
                dve.wait_ge(ranked, 1)
                for t in range(NT):
                    step.inc(dve.scalar_tensor_tensor(K.rank[:, t, 0:E], B[5][:, t * E:(t + 1) * E], 1.0, mask[:, t, :], ALU.add, ALU.mult))
                dve.wait_ge(steps, step.n)
                step(dve.tensor_scalar_add(K.rank[:, :, 0:E], K.rank[:, :, 0:E], -1.0))
                cnt = B[5][:, NT * E:(NT + 1) * E].rearrange("p (i a) -> p i a", a=2)
                step(dve.tensor_reduce(most[:, :, 0], cnt, AX.X, ALU.max))
                step(dve.tensor_tensor(over[:], most[:].to_broadcast([P, PAIRS, EXTRA]), K.levels[:].unsqueeze(1).to_broadcast([P, PAIRS, EXTRA]), ALU.is_gt))
                step(dve.tensor_reduce(n_extra[:], over[:], AX.X, ALU.add))
                step(dve.tensor_scalar_add(n_extra[:], n_extra[:], 1.0))
                step(dve.tensor_tensor_scan(end[:], n_extra[:], n_extra[:], 0.0, ALU.add, ALU.bypass))
                step.inc(dve.tensor_copy(K.plan_end[:], end[0:1, :]))
                step(dve.tensor_scalar(turn[:], K.iota_s[:, 0:MAX_PASSES].rearrange("p (k u) -> p k u", u=2)[:, :, 0],
                                       end[:, PAIRS - 1:PAIRS], None, ALU.is_lt))
                step(dve.tensor_reduce(gsum[:, 0, :], turn[:], AX.X, ALU.add))
                step.inc(dve.tensor_copy(K.plan_turns[:], gsum[0:1, 0, :]))
                number = K.slot_cols[:, 0, 0, 0:1]
                step(dve.tensor_tensor(ended[:], end[:, 0:PAIRS - 1], number.to_broadcast([P, PAIRS - 1]), ALU.is_le))
                step(dve.tensor_reduce(plan[:, 0:1], ended[:], AX.X, ALU.add))
                step(dve.tensor_reduce(evens[:], ended[:, 0:PAIRS - 1:2], AX.X, ALU.add))
                step(dve.scalar_tensor_tensor(plan[:, 1:2], evens[:], 2.0, plan[:, 0:1], ALU.mult, ALU.subtract))
                step(dve.tensor_tensor(ended[:], ended[:], end[:, 0:PAIRS - 1], ALU.mult))
                step(dve.tensor_reduce(plan[:, 2:3], ended[:], AX.X, ALU.max))
                step(dve.tensor_tensor(plan[:, 2:3], number, plan[:, 2:3], ALU.subtract))
                dve.tensor_scalar_min(plan[:, 2:3], plan[:, 2:3], float(EXTRA)).then_inc(planned, 1)
                for j in range(2):
                    dve.wait_ge(sh_exp, j + 1)
                    step(dve.tensor_tensor(sh_e[:, j, :], sh_e[:, j, :], B[j][:], ALU.mult))
                    dve.wait_ge(sh_gu, 3 + j)
                    dve.tensor_tensor(sh_h[:, j, :], sh_e[:, j, :], B[2 + j][:], ALU.mult).then_inc(sh_hidden, 1)
                dve.wait_ge(plan_turned, 1)
                for q, table in enumerate((K.plan_pair, K.plan_slot, K.plan_level)):
                    step.inc(dve.tensor_copy(table[:], B[4][0:1, q * P:q * P + MAX_PASSES + 4]))
                dve.wait_ge(stored, 16)
                for t in range(NT):
                    for n in range(2):
                        dve.wait_ge(sh_out, t * 2 + n + 1)
                        xs = X[:, t, n * 512:(n + 1) * 512]
                        dve.scalar_tensor_tensor(xs, xs, ALPHA, B[6 + n][:], ALU.mult, ALU.add).then_inc(K.sh_added, 1)


def load_pair(K, sp, L, i, slot, which=(0, 1, 2)):
    for m in which:
        name = ("w_exp_gate", "w_exp_up", "w_exp_down")[m]
        src = K.in_[name].rearrange("l e r c -> (l e) r c")[bass.ds(L * E + i * 2, 2)]
        src = src.rearrange("e (p k) f -> p e (k f)", p=P)
        sp.dma_start(K.W[:, slot, :, m, :], src).then_inc(K.w_gu[slot] if m < 2 else K.w_dn[slot], 16)


def expert_loop(K, L):
    nc, B, ident = K.nc, K.banks, K.ident
    with Phase(nc) as scope:
        def sb(name, shape, dt=F32):
            return scope.enter_context(nc.sbuf_tensor(f"{name}{L}", shape, dt))

        def sem(name):
            return scope.sem(f"experts{L}_{name}")

        xt_room = K.XT[:].rearrange("p k t -> p (k t)")
        onehot = [sb(f"onehot{s}", [P, NT, 2, SLOTS], BF16) for s in range(2)]
        tok_f = [sb(f"tok_f{s}", [P, 1]) for s in range(2)]
        tok = [sb(f"tok{s}", [P, 1], I32) for s in range(2)]
        ahead = [sb(f"ahead{s}", [P, 3], I32) for s in range(2)]
        row = [sb(f"row{s}", [P, 1], I32) for s in range(2)]
        xg = [xt_room[:, s * D:(s + 1) * D] for s in range(2)]
        xt = [sb(f"xt{s}", [P, KD, P]) for s in range(2)]
        y = [sb(f"y{s}", [P, D]) for s in range(2)]
        sig, gu, h = sb("sig", [P, FE]), sb("gu", [P, FE]), sb("h", [P, FE])
        ht = sb("ht", [P, 2, P])
        slots = B[4][:, 0:4]
        gate, up = B[2][:, 0:FE], B[7][:, 0:FE]

        cleared = sem("cleared")
        onehot_made, slots_made, index_made = sem("onehot_made"), sem("slots_made"), sem("index_made")
        gathered = [sem("gathered0"), sem("gathered1")]
        x_turned, xt_a, xt_d = sem("x_turned"), sem("xt_a"), sem("xt_d")
        gate_done, gate_up_done, sigmoid_done, hidden_done = sem("gate_done"), sem("gate_up_done"), sem("sigmoid_done"), sem("hidden_done")
        h_turned, ht_kept, down_done = sem("h_turned"), sem("ht_kept"), sem("down_done")
        y_a, y_d = sem("y_a"), sem("y_d")
        stored = [sem("stored0"), sem("stored1")]
        steps = sem("steps")

        def entry(eng, table, n, most):
            return eng.value_load(table[0:1, bass.ds(n, 1)] if not isinstance(n, int) else table[0:1, n:n + 1],
                                  min_val=0, max_val=most)

        def through(n, s):
            return 8 * (n - s) + 16

        def held(eng, value):
            return value if isinstance(value, int) else eng.to_reg(value)

        def loop(eng, body):
            for u in range(2):
                body(u, u)
            turns = eng.value_load(K.plan_turns[0:1, 0:1], min_val=PAIRS // 2, max_val=MAX_PASSES // 2)
            with eng.Fori(1, turns) as turn:
                for u in range(2):
                    body(turn * 2 + u, u)

        def one_hot(dve, s, n):
            pair, level = entry(dve, K.plan_pair, n, PAIRS - 1), entry(dve, K.plan_level, n, EXTRA)
            for t in range(NT):
                last = dve.tensor_tensor(
                    onehot[s][:, t], K.rank[:, t, bass.ds(pair * 2, 2)].unsqueeze(2).to_broadcast([P, 2, SLOTS]),
                    K.iota_s[:, bass.ds(level * SLOTS, SLOTS)].unsqueeze(1).to_broadcast([P, 2, SLOTS]), ALU.is_equal)
            last.then_inc(onehot_made, 1)

        def slot_rows(pe, s, n):
            pair = entry(pe, K.plan_pair, n, PAIRS - 1)
            wait_from(pe, index_made, n)
            pe.wait_ge(onehot_made, n + 1)
            for t in range(NT):
                last = pe.matmul(slots, onehot[s][:, t].rearrange("p a s -> p (a s)"),
                                 K.slot_cols[:, t, bass.ds(pair, 1), :].rearrange("p i c -> p (i c)"),
                                 start=(t == 0), stop=(t == NT - 1))
            last.then_inc(slots_made, 1)

        def index_rows(dve, s, dst, n, step):
            dve.wait_ge(slots_made, n + 1)
            wait_from(dve, gathered[s], through(n - 2, s))
            step(dve.tensor_scalar(tok_f[s][:], slots[:, 0:1], float(NOBODY), slots[:, 1:2], ALU.add, ALU.add))
            dve.tensor_copy(tok[s][:], tok_f[s][:])
            for a in range(2):
                half = slice(64 * a, 64 * a + 64)
                last = dve.tensor_tensor(dst[half, :], slots[half, 2 + a:3 + a], tok_f[s][half, :], ALU.add)
            last.then_inc(index_made, 1)

        def gather(pool, s, n):
            value = held(pool, n + 1)
            pool.wait_ge(cleared, 1)
            pool.wait_ge(index_made, value)
            pool.indirect_dma_start(out=xg[s], out_offset=None, in_=K.x_rows,
                                    in_offset=bass.IndirectOffsetOnAxis(ap=tok[s][:], axis=0),
                                    bounds_check=T - 1, oob_is_err=False).then_inc(gathered[s], 16)

        def turn_x(pe, s, n):
            pe.wait_ge(gathered[s], through(n, s))
            xk = xg[s].rearrange("p (q k) -> p k q", k=KD)
            for k in range(KD):
                ins = pe.transpose(B[k // 4][:, (k % 4) * P:(k % 4 + 1) * P], xk[:, k, :], ident[:])
                if k % 4 == 3:
                    ins.then_inc(x_turned, 1)

        def keep_xt(eng, s, n, half):
            eng.wait_ge(x_turned, 2 * n + 1 + half)
            dst = xt[s][:, 4 * half:4 * half + 4, :].rearrange("p k t -> p (k t)")
            if half == 0:
                eng.activation(dst, B[0][:], ACT.Copy).then_inc(xt_a, 1)
            else:
                eng.tensor_copy(dst, B[1][:]).then_inc(xt_d, 1)

        def gate_up(pe, s, n, pair, w):
            pe.wait_ge(K.w_gu[w], pair * 16 + (K.w_gu_base + 32 - 16 * w))
            pe.wait_ge(xt_a, n + 1)
            pe.wait_ge(xt_d, n + 1)
            wait_from(pe, hidden_done, n)
            for m, done in ((0, gate_done), (1, gate_up_done)):
                for k in range(KD):
                    for a in range(2):
                        last = pe.matmul((gate, up)[m][64 * a:64 * a + 64, :], xt[s][:, k, 64 * a:64 * a + 64],
                                         K.W[:, w, a, m, k * FE:(k + 1) * FE], start=(k == 0), stop=(k == KD - 1))
                last.then_inc(done, 1)

        def sigmoid(act, n):
            wait_from(act, hidden_done, n)
            act.wait_ge(gate_done, n + 1)
            act.activation(sig[:], gate, ACT.Sigmoid).then_inc(sigmoid_done, 1)

        def hidden(dve, n, step):
            dve.wait_ge(sigmoid_done, n + 1)
            step(dve.tensor_tensor(gu[:], sig[:], gate, ALU.mult))
            dve.wait_ge(gate_up_done, n + 1)
            dve.tensor_tensor(h[:], gu[:], up, ALU.mult).then_inc(hidden_done, 1)

        def turn_h(pe, n):
            pe.wait_ge(hidden_done, n + 1)
            hk = h[:].rearrange("p (q j) -> p j q", j=2)
            for j in range(2):
                last = pe.transpose(B[3][:, j * P:(j + 1) * P], hk[:, j, :], ident[:])
            last.then_inc(h_turned, 1)

        def keep_ht(dve, n):
            dve.wait_ge(h_turned, n + 1)
            dve.tensor_copy(ht[:].rearrange("p j t -> p (j t)"), B[3][:, 0:2 * P]).then_inc(ht_kept, 1)

        def down(pe, n, pair, w):
            pe.wait_ge(K.w_dn[w], pair * 8 + (K.w_dn_base + 16 - 8 * w))
            pe.wait_ge(ht_kept, n + 1)
            wait_from(pe, y_a, n)
            wait_from(pe, y_d, n)
            for half in range(2):
                for j in range(2):
                    for a in range(2):
                        at = j * D + half * 512
                        last = pe.matmul(B[5 + half][64 * a:64 * a + 64, :], ht[:, j, 64 * a:64 * a + 64],
                                         K.W[:, w, a, 2, at:at + 512], start=(j == 0), stop=(j == 1))
                last.then_inc(down_done, 1)

        def keep_y(eng, s, n, half):
            wait_from(eng, stored[s], through(n - 2, s))
            eng.wait_ge(down_done, 2 * n + 1 + half)
            dst = y[s][:, half * 512:half * 512 + 512]
            if half == 0:
                eng.activation(dst, B[5][:], ACT.Copy).then_inc(y_a, 1)
            else:
                eng.tensor_copy(dst, B[6][:]).then_inc(y_d, 1)

        def scatter(pool, s, n):
            value = held(pool, n + 1)
            pool.wait_ge(cleared, 1)
            pool.wait_ge(y_a, value)
            pool.wait_ge(y_d, value)
            pool.indirect_dma_start(out=K.y_rows, out_offset=bass.IndirectOffsetOnAxis(ap=row[s][:], axis=0),
                                    in_=y[s][:], in_offset=None,
                                    bounds_check=TOPK * T - 1, oob_is_err=False).then_inc(stored[s], 16)

        with nc.Block() as block:
            @block.sync
            def _(sp):
                def refill(i, slot):
                    passes = sp.value_load(K.plan_end[0:1, bass.ds(i, 1)], min_val=1, max_val=MAX_PASSES)
                    used, used2 = held(sp, passes), held(sp, passes * 2)
                    sp.wait_ge(gate_up_done, 1)
                    sp.wait_ge(gate_up_done, used)
                    load_pair(K, sp, L, i + 2, slot, (0, 1))
                    sp.wait_ge(down_done, 2)
                    sp.wait_ge(down_done, used2)
                    load_pair(K, sp, L, i + 2, slot, (2,))

                with sp.Fori(0, PAIRS // 2 - 1) as turn:
                    for u in range(2):
                        refill(turn * 2 + u, u)

            @block.gpsimd
            def _(pool):
                pool.memset(xg[0], 0.0)
                pool.memset(xg[1], 0.0).then_inc(cleared, 1)
                pool.wait_ge(cleared, 1)
                gather(pool, 0, 0)
                gather(pool, 1, 1)

                def one_pass(n, u):
                    read = held(pool, 2 * (n + 1))
                    pool.wait_ge(cleared, 1)
                    pool.wait_ge(x_turned, read)
                    gather(pool, u, n + 2)
                    scatter(pool, u, n)

                loop(pool, one_pass)
                turns = pool.value_load(K.plan_turns[0:1, 0:1], min_val=PAIRS // 2, max_val=MAX_PASSES // 2)
                all_stored, all_gathered = held(pool, turns * 16), held(pool, turns * 16 + 16)
                for s in range(2):
                    pool.wait_ge(cleared, 1)
                    pool.wait_ge(stored[s], all_stored)
                    pool.wait_ge(gathered[s], all_gathered)

            @block.tensor
            def _(pe):
                for n in range(3):
                    slot_rows(pe, n % 2, n)
                turn_x(pe, 0, 0)

                def one_pass(n, u):
                    pair, slot = entry(pe, K.plan_pair, n, PAIRS - 1), entry(pe, K.plan_slot, n, 1)

                    def from_slot(w):
                        gate_up(pe, u, n, pair, w)
                        turn_x(pe, 1 - u, n + 1)
                        turn_h(pe, n)
                        slot_rows(pe, 1 - u, n + 3)
                        down(pe, n, pair, w)

                    with pe.If(slot > 0):
                        from_slot(1)
                    with pe.Else():
                        from_slot(0)

                loop(pe, one_pass)

            @block.scalar
            def _(act):
                keep_xt(act, 0, 0, 0)

                def one_pass(n, u):
                    sigmoid(act, n)
                    keep_xt(act, 1 - u, n + 1, 0)
                    keep_y(act, u, n, 0)

                loop(act, one_pass)

            @block.vector
            def _(dve):
                step = Chain(dve, steps)
                one_hot(dve, 0, 0)
                one_hot(dve, 1, 1)
                for n in range(3):
                    index_rows(dve, n % 2, ahead[1][:, n:n + 1], n, step)
                    if n < 2:
                        one_hot(dve, n % 2, n + 2)
                keep_xt(dve, 0, 0, 1)
                start = step.n

                def one_pass(n, u):
                    step = Chain(dve, steps, start + n * PASS_STEPS)
                    hidden(dve, n, step)
                    keep_xt(dve, 1 - u, n + 1, 1)
                    keep_ht(dve, n)
                    wait_from(dve, stored[u], through(n - 2, u))
                    dve.wait_ge(index_made, n + 3)
                    dve.tensor_copy(row[u][:], ahead[1 - u][:, 0:1])
                    dve.tensor_copy(ahead[u][:, 0:2], ahead[1 - u][:, 1:3])
                    index_rows(dve, 1 - u, ahead[u][:, 2:3], n + 3, step)
                    one_hot(dve, u, n + 4)
                    keep_y(dve, u, n, 1)

                loop(dve, one_pass)


def combine(K, L, out=None):
    nc, X, B = K.nc, K.X, K.banks
    with Phase(nc) as scope:
        def sb(name, shape, dt=F32):
            return scope.enter_context(nc.sbuf_tensor(f"{name}{L}", shape, dt))

        def sem(name):
            return scope.sem(f"combine{L}_{name}")
        BY_TENSOR = TOPK - BY_VECTOR
        rows = K.arena.rearrange("p (t j d) -> p t j d", t=NT, j=TOPK)
        diagonal = sb("diagonal", [P, NT, BY_TENSOR, P])
        loaded = [sem(f"rows{t}") for t in range(NT)]
        added, diagonals, summed = sem("added"), sem("diagonals"), sem("summed")
        ADDS = BY_VECTOR + 2
        ln = LayerNorm(K, scope, f"ln2_{L}", K.in_["ln2_g"][L:L + 1, :], K.in_["ln2_b"][L:L + 1, :])
        y = K.y_rows.rearrange("(j t p) d -> t p j d", j=TOPK, p=P)
        with nc.Block() as block:
            @block.sync
            def _(sp):
                for t in range(NT):
                    sp.dma_start(rows[:, t], y[t]).then_inc(loaded[t], 16)
                    if t == 0:
                        ln.load(sp)
                if out is not None:
                    for t in range(NT):
                        sp.wait_ge(ln.done, 2 * (t + 1))
                        sp.dma_start(out[0, t * P:(t + 1) * P, :], X[:, t, :]).then_inc(K.out_stored, 16)
                    sp.wait_ge(K.out_stored, 16 * NT)

            @block.tensor
            def _(pe):
                pe.wait_ge(diagonals, NT * BY_TENSOR)
                for t in range(NT):
                    pe.wait_ge(loaded[t], 16)
                    if t >= 2:
                        pe.wait_ge(added, ADDS * (t - 1))
                    for half in range(2):
                        for j in range(BY_TENSOR):
                            last = pe.matmul(B[2 * (t % 2) + half][:], diagonal[:, t, j, :],
                                             rows[:, t, BY_VECTOR + j, half * 512:(half + 1) * 512],
                                             start=(j == 0), stop=(j == BY_TENSOR - 1))
                        last.then_inc(summed, 1)

            @block.vector
            def _(dve):
                step = Chain(dve, added)
                for t in range(NT):
                    dve.wait_ge(loaded[t], 16)
                    for j in range(BY_VECTOR):
                        step(dve.scalar_tensor_tensor(X[:, t, :], rows[:, t, j, :], K.gates[:, t, j:j + 1], X[:, t, :],
                                                      ALU.mult, ALU.add))
                    for half in range(2):
                        dve.wait_ge(summed, 2 * t + half + 1)
                        x = X[:, t, half * 512:(half + 1) * 512]
                        step.inc(dve.tensor_tensor(x, x, B[2 * (t % 2) + half][:], ALU.add))
                    dve.wait_ge(added, step.n)
                    ln.normalize(dve, X[:, t, :], t)

            @block.scalar
            def _(act):
                for t in range(NT):
                    for j in range(BY_TENSOR):
                        act.activation(diagonal[:, t, j, :], K.ident[:], ACT.Copy,
                                       scale=K.gates[:, t, BY_VECTOR + j:BY_VECTOR + j + 1]).then_inc(diagonals, 1)
                for t in range(NT):
                    ln.root(act, t)

            @block.gpsimd
            def _(pool):
                for t in range(NT):
                    ln.affine(pool, X[:, t, :], t)


class LayerNorm:

    def __init__(self, K, scope, name, g, b):
        nc = K.nc
        self.src = (g, b)
        self.g = scope.enter_context(nc.sbuf_tensor(f"{name}_g", [P, D], F32))
        self.b = scope.enter_context(nc.sbuf_tensor(f"{name}_b", [P, D], F32))
        self.stats = scope.enter_context(nc.sbuf_tensor(f"{name}_stats", [P, 2, 6], F32))
        self.mv = scope.enter_context(nc.sbuf_tensor(f"{name}_mv", [P, 2], F32))
        self.rstd = scope.enter_context(nc.sbuf_tensor(f"{name}_rstd", [P, 1], F32))
        self.loaded = scope.sem(f"{name}_loaded")
        self.steps = scope.sem(f"{name}_steps")
        self.normal = scope.sem(f"{name}_normal")
        self.rooted = scope.sem(f"{name}_rooted")
        self.done = scope.sem(f"{name}_done")

    def load(self, eng):
        for dst, src in zip((self.g, self.b), self.src):
            eng.dma_start(dst[:], src.broadcast_to([P, D])).then_inc(self.loaded, 16)

    def normalize(self, dve, x, t):
        step = Chain(dve, self.steps, t * 4)
        dve.bn_stats(self.stats[:, 0, :], x[:, 0:512])
        step(dve.bn_stats(self.stats[:, 1, :], x[:, 512:D]))
        step(dve.bn_aggr(self.mv[:], self.stats[:].rearrange("p a b -> p (a b)")))
        step(dve.tensor_scalar_add(self.rstd[:], self.mv[:, 1:2], LN_EPS))
        dve.wait_ge(self.rooted, t + 1)
        step(dve.reciprocal(self.rstd[:], self.rstd[:]))
        ins = dve.tensor_scalar(x, x, self.mv[:, 0:1], self.rstd[:], ALU.subtract, ALU.mult)
        ins.then_inc(self.normal, 1)
        dve.wait_ge(self.normal, t + 1)

    def root(self, act, t):
        act.wait_ge(self.steps, 4 * t + 3)
        act.activation(self.rstd[:], self.rstd[:], ACT.Sqrt).then_inc(self.rooted, 1)

    def affine(self, pool, x, t):
        if t == 0:
            pool.wait_ge(self.loaded, 32)
        pool.wait_ge(self.normal, t + 1)
        pool.tensor_tensor(x, x, self.g[:], ALU.mult).then_inc(self.done, 1)
        pool.wait_ge(self.done, 2 * t + 1)
        pool.tensor_tensor(x, x, self.b[:], ALU.add).then_inc(self.done, 1)


class Turner:

    def __init__(self, K, scope, name, src, dst, n_tiles):
        self.K, self.dst, self.n_tiles = K, dst, n_tiles
        self.src = src.rearrange("p t (q k) -> p t k q", k=KD)
        self.turned = scope.sem(f"{name}_turned")
        self.by_act = scope.sem(f"{name}_by_act")
        self.by_dve = scope.sem(f"{name}_by_dve")

    def turn(self, pe):
        for k in range(KD):
            if k >= 4:
                pe.wait_ge(self.by_dve if k % 2 else self.by_act, (k - 4) // 2 + 1)
            for t in range(self.n_tiles):
                last = pe.transpose(self.K.banks[k % 4][:, t * P:(t + 1) * P], self.src[:, t, k, :], self.K.ident[:])
            last.then_inc(self.turned, 1)

    def copy_even(self, act):
        for k in range(0, KD, 2):
            act.wait_ge(self.turned, k + 1)
            act.activation(self.dst[:, k, :], self.K.banks[k % 4][:, 0:self.n_tiles * P], ACT.Copy).then_inc(self.by_act, 1)

    def copy_odd(self, dve):
        for k in range(1, KD, 2):
            dve.wait_ge(self.turned, k + 1)
            dve.tensor_copy(self.dst[:, k, :], self.K.banks[k % 4][:, 0:self.n_tiles * P]).then_inc(self.by_dve, 1)

    def await_all(self, eng):
        eng.wait_ge(self.by_act, KD // 2)
        eng.wait_ge(self.by_dve, KD // 2)


def memory_keys(K, make_constants):
    nc, B = K.nc, K.banks
    NM = NMEM // P
    with Phase(nc) as scope:
        def sb(name, shape, dt=F32):
            return scope.enter_context(nc.sbuf_tensor(name, shape, dt))

        def sem(name):
            return scope.sem(f"mem_{name}")

        M = sb("mem", [P, NM, D])
        MT = sb("memT", [P, KD, NMEM])
        w = sb("w_mem", [P, KD, 2 * MEMW])
        ln = LayerNorm(K, scope, "mem_ln", K.in_["mem_ln_g"].rearrange("(a d) -> a d", a=1),
                       K.in_["mem_ln_b"].rearrange("(a d) -> a d", a=1))
        turner = Turner(K, scope, "mem_turn", M[:], MT, NM)
        loaded, loaded_w, made, kept = sem("loaded"), sem("loaded_w"), sem("made"), sem("kept")
        with nc.Block() as block:
            @block.sync
            def _(sp):
                sp.dma_start(M[:], K.in_["mem"][0].rearrange("(t p) d -> p t d", p=P)).then_inc(loaded, 16)
                ln.load(sp)
                sp.dma_start(K.X[:], K.in_["x"][0].rearrange("(t p) d -> p t d", p=P)).then_inc(K.x_loaded, 16)
                sp.dma_start(w[:], K.in_["w_mem_kv"].rearrange("(p k) n -> p k n", k=KD)).then_inc(loaded_w, 16)
                sp.wait_ge(K.x_loaded, 16)

            @block.gpsimd
            def _(pool):
                make_constants(pool)

            @block.vector
            def _(dve):
                dve.wait_ge(loaded, 16)
                for t in range(NM):
                    ln.normalize(dve, M[:, t, :], t)
                    ln.affine(dve, M[:, t, :], t)
                turner.copy_odd(dve)
                for j in range(2):
                    dve.wait_ge(made, 3 + j)
                    dve.tensor_copy(K.v_mem[:, j, :], B[6 + j][:, 0:MEMW]).then_inc(kept, 1)

            @block.scalar
            def _(act):
                for t in range(NM):
                    ln.root(act, t)
                turner.copy_even(act)
                for j in range(2):
                    act.wait_ge(made, j + 1)
                    for o in range(2):
                        act.activation(K.k_memT[:, 2 * j + o, :], B[4 + j][o * HD:(o + 1) * HD, 0:NMEM], ACT.Copy).then_inc(kept, 1)


            @block.tensor
            def _(pe):
                pe.wait_ge(K.constants_made, K.ident_made)
                pe.wait_ge(ln.done, 2 * NM)
                turner.turn(pe)
                turner.await_all(pe)
                pe.wait_ge(loaded_w, 16)
                for j in range(2):
                    for k in range(KD):
                        last = pe.matmul(B[4 + j][:, 0:NMEM], w[:, k, j * P:(j + 1) * P], MT[:, k, :], start=(k == 0), stop=(k == KD - 1))
                    last.then_inc(made, 1)
                for j in range(NM):
                    for k in range(KD):
                        last = pe.matmul(B[6 + j][:, 0:MEMW], MT[:, k, j * P:(j + 1) * P], w[:, k, MEMW:2 * MEMW], start=(k == 0), stop=(k == KD - 1))
                    last.then_inc(made, 1)


WC = 256


def fox_layer(K, L, j):
    nc, B, arena = K.nc, K.banks, K.arena
    at = [0]

    def carve(parts, shape):
        n = int(np.prod(shape))
        view = arena[0:parts, at[0]:at[0] + n]
        at[0] += n
        return view.rearrange("p (a b) -> p a b", a=shape[0])

    HK = HD + 1
    qT = carve(HK, (NH, T))
    kT = carve(HK, (NH, T))
    v = carve(P, (NT, TOKW))
    sg = carve(P, (NT, TOKW))
    qmT = carve(HD, (NMH, T))
    mix = carve(P, (NT, D))
    w_in = K.in_["fox_w_in"][j].rearrange("(p k) n -> p k n", k=KD)

    with Phase(nc) as scope:
        def sb(name, shape, dt=F32):
            return scope.enter_context(nc.sbuf_tensor(name, shape, dt))

        def sem(name):
            return scope.sem(f"foxin_{name}")

        NB = 4
        wc = [sb(f"foxw{s}", [P, KD, WC]) for s in range(NB)]
        wf = sb("foxwf", [P, KD, NH])
        bf = sb("foxbf", [P, 1, NH])
        fl = sb("foxfl", [P, NT, NH])
        ab = sb("foxab", [P, NT, NH])
        cT = sb("foxcT", [NH, T])
        chunks = [("q", c) for c in range(3)] + [("k", c) for c in range(3)] + [("v", c) for c in range(3)] \
            + [("g", c) for c in range(3)] + [("m", 0)]
        first_col = {"q": 0, "k": TOKW, "v": 2 * TOKW, "g": 3 * TOKW, "m": 4 * TOKW + NH}
        turner = Turner(K, scope, "fox_turn", K.X[:], K.XT, NT)
        loaded = [sem(f"loaded{s}") for s in range(NB)]
        loaded_f, made, kept_a, kept_d = sem("loaded_f"), sem("made"), sem("kept_a"), sem("kept_d")
        f_made, f_steps, f_act, c_made, c_kept, c_moved = (sem(n) for n in ("f_made", "f_steps", "f_act", "c_made", "c_kept", "c_moved"))
        ones_row = sem("ones_row")

        with nc.Block() as block:
            @block.sync
            def _(sp):
                sp.dma_start(wf[:], w_in[:, :, 4 * TOKW:4 * TOKW + NH]).then_inc(loaded_f, 16)
                sp.dma_start(bf[:, 0, :], K.in_["fox_b_f"][j:j + 1, :].broadcast_to([P, NH])).then_inc(loaded_f, 16)
                for n, (kind, c) in enumerate(chunks):
                    if n >= NB:
                        sp.wait_ge(made, 2 * (n - NB + 1))
                    c0 = first_col[kind] + c * WC
                    sp.dma_start(wc[n % NB][:], w_in[:, :, c0:c0 + WC]).then_inc(loaded[n % NB], 16)
                sp.wait_ge(c_kept, 1)
                sp.wait_ge(ones_row, 1)
                sp.dma_start(kT[HD:HK, :, :].rearrange("p h t -> p (h t)"), cT[:, :]).then_inc(c_moved, 16)
                sp.wait_ge(c_moved, 16)

            @block.gpsimd
            def _(pool):
                pool.memset(qT[HD:HK], 1.0).then_inc(ones_row, 1)

            @block.tensor
            def _(pe):
                turner.turn(pe)
                turner.await_all(pe)
                pe.wait_ge(loaded_f, 32)
                for t in range(NT):
                    for k in range(KD):
                        last = pe.matmul(B[0][:, t * NH:(t + 1) * NH], K.XT[:, k, t * P:(t + 1) * P], wf[:, k, :],
                                         start=(k == 0), stop=(k == KD - 1))
                last.then_inc(f_made, 1)
                for n, (kind, c) in enumerate(chunks):
                    pe.wait_ge(loaded[n % NB], 16 * (n // NB + 1))
                    for o in range(2):
                        bank = B[4 + (2 * n + o) % 4]
                        if n >= 2:
                            pe.wait_ge(kept_a if o == 0 else kept_d, n - 1)
                        if kind in "qkm":
                            for k in range(KD):
                                last = pe.matmul(bank[:], wc[n % NB][:, k, o * P:(o + 1) * P], K.XT[:, k, :],
                                                 start=(k == 0), stop=(k == KD - 1))
                        else:
                            for t in range(2):
                                for k in range(KD):
                                    tt = 2 * o + t
                                    last = pe.matmul(bank[:, t * WC:(t + 1) * WC], K.XT[:, k, tt * P:(tt + 1) * P], wc[n % NB][:, k, :],
                                                     start=(k == 0), stop=(k == KD - 1))
                        last.then_inc(made, 1)
                    if n == 4:
                        pe.wait_ge(f_steps, 4)
                        for t in range(NT):
                            for t0 in range(t + 1):
                                last = pe.matmul(B[1][0:NH, t * P:(t + 1) * P], fl[:, t0, :], (K.upto if t0 == t else K.ones)[:],
                                                 start=(t0 == 0), stop=(t0 == t))
                        last.then_inc(c_made, 1)

            def keep(eng, o, is_act, kept):
                for n, (kind, c) in enumerate(chunks):
                    eng.wait_ge(made, 2 * n + 1 + o)
                    bank = B[4 + (2 * n + o) % 4]
                    if kind in "qkm":
                        dst = {"q": qT, "k": kT, "m": qmT}[kind]
                        for e in range(2):
                            out, src = dst[0:HD, 4 * c + 2 * o + e, :], bank[e * HD:(e + 1) * HD, :]
                            last = eng.activation(out, src, ACT.Copy) if is_act else eng.tensor_copy(out, src)
                    else:
                        dst = (v if kind == "v" else sg)[:, 2 * o:2 * o + 2, c * WC:(c + 1) * WC]
                        src = bank[:].rearrange("p (t c) -> p t c", t=2)
                        if kind == "g":
                            last = eng.activation(dst, src, ACT.Sigmoid) if is_act else eng.tensor_copy(dst, src)
                        else:
                            last = eng.activation(dst, src, ACT.Copy) if is_act else eng.tensor_copy(dst, src)
                    last.then_inc(kept, 1)
                    yield n

            @block.scalar
            def _(act):
                turner.copy_even(act)
                for n in keep(act, 0, True, kept_a):
                    if n == 0:
                        act.wait_ge(f_steps, 2)
                        act.activation(ab[:], ab[:], ACT.Exp, scale=-1.0).then_inc(f_act, 1)
                    if n == 1:
                        act.wait_ge(f_steps, 3)
                        act.activation(ab[:], ab[:], ACT.Ln).then_inc(f_act, 1)
                act.wait_ge(kept_d, len(chunks))
                act.activation(sg[:, 2:4, :], sg[:, 2:4, :], ACT.Sigmoid)

            @block.vector
            def _(dve):
                step = Chain(dve, f_steps)
                turner.copy_odd(dve)
                for n in keep(dve, 1, False, kept_d):
                    if n == 0:
                        dve.wait_ge(f_made, 1)
                        step(dve.tensor_tensor(fl[:], B[0][:, 0:NT * NH].rearrange("p (t h) -> p t h", t=NT),
                                               bf[:].to_broadcast([P, NT, NH]), ALU.add))
                        step(dve.scalar_tensor_tensor(ab[:], fl[:], -1.0, fl[:], ALU.mult, ALU.max))
                        dve.wait_ge(f_act, 1)
                        step(dve.tensor_scalar_add(ab[:], ab[:], 1.0))
                        dve.wait_ge(f_act, 2)
                        step(dve.scalar_tensor_tensor(fl[:], fl[:], 0.0, ab[:], ALU.min, ALU.subtract))
                    if n == 6:
                        dve.wait_ge(c_made, 1)
                        dve.tensor_scalar_mul(cT[:], B[1][0:NH, :], -(HD ** 0.5)).then_inc(c_kept, 1)

    units = [("tok", h, t) for h in range(NH) for t in range(NT)] + [("mem", h, t) for h in range(NMH) for t in range(NT)]
    attention(K, f"att{L}", units, dict(qT=qT, kT=kT, v=v, sg=sg, qmT=qmT, mix=mix))
    output_projection(K, L, mix)


def attention(K, name, units, d):
    nc, B = K.nc, K.banks
    SCALE = HD ** -0.5
    with Phase(nc) as scope:
        def sb(nm, shape, dt=F32):
            return scope.enter_context(nc.sbuf_tensor(f"{name}_{nm}", shape, dt))

        def sem(nm):
            return scope.sem(f"{name}_{nm}")
        prob = [sb(f"prob{s}", [P, T]) for s in range(2)]
        probT = [sb(f"probT{s}", [P, T]) for s in range(2)]
        N = len(units)
        nmax = sb("nmax", [P, 2])
        total = sb("total", [P, 4])
        inv = sb("inv", [P, 2])
        scored, maxed, exped, turned, kept, weighed, out = (sem(n) for n in ("scored", "maxed", "exped", "turned", "kept", "weighed", "out"))
        steps = sem("steps")

        def keys(u):
            return P * (u[2] + 1) if u[0] == "tok" else NMEM

        with nc.Block() as block:
            @block.tensor
            def _(pe):
                def scores(n):
                    kind, h, t = units[n]
                    if n >= 2:
                        pe.wait_ge(exped, n - 1)
                    bank = B[n % 2]
                    if kind == "tok":
                        pe.matmul(bank[:, 0:keys(units[n])], d["qT"][:, h, t * P:(t + 1) * P], d["kT"][:, h, 0:keys(units[n])],
                                  start=True, stop=False, skip_group_check=True)
                        last = pe.matmul(bank[:, t * P:(t + 1) * P], K.ident16[:], K.causal[:], start=False, stop=True, skip_group_check=True)
                    else:
                        last = pe.matmul(bank[:, 0:NMEM], d["qmT"][:, h, t * P:(t + 1) * P], K.k_memT[:, h, :], start=True, stop=True)
                    last.then_inc(scored, 1)

                def turn(n):
                    pe.wait_ge(exped, n + 1)
                    if n >= 2:
                        pe.wait_ge(kept, n - 1)
                    for b in range(keys(units[n]) // P):
                        last = pe.transpose(B[2 + n % 2][:, b * P:(b + 1) * P], prob[n % 2][:, b * P:(b + 1) * P], K.ident[:])
                    last.then_inc(turned, 1)

                def weigh(n):
                    kind, h, t = units[n]
                    pe.wait_ge(kept, n + 1)
                    if n >= 2:
                        pe.wait_ge(out, n - 1)
                    val = d["v"] if kind == "tok" else K.v_mem
                    nb = keys(units[n]) // P
                    for b in range(nb):
                        last = pe.matmul(B[4 + n % 2][:, 0:HD], probT[n % 2][:, b * P:(b + 1) * P], val[:, b, h * HD:(h + 1) * HD],
                                         start=(b == 0), stop=(b == nb - 1))
                    last.then_inc(weighed, 1)

                for n in range(N + 2):
                    if n < N:
                        scores(n)
                    if 1 <= n <= N:
                        turn(n - 1)
                    if n >= 2:
                        weigh(n - 2)

            @block.scalar
            def _(act):
                for n in range(N + 1):
                    if n < N:
                        act.wait_ge(maxed, n + 1)
                        if n >= 2:
                            act.wait_ge(turned, n - 1)
                        if n >= 4:
                            act.wait_ge(out, n - 3)
                        w = keys(units[n])
                        act.activation(prob[n % 2][:, 0:w], B[n % 2][:, 0:w], ACT.Exp, bias=nmax[:, n % 2:n % 2 + 1], scale=SCALE,
                                       accum_out=total[:, n % 4:n % 4 + 1]).then_inc(exped, 1)
                    if n >= 1:
                        m = n - 1
                        act.wait_ge(turned, m + 1)
                        if m >= 2:
                            act.wait_ge(weighed, m - 1)
                        w = keys(units[m])
                        act.activation(probT[m % 2][:, 0:w], B[2 + m % 2][:, 0:w], ACT.Copy).then_inc(kept, 1)

            @block.vector
            def _(dve):
                step = Chain(dve, steps)
                for n in range(N + 2):
                    if n < N:
                        dve.wait_ge(scored, n + 1)
                        if n >= 2:
                            dve.wait_ge(exped, n - 1)
                        step(dve.tensor_reduce(nmax[:, n % 2:n % 2 + 1], B[n % 2][:, 0:keys(units[n])], AX.X, ALU.max))
                        dve.tensor_scalar_mul(nmax[:, n % 2:n % 2 + 1], nmax[:, n % 2:n % 2 + 1], -SCALE).then_inc(maxed, 1)
                    if n >= 2:
                        m = n - 2
                        kind, h, t = units[m]
                        dve.wait_ge(exped, m + 1)
                        step(dve.reciprocal(inv[:, m % 2:m % 2 + 1], total[:, m % 4:m % 4 + 1]))
                        dve.wait_ge(weighed, m + 1)
                        o = B[4 + m % 2][:, 0:HD]
                        if kind == "tok":
                            dve.scalar_tensor_tensor(d["mix"][:, t, h * HD:(h + 1) * HD], o, inv[:, m % 2:m % 2 + 1],
                                                     d["sg"][:, t, h * HD:(h + 1) * HD], ALU.mult, ALU.mult).then_inc(out, 1)
                        else:
                            dve.tensor_scalar_mul(d["mix"][:, t, TOKW + h * HD:TOKW + (h + 1) * HD], o, inv[:, m % 2:m % 2 + 1]).then_inc(out, 1)


def output_projection(K, L, mix):
    nc, B, X = K.nc, K.banks, K.X
    with Phase(nc) as scope:
        w = scope.enter_context(nc.sbuf_tensor(f"w_out{L}", [P, KD, D], F32))
        ln = LayerNorm(K, scope, f"ln1_{L}", K.in_["ln1_g"][L:L + 1, :], K.in_["ln1_b"][L:L + 1, :])
        turner = Turner(K, scope, f"mix_turn{L}", mix, K.XT, NT)
        loaded, made, added = (scope.sem(f"outp{L}_{n}") for n in ("loaded", "made", "added"))
        with nc.Block() as block:
            @block.sync
            def _(sp):
                sp.dma_start(w[:], K.in_["w_out"][L].rearrange("(p k) n -> p k n", k=KD)).then_inc(loaded, 16)
                ln.load(sp)

            @block.tensor
            def _(pe):
                turner.turn(pe)
                turner.await_all(pe)
                pe.wait_ge(loaded, 16)
                for t in range(NT):
                    for n in range(2):
                        i = 2 * t + n
                        if i >= 4:
                            pe.wait_ge(added, i - 3)
                        for k in range(KD):
                            last = pe.matmul(B[4 + i % 4][:], K.XT[:, k, t * P:(t + 1) * P], w[:, k, n * 512:(n + 1) * 512],
                                             start=(k == 0), stop=(k == KD - 1))
                        last.then_inc(made, 1)

            @block.scalar
            def _(act):
                turner.copy_even(act)
                for t in range(NT):
                    ln.root(act, t)

            @block.vector
            def _(dve):
                turner.copy_odd(dve)
                for t in range(NT):
                    for n in range(2):
                        i = 2 * t + n
                        dve.wait_ge(made, i + 1)
                        xs = X[:, t, n * 512:(n + 1) * 512]
                        dve.scalar_tensor_tensor(xs, xs, ALPHA, B[4 + i % 4][:], ALU.mult, ALU.add).then_inc(added, 1)
                    dve.wait_ge(added, 2 * t + 2)
                    ln.normalize(dve, X[:, t, :], t)

            @block.gpsimd
            def _(pool):
                for t in range(NT):
                    ln.affine(pool, X[:, t, :], t)


C0 = float(np.exp(-0.5))
TILES = TOKW // P
N_VEC = 20 + 5 * TILES
MU, W0, A0, KK, KA, RK = 0, 20, 26, 32, 38, 44
GROUPS, GH = 3, 4
ROOT_SLOTS = 5
LEVELS = 7


def rwkv_layer(K, L, j):
    nc, B, arena = K.nc, K.banks, K.arena
    at = [0]

    def carve(parts, shape, start=None):
        n = int(np.prod(shape))
        s = at[0] if start is None else start
        if start is None:
            at[0] += n
        return arena[0:parts, s:s + n].rearrange("p (a b) -> p a b", a=shape[0])

    R = Names()
    R.AR = carve(P, (TILES * NT, 2 * P))
    R.vT = carve(P, (TILES, T), 0)
    R.bT = carve(P, (TILES, T))
    R.kT = carve(P, (TILES, T))
    R.V = carve(P, (NT, TOKW))
    rk_at = at[0]
    R.r = carve(P, (TILES, T))
    R.k = carve(P, (TILES, T))
    mix = carve(P, (NT, D), rk_at)
    R.Bt = carve(P, (1, TOKW), rk_at + NT * D)
    R.Kt = carve(P, (1, TOKW), rk_at + NT * D + TOKW)
    R.gd = carve(P, (1, T))
    qmT = carve(HD, (NMH, T))
    R.S = carve(P, (TILES, HD))
    w_in = K.in_["rwkv_w_in"][j].rearrange("(p k) n -> p k n", k=KD)

    with ExitStack() as outer:
        def sbo(name, shape, dt=F32):
            return outer.enter_context(nc.sbuf_tensor(f"rwkv_{name}", shape, dt))
        R.bonus = sbo("bonus", [P, NT, NH])
        R.f = sbo("f", [P, TILES, NT])
        g2 = sbo("g2", [P, TOKW])
        with Phase(nc) as scope:
            def sb(name, shape, dt=F32):
                return scope.enter_context(nc.sbuf_tensor(f"rwkv_{name}", shape, dt))
            R.vec = sb("vec", [P, N_VEC])
            R.one_ka = sb("one_ka", [P, TILES])
            R.lo = sb("lo", [P, T])
            R.w2a2 = sb("w2a2", [P, TOKW])
            rwkv_inputs(K, R, j, w_in, qmT, g2)
            rwkv_channels(K, R)
        rwkv_chunks(K, R, j, g2, mix)
    units = [("mem", h, t) for h in range(NMH) for t in range(NT)]
    attention(K, f"att{L}", units, dict(qmT=qmT, mix=mix))
    output_projection(K, L, mix)


def rwkv_inputs(K, R, j, w_in, qmT, g2):
    nc, B = K.nc, K.banks
    with Phase(nc) as scope:
        def sb(name, shape, dt=F32):
            return scope.enter_context(nc.sbuf_tensor(f"rin_{name}", shape, dt))

        def sem(name):
            return scope.sem(f"rin_{name}")
        NB = 3
        wc = [sb(f"w{s}", [P, KD, WC]) for s in range(NB)]
        h = [sb(f"h{s}", [P, T + 1]) for s in range(2)]
        rows = sb("rows", [N_VEC, P])
        sq = [sb(f"sq{s}", [P, T]) for s in range(2)]
        nrm = [sb(f"nrm{s}", [P, T]) for s in range(2)]
        kk1, sqd, ssd, rooted, norm = (sem(n) for n in ("kk1", "sqd", "ssd", "rooted", "norm"))
        K0 = 6
        turner = Turner(K, scope, "rin_turn", K.X[:], K.XT, NT)
        loaded = [sem(f"loaded{s}") for s in range(NB)]
        small, vec_t, vec_k, made, copied, zeroed, mixed, steps = (
            sem(n) for n in ("small", "vec_t", "vec_k", "made", "copied", "zeroed", "mixed", "steps"))
        dests = [R.r[:, i, :] for i in range(6)] + [R.k[:, i, :] for i in range(6)] + [R.vT[:, i, :] for i in range(6)] \
            + [R.lo[:], R.gd[:, 0, :]]
        n_mixed, n_tiles = len(dests), len(dests) + 2
        with nc.Block() as block:
            @block.sync
            def _(sp):
                I = K.in_
                vectors = [(I["rwkv_mu"][j].rearrange("(n p) -> n p", p=P), MU)] + [
                    (I[nm][j].rearrange("(n p) -> n p", p=P), o)
                    for nm, o in (("rwkv_w0", W0), ("rwkv_a0", A0), ("rwkv_k_k", KK), ("rwkv_k_a", KA))] + [
                    (I["rwkv_r_k"][j].rearrange("(n two) d -> n (two d)", two=2), RK)]
                for src, o in vectors:
                    sp.dma_start(rows[o:o + src.shape[0], :], src).then_inc(small, 16)
                sp.dma_start(R.w2a2[0:64, :], I["rwkv_w2"][j]).then_inc(small, 16)
                sp.dma_start(R.w2a2[64:128, :], I["rwkv_a2"][j]).then_inc(small, 16)
                sp.dma_start(g2[:], I["rwkv_g2"][j]).then_inc(small, 16)
                for n in range(n_tiles // 2):
                    if n >= NB:
                        sp.wait_ge(made, 2 * (n - NB + 1))
                    sp.dma_start(wc[n % NB][:], w_in[:, :, n * WC:(n + 1) * WC]).then_inc(loaded[n % NB], 16)
                sp.wait_ge(small, 16 * 9)

            @block.tensor
            def _(pe):
                turner.turn(pe)
                pe.wait_ge(small, 16 * 9)
                turner.await_all(pe)
                pe.transpose(B[0][:, 0:N_VEC], rows[:], K.ident[0:N_VEC, 0:N_VEC]).then_inc(vec_t, 1)
                for i in range(n_tiles):
                    n, o = i // 2, i % 2
                    pe.wait_ge(loaded[n % NB], 16 * (n // NB + 1))
                    if i >= 4:
                        pe.wait_ge(copied, i - 3)
                    for k in range(KD):
                        last = pe.matmul(B[4 + i % 4][:], wc[n % NB][:, k, o * P:(o + 1) * P], K.XT[:, k, :],
                                         start=(k == 0), stop=(k == KD - 1))
                    last.then_inc(made, 1)
                    m = i - K0 - 2
                    if 0 <= m < TILES:
                        pe.wait_ge(sqd, m + 1)
                        if m >= 2:
                            pe.wait_ge(rooted, m - 1)
                        pe.matmul(B[1 + m % 2][:], K.heads[:], sq[m % 2][:], start=True, stop=True).then_inc(ssd, 1)

            @block.gpsimd
            def _(pool):
                for s in range(2):
                    last = pool.memset(h[s][:, 0:1], 0.0)
                last.then_inc(zeroed, 1)
                for i in range(TILES):
                    pool.wait_ge(kk1, i + 1)
                    if i >= 2:
                        pool.wait_ge(ssd, i - 1)
                    pool.tensor_tensor(sq[i % 2][:], R.bT[:, i, :], R.bT[:, i, :], ALU.mult).then_inc(sqd, 1)

            @block.scalar
            def _(act):
                turner.copy_even(act)
                for i in range(n_tiles):
                    act.wait_ge(made, i + 1)
                    if i < n_mixed:
                        if i >= 2:
                            act.wait_ge(mixed, i - 1)
                        act.activation(h[i % 2][:, 1:T + 1], B[4 + i % 4][:], ACT.Copy).then_inc(copied, 1)
                    else:
                        for e in range(2):
                            last = act.activation(qmT[:, 2 * (i - n_mixed) + e, :], B[4 + i % 4][e * HD:(e + 1) * HD, :], ACT.Copy)
                        last.then_inc(copied, 1)
                    m = i - K0 - 3
                    if 0 <= m < TILES:
                        act.wait_ge(ssd, m + 1)
                        if m >= 2:
                            act.wait_ge(norm, m - 1)
                        act.activation(nrm[m % 2][:], B[1 + m % 2][:], ACT.Sqrt).then_inc(rooted, 1)
                act.wait_ge(mixed, n_mixed)
                act.activation(R.lo[0:64, :], R.lo[0:64, :], ACT.Tanh)
                act.activation(R.gd[:, 0, :], R.gd[:, 0, :], ACT.Sigmoid)

            @block.vector
            def _(dve):
                turner.copy_odd(dve)
                step = Chain(dve, steps)
                dve.wait_ge(vec_t, 1)
                dve.tensor_copy(R.vec[:], B[0][:, 0:N_VEC]).then_inc(vec_k, 1)
                dve.wait_ge(vec_k, 1)
                step(dve.tensor_scalar(R.one_ka[:], R.vec[:, KA:KA + TILES], -1.0, 1.0, ALU.mult, ALU.add))
                dve.wait_ge(zeroed, 1)
                for i in range(n_mixed):
                    dve.wait_ge(copied, i + 1)
                    hi = h[i % 2]
                    step(dve.tensor_tensor(dests[i], hi[:, 0:T], hi[:, 1:T + 1], ALU.subtract))
                    dve.scalar_tensor_tensor(dests[i], dests[i], R.vec[:, MU + i:MU + i + 1], hi[:, 1:T + 1], ALU.mult, ALU.add).then_inc(mixed, 1)
                    if K0 <= i < K0 + TILES:
                        m = i - K0
                        dve.wait_ge(mixed, i + 1)
                        dve.tensor_scalar_mul(R.bT[:, m, :], R.k[:, m, :], R.vec[:, KK + m:KK + m + 1]).then_inc(kk1, 1)
                    m = i - K0 - 4
                    if 0 <= m < TILES:
                        nm = nrm[m % 2][:]
                        dve.wait_ge(rooted, m + 1)
                        step(dve.tensor_scalar_max(nm, nm, 1e-12))
                        step(dve.reciprocal(nm, nm))
                        dve.wait_ge(sqd, m + 1)
                        dve.tensor_tensor(R.bT[:, m, :], R.bT[:, m, :], nm, ALU.mult).then_inc(norm, 1)


def rwkv_channels(K, R):
    nc, B = K.nc, K.banks
    with Phase(nc) as scope:
        def sb(name, shape, dt=F32):
            return scope.enter_context(nc.sbuf_tensor(f"rch_{name}", shape, dt))

        def sem(name):
            return scope.sem(f"rch_{name}")
        ew = [sb(f"ew{i}", [P, T]) for i in range(TILES)]
        ea = [sb(f"ea{i}", [P, T]) for i in range(TILES)]
        Sx = [sb(f"S{s}", [P, NT, P + 1]) for s in range(2)]
        ep = [sb(f"ep{s}", [P, NT, P + 1]) for s in range(2)]
        en = [sb(f"en{s}", [P, NT, P]) for s in range(2)]
        kf = [sb(f"kf{s}", [P, T]) for s in range(2)]
        rk = [sb(f"rk{s}", [P, T]) for s in range(2)]
        mid = [sb(f"mid{s}", [P, 2, NT]) for s in range(2)]
        fa = [sb(f"fa{s}", [P, NT - 1]) for s in range(2)]
        v_t, v_k, steps = sem("v_t"), sem("v_k"), sem("steps")
        lin, sigmoids, scanned, decayed, af, rkd, bonus, zeroed, b_made, tile_done = (
            sem(n) for n in ("lin", "sigmoids", "scanned", "decayed", "af", "rkd", "bonus", "zeroed", "b_made", "tile_done"))
        AR = R.AR.rearrange("p (i c) (x t) -> p i c x t", i=TILES, x=2)
        halves = ((0, 4), (4, 2))

        with nc.Block() as block:
            @block.tensor
            def _(pe):
                n = 0
                for t in range(NT):
                    for i0, ni in halves:
                        if n >= 4:
                            pe.wait_ge(v_k, n - 3)
                        for i in range(ni):
                            last = pe.transpose(B[n % 4][:, i * P:(i + 1) * P], R.vT[:, i0 + i, t * P:(t + 1) * P], K.ident[:])
                        last.then_inc(v_t, 1)
                        n += 1
                for i in range(TILES):
                    if i >= 1:
                        pe.wait_ge(sigmoids, 2 * i)
                    cols = slice(i * P, (i + 1) * P)
                    pe.matmul(B[4][:], R.w2a2[0:64, cols], R.lo[0:64, :], start=True, stop=True).then_inc(lin, 1)
                    pe.matmul(B[5][:], R.w2a2[64:128, cols], R.lo[64:128, :], start=True, stop=True).then_inc(lin, 1)
                for i in range(TILES):
                    pe.wait_ge(rkd, i + 1)
                    for t in range(NT):
                        last = pe.matmul(B[7][:, t * NH + 2 * i:t * NH + 2 * i + 2], rk[i % 2][:, t * P:(t + 1) * P],
                                         K.heads[:].rearrange("p (a b) -> p a b", a=2)[:, :, 0], start=True, stop=True)
                    last.then_inc(bonus, 1)

            @block.scalar
            def _(act):
                n = 0
                for t in range(NT):
                    for i0, ni in halves:
                        act.wait_ge(v_t, n + 1)
                        act.activation(R.V[:, t, i0 * P:(i0 + ni) * P], B[n % 4][:, 0:ni * P], ACT.Copy).then_inc(v_k, 1)
                        n += 1
                for i in range(TILES):
                    act.wait_ge(lin, 2 * i + 1)
                    act.activation(ew[i][:], B[4][:], ACT.Sigmoid, bias=R.vec[:, W0 + i:W0 + i + 1]).then_inc(sigmoids, 1)
                    act.wait_ge(lin, 2 * i + 2)
                    act.activation(ea[i][:], B[5][:], ACT.Sigmoid, bias=R.vec[:, A0 + i:A0 + i + 1]).then_inc(sigmoids, 1)
                for i in range(TILES):
                    s = i % 2
                    if i >= 2:
                        act.wait_ge(tile_done, i - 1)
                        act.wait_ge(b_made, i - 1)
                    act.wait_ge(scanned, i + 1)
                    for c in range(NT):
                        act.activation(ep[s][:, c, :], Sx[s][:, c, :], ACT.Exp, bias=mid[s][:, 0, c:c + 1], scale=-C0)
                        act.activation(en[s][:, c, :], Sx[s][:, c, 1:P + 1], ACT.Exp, bias=mid[s][:, 1, c:c + 1], scale=C0)
                    act.activation(R.f[:, i, 0:NT - 1], fa[s][:], ACT.Exp, scale=-C0).then_inc(decayed, 1)

            @block.gpsimd
            def _(pool):
                for s in range(2):
                    last = pool.memset(Sx[s][:], 0.0)
                last.then_inc(zeroed, 1)
                for i in range(TILES):
                    pool.wait_ge(tile_done, i + 1)
                    pool.tensor_tensor(R.bT[:, i, :], R.bT[:, i, :], ea[i][:], ALU.mult).then_inc(af, 1)
                    pool.wait_ge(af, i + 1)
                    pool.tensor_tensor(R.bT[:, i, :], R.bT[:, i, :], en[i % 2][:].rearrange("p c t -> p (c t)"), ALU.mult).then_inc(b_made, 1)

            @block.vector
            def _(dve):
                step = Chain(dve, steps)
                dve.wait_ge(v_t, 2 * NT)
                dve.wait_ge(zeroed, 1)
                def sums(i):
                    s = i % 2
                    dve.wait_ge(sigmoids, 2 * i + 1)
                    for c in range(NT):
                        w = ew[i][:, c * P:(c + 1) * P]
                        step.inc(dve.tensor_tensor_scan(Sx[s][:, c, 1:P + 1], w, w, 0.0, ALU.add, ALU.bypass))
                    dve.wait_ge(steps, step.n)
                    middle, end = Sx[s][:, :, P // 2], Sx[s][:, :, P]
                    step.inc(dve.tensor_scalar_mul(mid[s][:, 0, :], middle, C0))
                    step.inc(dve.tensor_scalar_mul(mid[s][:, 1, :], middle, -C0))
                    step(dve.tensor_tensor(fa[s][:], end[:, 0:NT - 1], middle[:, 0:NT - 1], ALU.subtract))
                    dve.tensor_tensor(fa[s][:], fa[s][:], middle[:, 1:NT], ALU.add).then_inc(scanned, 1)

                sums(0)
                for i in range(TILES):
                    s = i % 2
                    if i + 1 < TILES:
                        sums(i + 1)
                    dve.wait_ge(sigmoids, 2 * i + 2)
                    if i >= 2:
                        dve.wait_ge(bonus, i - 1)
                    step(dve.tensor_scalar(kf[s][:], ea[i][:], R.vec[:, KA + i:KA + i + 1], R.one_ka[:, i:i + 1], ALU.mult, ALU.add))
                    step(dve.tensor_tensor(kf[s][:], kf[s][:], R.k[:, i, :], ALU.mult))
                    dve.scalar_tensor_tensor(rk[s][:], R.r[:, i, :], R.vec[:, RK + i:RK + i + 1], kf[s][:], ALU.mult, ALU.mult).then_inc(rkd, 1)
                    dve.wait_ge(decayed, i + 1)
                    r4, k4 = (x[:, i, :].rearrange("p (c t) -> p c t", c=NT) for x in (R.r, R.bT))
                    dve.tensor_tensor(AR[:, i, :, 1, :], r4, ep[s][:, :, 1:P + 1], ALU.mult)
                    dve.scalar_tensor_tensor(AR[:, i, :, 0, :], k4, -1.0, ep[s][:, :, 0:P], ALU.mult, ALU.mult)
                    dve.tensor_tensor(R.kT[:, i, :], kf[s][:], en[s][:].rearrange("p c t -> p (c t)"), ALU.mult).then_inc(tile_done, 1)
                dve.wait_ge(bonus, TILES)
                step(dve.tensor_copy(R.bonus[:], B[7][:, 0:NT * NH].rearrange("p (t h) -> p t h", t=NT)))


def rwkv_chunks(K, R, j, g2, mix):
    nc, B = K.nc, K.banks
    with Phase(nc) as scope:
        def sb(name, shape, dt=F32):
            return scope.enter_context(nc.sbuf_tensor(f"rck_{name}", shape, dt))

        def sem(name):
            return scope.sem(f"rck_{name}")
        XTf = K.XT[:].rearrange("p k t -> p (k t)")
        Tm = XTf[:, 0:NH * P].rearrange("p (h t) -> p h t", h=NH)
        Xm = XTf[:, NH * P:2 * NH * P].rearrange("p (h t) -> p h t", h=NH)
        U = XTf[:, 2 * NH * P:2 * NH * P + TOKW].rearrange("p (h i) -> p h i", h=NH)
        A = sb("A", [P, NH, 4 * P])
        QT = sb("QT", [P, NH, P])
        W = sb("W", [P, NH, P])
        Z = sb("Z", [P, NH, HD])
        S = R.S
        y = sb("y", [P, NH, HD])
        yq = sb("yq", [P, NH, HD])
        G = sb("G", [P, TOKW])
        lnx = sb("lnx", [P, 2, TOKW])
        st = sb("st", [P, 3, NH])
        m = Names()
        m.small = sem("small")
        m.tok_t = sem("tok_t")
        m.tok_k = sem("tok_k")
        m.a_made = sem("a_made")
        m.a_kept = sem("a_kept")
        m.q = sem("q")
        m.w0 = sem("w0")
        m.t0_t = sem("t0_t")
        m.t0_k = sem("t0_k")
        m.x_made = sem("x_made")
        m.x_kept = sem("x_kept")
        m.t_made = sem("t_made")
        m.w_made = sem("w_made")
        m.t_added = sem("t_added")
        m.w_added = sem("w_added")
        m.z_made = sem("z_made")
        m.z_kept = sem("z_kept")
        m.u_made = sem("u_made")
        m.u_kept = sem("u_kept")
        m.y_made = sem("y_made")
        m.y_kept = sem("y_kept")
        m.st_made = sem("st_made")
        m.s_sum = sem("s_sum")
        m.s_done = sem("s_done")
        m.g_made = sem("g_made")
        m.g_kept = sem("g_kept")
        m.gn = sem("gn")
        m.v_ready = sem("v_ready")
        m.root = sem("root")
        m.outs = sem("outs")
        ARv = R.AR.rearrange("p (i c) x -> p i c x", i=TILES)
        LAST = LEVELS - 1

        def heads(h):
            return h // 2, slice(64 * (h % 2), 64 * (h % 2) + 64)

        def slot(bank_even, h):
            return B[bank_even + h % 2][:, (h // 2) * HD:(h // 2 + 1) * HD]

        with nc.Block() as block:
            @block.sync
            def _(sp):
                for n, nm in enumerate(("rwkv_lnx_g", "rwkv_lnx_b")):
                    sp.dma_start(lnx[:, n, :], K.in_[nm][j:j + 1, :].broadcast_to([P, TOKW])).then_inc(m.small, 16)

            @block.tensor
            def _(pe):
                for c in range(NT):
                    tok = slice(c * P, (c + 1) * P)
                    if c:
                        pe.wait_ge(m.y_kept, c)
                        pe.wait_ge(m.s_sum, c)
                        pe.wait_ge(m.g_kept, c)
                    n = 0
                    for src in (R.bT, R.kT):
                        for i0, ni in ((0, 4), (4, 2)):
                            for i in range(ni):
                                last = pe.transpose(B[n][:, i * P:(i + 1) * P], src[:, i0 + i, tok], K.ident[:])
                            last.then_inc(m.tok_t, 1)
                            n += 1
                    for h0 in range(0, NH, 2):
                        if h0 >= 4:
                            pe.wait_ge(m.a_kept, c * NH + h0 - 2)
                        for src, cols in ((R.bT, slice(0, 2 * P)), (R.kT, slice(2 * P, 4 * P))):
                            for h in (h0, h0 + 1):
                                i, p = heads(h)
                                last = pe.matmul(B[4 + h % 4][:, cols], src[p, i, tok], ARv[p, i, c, :], start=True, stop=True)
                                if cols.start:
                                    last.then_inc(m.a_made, 1)
                    pe.wait_ge(m.tok_k, 4 * (c + 1))
                    for g in range(GROUPS):
                        pe.wait_ge(m.w0, c * GROUPS + g + 1)
                        for h in range(GH * g, GH * g + GH):
                            last = pe.transpose(B[g][:, (h % GH) * P:(h % GH + 1) * P], W[:, h, :], K.ident[:])
                        last.then_inc(m.t0_t, 1)
                    pe.wait_ge(m.a_kept, (c + 1) * NH)
                    for l in range(1, LEVELS):
                        nt, nx = c * GROUPS * (LEVELS - 2) + (l - 1) * GROUPS, c * GROUPS * (LEVELS - 1) + (l - 1) * GROUPS
                        for g in range(GROUPS):
                            pe.wait_ge(m.q, c * GROUPS * LEVELS + l * GROUPS + g + 1)
                            if l == 1:
                                pe.wait_ge(m.t0_k, c * GROUPS + g + 1)
                            else:
                                pe.wait_ge(m.t_added, nt - GROUPS + g + 1)
                            for h in range(GH * g, GH * g + GH):
                                last = pe.matmul(B[g][:, (h % GH) * P:(h % GH + 1) * P], QT[:, h, :], Tm[:, h, :], start=True, stop=True)
                            last.then_inc(m.x_made, 1)
                        for g in range(GROUPS):
                            pe.wait_ge(m.x_kept, nx + g + 1)
                            if l > 1:
                                pe.wait_ge(m.w_added, nx - GROUPS + g + 1)
                            if l < LAST:
                                for h in range(GH * g, GH * g + GH):
                                    last = pe.matmul(B[g][:, (h % GH) * P:(h % GH + 1) * P], W[:, h, :], Xm[:, h, :], start=True, stop=True)
                                last.then_inc(m.t_made, 1)
                            for h in range(GH * g, GH * g + GH):
                                last = pe.matmul(B[3 + g][:, (h % GH) * P:(h % GH + 1) * P], Xm[:, h, :], W[:, h, :], start=True, stop=True)
                            last.then_inc(m.w_made, 1)
                    if c:
                        pe.wait_ge(m.s_done, c)
                    for h in range(NH):
                        i, p = heads(h)
                        last = pe.matmul(slot(6, h), A[:, h, 2 * P:3 * P], R.V[:, c, h * HD:(h + 1) * HD], start=True, stop=(c == 0))
                        if c:
                            last = pe.matmul(slot(6, h), ARv[p, i, c, 0:P], S[p, i, :], start=False, stop=True)
                    last.then_inc(m.z_made, 1)
                    pe.wait_ge(m.z_kept, c + 1)
                    pe.wait_ge(m.w_added, (c + 1) * GROUPS * (LEVELS - 1))
                    for h in range(NH):
                        last = pe.matmul(slot(0, h), W[:, h, :], Z[:, h, :], start=True, stop=True)
                    last.then_inc(m.u_made, 1)
                    for half in range(2):
                        last = pe.matmul(B[5 + half][:, 0:TOKW // 2], R.gd[:, 0, tok], g2[:, half * (TOKW // 2):(half + 1) * (TOKW // 2)],
                                         start=True, stop=True)
                    last.then_inc(m.g_made, 1)
                    pe.wait_ge(m.u_kept, c + 1)
                    if c < NT - 1:
                        for h in range(NH):
                            i, p = heads(h)
                            o = B[4][p, i * HD:(i + 1) * HD]
                            pe.matmul(o, R.Bt[:, 0, h * HD:(h + 1) * HD], U[:, h, :], start=True, stop=False)
                            last = pe.matmul(o, R.Kt[:, 0, h * HD:(h + 1) * HD], R.V[:, c, h * HD:(h + 1) * HD], start=False, stop=True)
                        last.then_inc(m.st_made, 1)
                    for h in range(NH):
                        i, p = heads(h)
                        pe.matmul(slot(2, h), A[:, h, P:2 * P], U[:, h, :], start=True, stop=False)
                        last = pe.matmul(slot(2, h), A[:, h, 3 * P:4 * P], R.V[:, c, h * HD:(h + 1) * HD], start=False, stop=(c == 0))
                        if c:
                            last = pe.matmul(slot(2, h), ARv[p, i, c, P:2 * P], S[p, i, :], start=False, stop=True)
                    last.then_inc(m.y_made, 1)

            @block.gpsimd
            def _(pool):
                for c in range(NT):
                    for l in range(LEVELS):
                        for g in range(GROUPS):
                            hs = slice(GH * g, GH * g + GH)
                            if l == 0:
                                pool.wait_ge(m.a_kept, c * NH + GH * (g + 1))
                                if c:
                                    pool.wait_ge(m.u_made, c)
                            elif l == 1:
                                pool.wait_ge(m.w0, c * GROUPS + g + 1)
                            else:
                                pool.wait_ge(m.x_made, c * GROUPS * (LEVELS - 1) + (l - 2) * GROUPS + g + 1)
                            nq = c * GROUPS * LEVELS + l * GROUPS + g + 1
                            pool.tensor_tensor(QT[:, hs, :], A[:, hs, 0:P], K.level[:, l:l + 1, :].to_broadcast([P, GH, P]), ALU.mult).then_inc(m.q, 1)
                            if l == 0:
                                pool.wait_ge(m.q, nq)
                                pool.tensor_tensor(W[:, hs, :], QT[:, hs, :], K.ident[:].unsqueeze(1).to_broadcast([P, GH, P]), ALU.add).then_inc(m.w0, 1)

            @block.scalar
            def _(act):
                def root(c):
                    act.wait_ge(m.v_ready, c + 1)
                    act.activation(st[:, 1, :], st[:, 1, :], ACT.Sqrt).then_inc(m.root, 1)

                for c in range(NT):
                    n = 0
                    for dst in (R.Bt, R.Kt):
                        for i0, ni in ((0, 4), (4, 2)):
                            act.wait_ge(m.tok_t, 4 * c + n + 1)
                            act.activation(dst[:, 0, i0 * P:(i0 + ni) * P], B[n][:, 0:ni * P], ACT.Copy).then_inc(m.tok_k, 1)
                            n += 1
                    for g in range(GROUPS):
                        act.wait_ge(m.t0_t, c * GROUPS + g + 1)
                        act.activation(Tm[:, GH * g:GH * g + GH, :], B[g][:].rearrange("p (h t) -> p h t", h=GH), ACT.Copy).then_inc(m.t0_k, 1)
                    for l in range(1, LEVELS):
                        nx = c * GROUPS * (LEVELS - 1) + (l - 1) * GROUPS
                        if c and l == 3:
                            root(c - 1)
                        for g in range(GROUPS):
                            act.wait_ge(m.x_made, nx + g + 1)
                            wait_from(act, m.w_made, nx - GROUPS + g + 1)
                            act.activation(Xm[:, GH * g:GH * g + GH, :], B[g][:].rearrange("p (h t) -> p h t", h=GH), ACT.Copy).then_inc(m.x_kept, 1)
                    act.wait_ge(m.z_made, c + 1)
                    for o in range(2):
                        last = act.activation(Z[:].rearrange("p (i o) d -> p i o d", o=2)[:, :, o, :],
                                              B[6 + o][:, 0:TILES * HD].rearrange("p (i d) -> p i d", i=TILES), ACT.Copy)
                    last.then_inc(m.z_kept, 1)
                    act.wait_ge(m.u_made, c + 1)
                    for o in range(2):
                        last = act.activation(U.rearrange("p (i o) d -> p i o d", o=2)[:, :, o, :],
                                              B[o][:, 0:TILES * HD].rearrange("p (i d) -> p i d", i=TILES), ACT.Copy)
                    last.then_inc(m.u_kept, 1)
                    act.wait_ge(m.g_made, c + 1)
                    wait_from(act, m.outs, c)
                    for o in range(2):
                        last = act.activation(G[:, o * (TOKW // 2):(o + 1) * (TOKW // 2)], B[5 + o][:, 0:TOKW // 2], ACT.Copy)
                    last.then_inc(m.g_kept, 1)
                root(NT - 1)

            @block.vector
            def _(dve):
                step = Chain(dve, m.gn)

                def outputs(c):
                    b3 = [P, NH, HD]
                    yf, qf = y[:].rearrange("p h d -> p (h d)"), yq[:].rearrange("p h d -> p (h d)")
                    step(dve.tensor_reduce(st[:, 0, :], y[:], AX.X, ALU.add))
                    step(dve.tensor_scalar_mul(st[:, 0, :], st[:, 0, :], 1.0 / HD))
                    yield
                    step(dve.tensor_tensor(y[:], y[:], st[:, 0, :].unsqueeze(2).to_broadcast(b3), ALU.subtract))
                    yield
                    step(dve.tensor_tensor(yq[:], y[:], y[:], ALU.mult))
                    yield
                    step(dve.tensor_reduce(st[:, 1, :], yq[:], AX.X, ALU.add))
                    dve.tensor_scalar(st[:, 1, :], st[:, 1, :], 1.0 / HD, GN_EPS, ALU.mult, ALU.add).then_inc(m.v_ready, 1)
                    yield
                    step(dve.tensor_tensor(yq[:], R.V[:, c, :].rearrange("p (h d) -> p h d", h=NH), R.bonus[:, c, :].unsqueeze(2).to_broadcast(b3), ALU.mult))
                    for _ in range(ROOT_SLOTS):
                        yield
                    dve.wait_ge(m.root, c + 1)
                    step(dve.reciprocal(st[:, 2, :], st[:, 1, :]))
                    step(dve.tensor_tensor(y[:], y[:], st[:, 2, :].unsqueeze(2).to_broadcast(b3), ALU.mult))
                    yield
                    dve.wait_ge(m.small, 32)
                    step(dve.tensor_tensor(yf, yf, lnx[:, 0, :], ALU.mult))
                    yield
                    step(dve.tensor_tensor(yf, yf, lnx[:, 1, :], ALU.add))
                    yield
                    step(dve.tensor_tensor(yf, yf, qf, ALU.add))
                    yield
                    dve.wait_ge(m.g_kept, c + 1)
                    dve.tensor_tensor(mix[:, c, 0:TOKW], yf, G[:], ALU.mult).then_inc(m.outs, 1)

                pieces = iter(())
                for c in range(NT):
                    for h in range(NH):
                        dve.wait_ge(m.a_made, c * NH + h + 1)
                        dve.tensor_tensor(A[:, h, :], B[4 + h % 4][:], K.masks4[:], ALU.mult).then_inc(m.a_kept, 1)
                    for l in range(1, LEVELS):
                        nt, nx = c * GROUPS * (LEVELS - 2) + (l - 1) * GROUPS, c * GROUPS * (LEVELS - 1) + (l - 1) * GROUPS
                        for g in range(GROUPS):
                            hs = slice(GH * g, GH * g + GH)
                            if l < LAST:
                                dve.wait_ge(m.t_made, nt + g + 1)
                                wait_from(dve, m.t_added, nt - GROUPS + g + 1)
                                dve.tensor_tensor(Tm[:, hs, :], Tm[:, hs, :], B[g][:].rearrange("p (h t) -> p h t", h=GH), ALU.add).then_inc(m.t_added, 1)
                            dve.wait_ge(m.w_made, nx + g + 1)
                            wait_from(dve, m.w_added, nx - GROUPS + g + 1)
                            dve.tensor_tensor(W[:, hs, :], W[:, hs, :], B[3 + g][:].rearrange("p (h t) -> p h t", h=GH), ALU.add).then_inc(m.w_added, 1)
                            next(pieces, None)
                    if c < NT - 1:
                        dve.wait_ge(m.st_made, c + 1)
                        stp = B[4][:, 0:TILES * HD].rearrange("p (i d) -> p i d", i=TILES)
                        dve.wait_ge(m.y_made, c + 1)
                        if c:
                            dve.wait_ge(m.s_done, c)
                            dve.tensor_tensor(S[:], S[:], stp, ALU.add).then_inc(m.s_sum, 1)
                        else:
                            dve.tensor_copy(S[:], stp).then_inc(m.s_sum, 1)
                        dve.wait_ge(m.s_sum, c + 1)
                        dve.tensor_tensor(S[:], S[:], R.f[:, :, c:c + 1].to_broadcast([P, TILES, HD]), ALU.mult).then_inc(m.s_done, 1)
                    dve.wait_ge(m.y_made, c + 1)
                    wait_from(dve, m.outs, c)
                    for o in range(2):
                        last = dve.tensor_copy(y[:].rearrange("p (i o) d -> p i o d", o=2)[:, :, o, :],
                                               B[2 + o][:, 0:TILES * HD].rearrange("p (i d) -> p i d", i=TILES))
                    last.then_inc(m.y_kept, 1)
                    dve.wait_ge(m.y_kept, c + 1)
                    pieces = outputs(c)
                for _ in pieces:
                    pass


def shared_state(nc, scope, ins):
    def sb(name, shape, dt=F32):
        return scope.enter_context(nc.sbuf_tensor(name, shape, dt))

    def sem(name):
        return scope.enter_context(nc.semaphore(name))

    K = Names()
    K.nc, K.in_ = nc, ins
    K.banks = [scope.enter_context(nc.psum_tensor(f"bank{i}", [P, 512], F32)) for i in range(8)]
    K.X = sb("X", [P, NT, D])
    K.XT = sb("XT", [P, KD, T])
    K.Xk = K.X[:].rearrange("p t (q k) -> p t k q", k=KD)
    K.W = sb("W", [P, 2, 2, 3, KD * FE])
    K.arena = K.W[:].rearrange("p a b c d -> p (a b c d)")
    K.k_memT = sb("k_memT", [HD, NMH, NMEM])
    K.v_mem = sb("v_mem", [P, NMEM // P, MEMW])
    K.x_rows = nc.dram_tensor("x_rows", [T, D], F32).ap()
    K.y_rows = nc.dram_tensor("y_rows", [TOPK * T, D], F32).ap()
    K.w_gu = [sem("w_gu0"), sem("w_gu1")]
    K.w_dn = [sem("w_dn0"), sem("w_dn1")]
    K.sh_added, K.x_loaded, K.out_stored = sem("sh_added"), sem("x_loaded"), sem("out_stored")
    return K


def decoder_trunk(nc, ins, out):
    with ExitStack() as scope:
        K = shared_state(nc, scope, ins)
        memory_keys(K, constants(K, scope))
        for L in range(DEPTH):
            if L % 2 == 0:
                fox_layer(K, L, L // 2)
            else:
                rwkv_layer(K, L, L // 2)
            K.w_gu_base, K.w_dn_base = L * 16 * PAIRS, L * 8 * PAIRS
            routed_experts_tables(K, L)
            expert_loop(K, L)
            combine(K, L, out if L == DEPTH - 1 else None)


_INS = ["x", "mem", "mem_ln_g", "mem_ln_b", "w_mem_kv", "fox_w_in", "fox_b_f", "rwkv_w_in", "rwkv_mu", "rwkv_w0",
        "rwkv_w2", "rwkv_a0", "rwkv_a2", "rwkv_g2", "rwkv_k_k", "rwkv_k_a", "rwkv_r_k", "rwkv_lnx_g", "rwkv_lnx_b",
        "w_out", "ln1_g", "ln1_b", "w_router", "router_bias", "w_exp_gate", "w_exp_up", "w_exp_down",
        "w_sh_gate", "w_sh_up", "w_sh_down", "ln2_g", "ln2_b"]


def kernel(**inputs):
    import numpy as _np
    import concourse.bacc as _bacc
    from concourse import mybir as _mybir
    from concourse.bass_utils import run_bass_kernel_spmd as _run

    nc = _bacc.Bacc("TRN2", target_bir_lowering=False, num_devices=1)
    arrays, aps = {}, {}
    for name in _INS:
        a = _np.ascontiguousarray(inputs[name])
        arrays[f"in_{name}_dram"] = a
        aps[name] = nc.dram_tensor(f"in_{name}_dram", a.shape, _mybir.dt.from_np(a.dtype), kind="ExternalInput").ap()
    out = nc.dram_tensor("out_dram", (1, T, D), F32, kind="ExternalOutput").ap()
    decoder_trunk(nc, aps, out)
    r = _run(nc, [arrays], core_ids=[0])
    return r.results[0]["out_dram"]
```
